# Optimizing a Trainium2 kernel written in Bass

```python
import math
import jax, jax.numpy as jnp
from jax import lax
import numpy as np

D_MODEL = 2048
BATCH = 1
SEQ = 256
DEPTH = 1

NSA_HEADS = 16
NSA_KV_HEADS = 4
NSA_Q_PER_KV = NSA_HEADS // NSA_KV_HEADS
NSA_HEAD_DIM = 128
CMP_BLOCK = 32
CMP_STRIDE = 16
SLC_BLOCK = 64
SLC_TOP = 16
WINDOW = 512
Q_BLOCK = 128
ROPE_THETA = 500000.0
ROPE_DIM = NSA_HEAD_DIM // 4
SSM_D_INNER = D_MODEL
SSM_HEAD_DIM = 64
SSM_HEADS = SSM_D_INNER // SSM_HEAD_DIM
SSM_GROUPS = 4
SSM_HEADS_PER_GROUP = SSM_HEADS // SSM_GROUPS
SSM_STATE = 128
SSM_CONV = 4
SSM_CHUNK = 128
SSM_CONV_CH = SSM_D_INNER + 2 * SSM_GROUPS * SSM_STATE
PEER_HEADS = 8
PEER_N_KEYS = 128
PEER_N_EXPERTS = PEER_N_KEYS * PEER_N_KEYS
PEER_D_KEY = 256
PEER_TOPK = 16
TOKEN_BLOCK = 128
Q_COLS = NSA_HEADS * NSA_HEAD_DIM
KV_COLS = 3 * 2 * NSA_KV_HEADS * NSA_HEAD_DIM
NSA_GATE_COLS = 3 * NSA_HEADS
Z_COLS = SSM_D_INNER
XBC_COLS = SSM_CONV_CH
DT_COLS = SSM_HEADS
MERGE_COLS = 2 * D_MODEL
IN_SIZES = (Q_COLS, KV_COLS, NSA_GATE_COLS, Z_COLS, XBC_COLS, DT_COLS, MERGE_COLS)
IN_COLS = Q_COLS + KV_COLS + NSA_GATE_COLS + Z_COLS + XBC_COLS + DT_COLS + MERGE_COLS
EPS = 1e-6
NEG_INF = -1e30
FORCE = 1e4

kernel_name = "hybrid_nsa_mamba2_peer_block"

def split_columns(a, sizes):
    out, start = [], 0
    for s in sizes:
        out.append(a[..., start:start + s])
        start += s
    return out

def rmsnorm(x, g):
    xf = x.astype(jnp.float32)
    y = xf * lax.rsqrt(jnp.mean(xf * xf, axis=-1, keepdims=True) + EPS)
    return (y * g.astype(jnp.float32)).astype(x.dtype)

def partial_rope(x, pos):
    half = ROPE_DIM // 2
    inv = ROPE_THETA ** (-jnp.arange(half, dtype=jnp.float32) / half)
    ang = pos.astype(jnp.float32)[:, None] * inv[None, :]
    cos = jnp.cos(ang)[None, :, None, :].astype(x.dtype)
    sin = jnp.sin(ang)[None, :, None, :].astype(x.dtype)
    x1, x2, rest = x[..., :half], x[..., half:ROPE_DIM], x[..., ROPE_DIM:]
    return jnp.concatenate([x1 * cos - x2 * sin, x2 * cos + x1 * sin, rest], axis=-1)

def masked_softmax(s, mask):
    s = jnp.where(mask, s.astype(jnp.float32), NEG_INF)
    return jax.nn.softmax(s, axis=-1) * mask

def compress_tokens(kv, pos_emb, w1, b1, w2):
    B, S, G, hd = kv.shape
    ratio = CMP_BLOCK // CMP_STRIDE
    n_chunks = S // CMP_STRIDE
    nc = n_chunks - ratio + 1
    chunks = kv.reshape(B, n_chunks, CMP_STRIDE, G, hd)
    blocks = jnp.concatenate([chunks[:, r:r + nc] for r in range(ratio)], axis=2)
    blocks = blocks + pos_emb[None, None, :, None, :]
    flat = blocks.transpose(0, 1, 3, 2, 4).reshape(B, nc, G, CMP_BLOCK * hd)
    hidden = jax.nn.gelu(flat @ w1 + b1, approximate=False)
    return hidden @ w2

def selection_scores(p_cmp, n_sel_blocks):
    spc = SLC_BLOCK // CMP_STRIDE
    ratio = CMP_BLOCK // CMP_STRIDE
    n_off = spc + ratio - 1
    nc = p_cmp.shape[-1]
    need = spc * (n_sel_blocks - 1) + n_off
    front = ratio - 1
    p_pad = jnp.pad(p_cmp, ((0, 0), (0, 0), (0, 0), (front, need - front - nc)))
    weights = [float(sum(1 for r in range(ratio) if 0 <= o - front + r < spc)) for o in range(n_off)]
    terms = [p_pad[..., o:o + spc * (n_sel_blocks - 1) + 1:spc] for o in range(n_off)]
    return jnp.stack(terms, axis=-1) @ jnp.asarray(weights, p_cmp.dtype)

def native_sparse_attention(q, kv, gate_logits, cmp_pos, cmp_w1, cmp_b1, cmp_w2, pos):
    B, S, _ = q.shape
    G, R, hd = NSA_KV_HEADS, NSA_Q_PER_KV, NSA_HEAD_DIM
    scale = hd ** -0.5
    q = partial_rope(q.reshape(B, S, NSA_HEADS, hd), pos).reshape(B, S, G, R, hd)
    kv = kv.reshape(B, S, 3, 2, G, hd)
    gates = jax.nn.sigmoid(gate_logits.reshape(B, S, G, R, 3))
    kc = compress_tokens(partial_rope(kv[:, :, 0, 0], pos), cmp_pos[0], cmp_w1[0], cmp_b1[0], cmp_w2[0])
    vc = compress_tokens(kv[:, :, 0, 1], cmp_pos[1], cmp_w1[1], cmp_b1[1], cmp_w2[1])
    nc = kc.shape[1]
    c_end = jnp.arange(nc) * CMP_STRIDE + CMP_BLOCK - 1
    ns = S // SLC_BLOCK
    n_sel = min(SLC_TOP, ns)
    kb = partial_rope(kv[:, :, 1, 0], pos).reshape(B, ns, SLC_BLOCK, G, hd).transpose(0, 3, 1, 2, 4)
    vb = kv[:, :, 1, 1].reshape(B, ns, SLC_BLOCK, G, hd).transpose(0, 3, 1, 2, 4)
    b_ix = jnp.arange(B)[:, None, None, None]
    g_ix = jnp.arange(G)[None, :, None, None]
    blk = jnp.arange(ns)
    pad = ((0, 0), (WINDOW, 0), (0, 0), (0, 0))
    kw_pad = jnp.pad(partial_rope(kv[:, :, 2, 0], pos), pad)
    vw_pad = jnp.pad(kv[:, :, 2, 1], pad)

    def query_block(i):
        start = i * Q_BLOCK
        t = start + jnp.arange(Q_BLOCK)
        qb = lax.dynamic_slice_in_dim(q, start, Q_BLOCK, axis=1)
        gb = lax.dynamic_slice_in_dim(gates, start, Q_BLOCK, axis=1)
        s_c = jnp.einsum('btgrd,bcgd->bgrtc', qb, kc) * scale
        p_c = masked_softmax(s_c, c_end[None, :] <= t[:, None])
        o_c = jnp.einsum('bgrtc,bcgd->btgrd', p_c.astype(vc.dtype), vc)
        imp = selection_scores(p_c.sum(axis=2), ns)
        cur = t[:, None] // SLC_BLOCK
        forced = (blk[None, :] == 0) | (blk[None, :] == cur) | (blk[None, :] == cur - 1)
        imp = jnp.where(forced, FORCE, imp)
        imp = jnp.where(blk[None, :] * SLC_BLOCK <= t[:, None], imp, NEG_INF)
        _, top_i = lax.top_k(imp, n_sel)
        ks = kb[b_ix, g_ix, top_i]
        vs = vb[b_ix, g_ix, top_i]
        kpos = top_i[..., None] * SLC_BLOCK + jnp.arange(SLC_BLOCK)
        m_s = (kpos <= t[None, None, :, None, None]).reshape(B, G, 1, Q_BLOCK, n_sel * SLC_BLOCK)
        s_s = jnp.einsum('btgrd,bgtksd->bgrtks', qb, ks) * scale
        p_s = masked_softmax(s_s.reshape(B, G, R, Q_BLOCK, n_sel * SLC_BLOCK), m_s)
        o_s = jnp.einsum('bgrtn,bgtnd->btgrd', p_s.astype(vs.dtype), vs.reshape(B, G, Q_BLOCK, n_sel * SLC_BLOCK, hd))
        kw = lax.dynamic_slice_in_dim(kw_pad, start, WINDOW + Q_BLOCK, axis=1)
        vw = lax.dynamic_slice_in_dim(vw_pad, start, WINDOW + Q_BLOCK, axis=1)
        wpos = start - WINDOW + jnp.arange(WINDOW + Q_BLOCK)
        m_w = (wpos[None, :] <= t[:, None]) & (wpos[None, :] > t[:, None] - WINDOW) & (wpos[None, :] >= 0)
        s_w = jnp.einsum('btgrd,bsgd->bgrts', qb, kw) * scale
        p_w = masked_softmax(s_w, m_w)
        o_w = jnp.einsum('bgrts,bsgd->btgrd', p_w.astype(vw.dtype), vw)
        return gb[..., 0:1] * o_c + gb[..., 1:2] * o_s + gb[..., 2:3] * o_w

    out = lax.map(query_block, jnp.arange(S // Q_BLOCK))
    return out.transpose(1, 0, 2, 3, 4, 5).reshape(B, S, NSA_HEADS * hd)

def causal_depthwise_conv(u, w, b):
    out = lax.conv_general_dilated(u, w[:, None, :], window_strides=(1,), padding=((SSM_CONV - 1, 0),),
                                   dimension_numbers=('NWC', 'WIO', 'NWC'), feature_group_count=u.shape[-1])
    return out + b

def ssd_chunked(x, a, bm, cm):
    B, S, G, R, P = x.shape
    N = bm.shape[-1]
    L = SSM_CHUNK
    nc = S // L
    x = x.reshape(B, nc, L, G, R, P)
    a = a.reshape(B, nc, L, G, R).transpose(0, 3, 4, 1, 2)
    bm = bm.reshape(B, nc, L, G, N)
    cm = cm.reshape(B, nc, L, G, N)
    a_cs = jnp.cumsum(a, axis=-1)
    seg = a_cs[..., :, None] - a_cs[..., None, :]
    causal = jnp.tril(jnp.ones((L, L), dtype=bool))
    decay = jnp.where(causal, jnp.exp(jnp.where(causal, seg, 0.0)), 0.0)
    cb = jnp.einsum('bclgn,bcsgn->bgcls', cm, bm)
    y_diag = jnp.einsum('bgcls,bgrcls,bcsgrp->bclgrp', cb, decay, x)
    decay_to_end = jnp.exp(a_cs[..., -1:] - a_cs)
    states = jnp.einsum('bclgn,bgrcl,bclgrp->bcgrpn', bm, decay_to_end, x)
    chunk_decay = jnp.exp(a_cs[..., -1])

    def step(h, inp):
        st, dec = inp
        return h * dec[..., None, None] + st, h

    _, prev = lax.scan(step, jnp.zeros_like(states[:, 0]),
                       (states.transpose(1, 0, 2, 3, 4, 5), chunk_decay.transpose(3, 0, 1, 2)))
    prev = prev.transpose(1, 0, 2, 3, 4, 5)
    y_off = jnp.einsum('bclgn,bcgrpn,bgrcl->bclgrp', cm, prev, jnp.exp(a_cs))
    return (y_diag + y_off).reshape(B, S, G, R, P)

def mamba2_mixer(z, xbc, dt, conv_w, conv_b, dt_bias, a_log, d_skip, norm_w):
    B, S, _ = xbc.shape
    G, R, P, N = SSM_GROUPS, SSM_HEADS_PER_GROUP, SSM_HEAD_DIM, SSM_STATE
    xbc = jax.nn.silu(causal_depthwise_conv(xbc, conv_w, conv_b))
    xs, bm, cm = split_columns(xbc, (SSM_D_INNER, G * N, G * N))
    xs = xs.reshape(B, S, G, R, P)
    bm = bm.reshape(B, S, G, N)
    cm = cm.reshape(B, S, G, N)
    dt = jax.nn.softplus(dt.astype(jnp.float32) + dt_bias.astype(jnp.float32)).reshape(B, S, G, R)
    a = -jnp.exp(a_log.astype(jnp.float32)).reshape(G, R)
    y = ssd_chunked(xs * dt[..., None], dt * a, bm, cm)
    y = y + d_skip.reshape(G, R)[:, :, None] * xs
    g = (y.reshape(B, S, SSM_D_INNER) * jax.nn.silu(z.astype(jnp.float32))).reshape(B, S, G, -1)
    g = g * lax.rsqrt(jnp.mean(g * g, axis=-1, keepdims=True) + EPS)
    return (g.reshape(B, S, SSM_D_INNER) * norm_w).astype(z.dtype)

def peer_ffn(h, w_q, sub_keys, u, v):
    B, S, D = h.shape
    q = (h @ w_q).reshape(B, S, PEER_HEADS, 2, PEER_D_KEY // 2)
    s = jnp.einsum('bshcd,hckd->bshck', q, sub_keys).astype(jnp.float32)
    s_top, i_top = lax.top_k(s, PEER_TOPK)
    cand = s_top[..., 0, :, None] + s_top[..., 1, None, :]
    cand_idx = i_top[..., 0, :, None] * PEER_N_KEYS + i_top[..., 1, None, :]
    best_s, best_pos = lax.top_k(cand.reshape(B, S, PEER_HEADS, -1), PEER_TOPK)
    experts = jnp.take_along_axis(cand_idx.reshape(B, S, PEER_HEADS, -1), best_pos, axis=-1)
    gate = jax.nn.softmax(best_s, axis=-1)
    nb = S // TOKEN_BLOCK

    def to_blocks(a):
        return a.reshape(B, nb, TOKEN_BLOCK, *a.shape[2:]).swapaxes(0, 1)

    def token_block(args):
        hb, eb, gb = args
        ue = u[eb]
        act = jax.nn.gelu(jnp.einsum('btd,bthkd->bthk', hb, ue).astype(jnp.float32), approximate=False)
        return jnp.einsum('bthk,bthkd->btd', (gb * act).astype(h.dtype), v[eb])

    out = lax.map(token_block, (to_blocks(h), to_blocks(experts), to_blocks(gate)))
    return out.swapaxes(0, 1).reshape(B, S, D)

def setup_inputs(seed: int = 0) -> dict:
    key = jax.random.key(seed)
    ks = jax.random.split(key, 24)
    L, D, f32 = DEPTH, D_MODEL, jnp.float32

    def nrm(k, shape, scale):
        return scale * jax.random.normal(k, shape, f32)

    dt = jnp.exp(jax.random.uniform(ks[10], (L, SSM_HEADS), f32, math.log(1e-3), math.log(1e-1)))
    return {
        "x": nrm(ks[0], (BATCH, SEQ, D), 1.0),
        "attn_norm": 1.0 + nrm(ks[1], (L, D), 0.01),
        "w_in": nrm(ks[2], (L, D, IN_COLS), D ** -0.5),
        "gate_bias": nrm(ks[3], (L, 2, D), 0.01),
        "nsa_cmp_pos": nrm(ks[4], (L, 2, CMP_BLOCK, NSA_HEAD_DIM), 0.02),
        "nsa_cmp_w1": nrm(ks[5], (L, 2, CMP_BLOCK * NSA_HEAD_DIM, NSA_HEAD_DIM), (CMP_BLOCK * NSA_HEAD_DIM) ** -0.5),
        "nsa_cmp_b1": nrm(ks[6], (L, 2, NSA_HEAD_DIM), 0.01),
        "nsa_cmp_w2": nrm(ks[7], (L, 2, NSA_HEAD_DIM, NSA_HEAD_DIM), NSA_HEAD_DIM ** -0.5),
        "ssm_conv_w": nrm(ks[8], (L, SSM_CONV, SSM_CONV_CH), SSM_CONV ** -0.5),
        "ssm_conv_b": nrm(ks[9], (L, SSM_CONV_CH), 0.01),
        "ssm_dt_bias": dt + jnp.log(-jnp.expm1(-dt)),
        "ssm_a_log": jnp.log(jax.random.uniform(ks[11], (L, SSM_HEADS), f32, 1.0, 16.0)),
        "ssm_d": 1.0 + nrm(ks[12], (L, SSM_HEADS), 0.01),
        "ssm_norm": 1.0 + nrm(ks[13], (L, SSM_D_INNER), 0.01),
        "w_branch_nsa": nrm(ks[14], (L, NSA_HEADS * NSA_HEAD_DIM, D), (NSA_HEADS * NSA_HEAD_DIM) ** -0.5),
        "w_branch_ssm": nrm(ks[15], (L, SSM_D_INNER, D), SSM_D_INNER ** -0.5),
        "w_out": nrm(ks[16], (L, D, D), D ** -0.5),
        "ffn_norm": 1.0 + nrm(ks[17], (L, D), 0.01),
        "peer_w_q": nrm(ks[18], (L, D, PEER_HEADS * PEER_D_KEY), D ** -0.5),
        "peer_sub_keys": nrm(ks[19], (L, PEER_HEADS, 2, PEER_N_KEYS, PEER_D_KEY // 2), (PEER_D_KEY // 2) ** -0.5),
        "peer_u": nrm(ks[20], (L, PEER_N_EXPERTS, D), D ** -0.5),
        "peer_v": nrm(ks[21], (L, PEER_N_EXPERTS, D), 0.3),
        "final_norm": 1.0 + nrm(ks[22], (D,), 0.01),
    }

def reference(x, attn_norm, w_in, gate_bias, nsa_cmp_pos, nsa_cmp_w1, nsa_cmp_b1, nsa_cmp_w2,
              ssm_conv_w, ssm_conv_b, ssm_dt_bias, ssm_a_log, ssm_d, ssm_norm,
              w_branch_nsa, w_branch_ssm, w_out, ffn_norm, peer_w_q, peer_sub_keys, peer_u, peer_v,
              final_norm):
    B, S, D = x.shape
    pos = jnp.arange(S)
    for l in range(DEPTH):
        h = rmsnorm(x, attn_norm[l])
        proj = h @ w_in[l]
        q, kv, nsa_g, z, xbc, dt, merge_g = split_columns(proj, IN_SIZES)
        o_nsa = native_sparse_attention(q, kv, nsa_g, nsa_cmp_pos[l], nsa_cmp_w1[l], nsa_cmp_b1[l],
                                        nsa_cmp_w2[l], pos)
        o_ssm = mamba2_mixer(z, xbc, dt, ssm_conv_w[l], ssm_conv_b[l], ssm_dt_bias[l], ssm_a_log[l],
                             ssm_d[l], ssm_norm[l])
        g = jax.nn.sigmoid(merge_g.reshape(B, S, 2, D) + gate_bias[l])
        merged = g[:, :, 0] * (o_nsa @ w_branch_nsa[l]) + g[:, :, 1] * (o_ssm @ w_branch_ssm[l])
        x = x + merged @ w_out[l]
        x = x + peer_ffn(rmsnorm(x, ffn_norm[l]), peer_w_q[l], peer_sub_keys[l], peer_u[l], peer_v[l])
    return rmsnorm(x, final_norm)


_drawn_inputs = setup_inputs


def setup_inputs(seed=0):
    import zlib

    import numpy as np

    out = dict(_drawn_inputs(seed))
    spreads = {}
    factors = {'attn_norm': 3.615,
     'gate_bias': 8.0,
     'nsa_cmp_pos': 20.664,
     'nsa_cmp_b1': 37.949,
     'ssm_conv_b': 14.944,
     'ssm_d': 54.04,
     'ssm_norm': 24.716,
     'ffn_norm': 21.81,
     'final_norm': 31.918}
    for name, (base, spread) in spreads.items():
        noise = np.random.default_rng([zlib.crc32(name.encode()), seed]).standard_normal(out[name].shape)
        drawn = base * np.exp(spread * noise) if base else spread * noise
        out[name] = __import__('jax').numpy.asarray(drawn.astype(out[name].dtype))
    for name, factor in factors.items():
        out[name] = (out[name] * factor).astype(out[name].dtype)
    return out
```

```python
from contextlib import ExitStack

import numpy as np

import concourse.bass as bass
from concourse import mybir
from concourse.alu_op_type import AluOpType as ALU

ACT = mybir.ActivationFunctionType
AX = mybir.AxisListType
F32 = mybir.dt.float32
F32R = mybir.dt.float32r
U32 = mybir.dt.uint32
ds = bass.ds

P = 128
D = 2048
KT = D // P
S = 256
TT = S // P
EPS = 1e-6
NEG = -1e30
PIECE = 1024
HKT = KT // 2

HEADS, GROUPS, RPG, HD = 16, 4, 4, 128
SCALE = HD ** -0.5
CB, CS = 32, 16
NC = S // CS - CB // CS + 1
ROPE = HD // 4
THETA = 500000.0

SH, SG, SHG, SP_, SN, CHUNK = 32, 4, 8, 64, 128, 128
CONV = 4
XT_T, XBC_T, Z_T, MG_T = 16, 24, 16, 32

PH, TOPK, NKEY = 8, 16, 128

QKV_A = HEADS + 2 * GROUPS + 2
QKV_B = 4 * GROUPS
ATT_T = XBC_T + Z_T + 8
SSD_T = MG_T - 8
T_A, T_B = 0, QKV_A
T_ATT = T_B + QKV_B
T_SSD = T_ATT + ATT_T
T_BN = T_SSD + SSD_T
T_BS, T_WO, T_WQ = T_BN + KT, T_BN + 2 * KT, T_BN + 3 * KT
T_U = T_BN + 4 * KT
U1_T = 64
T_U2 = T_U + U1_T
T_V = T_U + NKEY
P_V = 2 * T_V

KB = 256
A_Q, A_VT, A_GD, A_K, A_VTOK, A_XBC, A_Z, A_MG = (k * KB for k in (0, 16, 24, 32, 48, 56, 80, 96))
A_END = 128 * KB

C_IDENT, C_IOTA, C_ONES, C_TRI = 0, P, 2 * P, 3 * P
C_KEEP = 4 * P
C_ROT, C_COS, C_SIN, C_MASK, C_CB, C_C01 = 0, P, P + S, P + 2 * S, P + 3 * S, P + 3 * S + 2 * NC
C_PHASE = P + 3 * S + 4 * NC

V_AN, V_SN, V_GB, V_CW, V_FN, V_ON, V_CB, V_B1, V_DS, V_POS, V_DTB, V_AL = (
    0, 16, 32, 64, 160, 176, 192, 216, 218, 234, 298, 330)
V_END = 362


def shape_constants():
    keep = np.zeros((P, C_KEEP), np.float32)
    r = np.arange(P)
    keep[:, C_IDENT:C_IDENT + P] = np.eye(P)
    keep[:, C_IOTA:C_IOTA + P] = r[None, :]
    keep[:, C_ONES:C_ONES + P] = 1
    keep[:, C_TRI:C_TRI + P] = r[:, None] <= r[None, :]
    phase = np.zeros((P, C_PHASE), np.float32)
    half = ROPE // 2
    for d in range(half):
        phase[d + half, C_ROT + d] = -1
        phase[d, C_ROT + d + half] = 1
    inv = np.float32(THETA) ** (-np.arange(half, dtype=np.float32) / np.float32(half))
    ang = np.arange(S, dtype=np.float32)[None, :] * inv.astype(np.float32)[:, None]
    phase[:, C_COS:C_COS + S] = 1
    phase[0:half, C_COS:C_COS + S] = phase[half:ROPE, C_COS:C_COS + S] = np.cos(ang)
    phase[0:half, C_SIN:C_SIN + S] = phase[half:ROPE, C_SIN:C_SIN + S] = np.sin(ang)
    phase[:, C_MASK + P:C_MASK + S] = np.where(r[None, :] <= r[:, None], 0, NEG)
    for tt in range(TT):
        ok = np.arange(NC)[None, :] * CS + CB - 1 <= (r + tt * P)[:, None]
        phase[:, C_CB + tt * NC:C_CB + (tt + 1) * NC] = np.where(ok, 0, NEG)
        phase[:, C_C01 + tt * NC:C_C01 + (tt + 1) * NC] = ok
    return keep, phase


class Tile:

    def __init__(self, i, k, c):
        self.i, self.k, self.c = i, k, c

    def times(self, m, a=0):
        return self.i * (self.k * m) + (self.c * m + a)

    def half(self, a=0):
        return self.i * (self.k // 2) + (self.c // 2 + a)

    def __add__(self, n):
        return Tile(self.i, self.k, self.c + n)


def wait(eng, sem, value):
    if not isinstance(value, int) or value > 0:
        eng.wait_ge(sem, value)


class Steps:

    def __init__(self, eng, sem):
        self.eng, self.sem, self.base, self.n, self.at = eng, sem, 0, 0, 0

    def mark(self, ins):
        self.n += 1
        ins.then_inc(self.sem, 1)

    def wait(self):
        self.eng.wait_ge(self.sem, self.base + self.n)

    def __call__(self, ins):
        self.mark(ins)
        self.wait()

    def apart(self, ins):
        self(ins)
        self.eng.nop(nofuse=True)

    def turns(self, first, end, per, body):
        start = self.n
        with self.eng.Fori(first, end) as i:
            self.base, self.n = i * per + (start - first * per), 0
            body(i)
            assert self.n == per, (self.n, per)
        self.base, self.n = 0, start + (end - first) * per


def build(nc, a, stop=99):
    with ExitStack() as ctx:
        def sb(name, shape, dt=F32, stack=ctx):
            return stack.enter_context(nc.sbuf_tensor(name, shape, dt))

        def sem(name):
            return ctx.enter_context(nc.semaphore(name))

        with ExitStack() as early:
            act1_hi = sb("act1_hi", [P, KT * S], F32R, early)
            act1_lo = sb("act1_lo", [P, KT * S], F32R, early)
        arena = sb("arena", [P, A_END])
        with ExitStack() as early:
            act0_hi = sb("act0_hi", [P, KT * S], F32R, early)
            act0_lo = sb("act0_lo", [P, KT * S], F32R, early)
        onehot = sb("onehot", [P, 8 * KB])
        av_hi = sb("av_hi", [P, 4 * S], F32R)
        av_lo = sb("av_lo", [P, 4 * S], F32R)
        x3 = sb("x3", [P, KT * S])
        raw = sb("raw", [P, 4 * PIECE])
        w_hi = sb("w_hi", [P, 4 * PIECE], F32R)
        w_lo = sb("w_lo", [P, 2 * PIECE], F32R)
        kept = sb("kept", [P, C_KEEP + V_END])
        const, par = kept[:, 0:C_KEEP], kept[:, C_KEEP:C_KEEP + V_END]
        r2 = kept[:, C_TRI:C_TRI + S]
        small = sb("small", [P, 872])

        bank = [ctx.enter_context(nc.psum_tensor(f"bank{i}", [P, 512], F32)) for i in range(8)]

        def ar(at, n):
            return arena[:, at:at + n]

        def slot_major(n):
            return small[:, n * S:(n + 1) * S]

        def gate_cols(n, i, b):
            return small[:, ds(i * 8 + (n * S + 4 * b), 4)].unsqueeze(2).broadcast_to([P, 4, P])

        ident, iota, ones, tri = (const[:, k:k + P] for k in (C_IDENT, C_IOTA, C_ONES, C_TRI))
        phase_at = A_MG + 28 * KB
        rot = ar(phase_at + C_ROT, P)
        cos_t, sin_t = ar(phase_at + C_COS, S), ar(phase_at + C_SIN, S)
        mask_t = ar(phase_at + C_MASK, S)
        cmp_bias = ar(phase_at + C_CB, 2 * NC)
        cmp_01 = ar(phase_at + C_C01, 2 * NC)

        raw_landed = [sem(f"raw_landed{k}") for k in range(4)]
        hi_ready, lo_ready = sem("hi_ready"), sem("lo_ready")
        piece_used, tile_evicted = sem("piece_used"), sem("tile_evicted")
        v_step, a_step, p_step = sem("v_step"), sem("a_step"), sem("p_step")
        par_in, x_in, w1_in, phase_in = sem("par_in"), sem("x_in"), sem("w1_in"), sem("phase_in")
        E = {}

        def ev(name):
            if name not in E:
                E[name] = sem(name)
            return E[name]

        for name in ("sq_ready", "sum_ready", "var_ready", "root_ready", "h_ready", "h_hi", "h_split",
                     "krot", "krot_used", "krope", "v_turned", "v_kept", "g_turned", "g_kept", "hid_sum", "hid_used",
                     "hid_ready", "cmp_out", "cmp_kept",
                     "q_rot", "q_roped", "scores", "scored", "exps", "probs", "p_turned", "p_kept_a",
                     "p_kept_b", "pv", "o_hi", "o_lo", "v_staged",
                     "conv_done", "silu_done", "z_done", "dt_in", "dt_exp", "dta_ready", "acs_sum", "acs_kept",
                     "dte_in", "dte_ready",
                     "x_staged", "x_turned", "b_turned", "b_kept", "xdt_ready", "cbm_ready", "dtatri", "acsb",
                     "seg_ready", "seg_exp", "m_ready", "c_exp", "c_ready", "state", "state_kept", "y_sum",
                     "y_used", "g_ready", "gsq_ready", "gsum", "gsum_kept",
                     "gvar", "groot", "gn_ready", "gn_hi", "g_split",
                     "gate_ready", "merged", "merged_hi", "merged_lo", "res_in", "x2_ready", "x2g_hi", "x2g_lo",
                     "sumsq", "x2sum", "x2var", "x2root", "rstd2", "spilled", "subk_in", "s_sum", "s_kept",
                     "top_done", "gate_in", "gate_exp", "gate_done", "i_turned", "i_kept",
                     "dots_scaled", "g_done", "rows_ready", "ohi", "gj", "w_sum", "w_used", "v_zero", "av_hi_r", "av_lo_r", "back_in",
                     "sweep", "sweep_used", "fsq", "fsum", "fvar", "froot", "out_ready", "stored"):
            ev(name)

        block = ctx.enter_context(nc.Block())

        def piece_ap(ring, slot):
            return ring[:, slot * PIECE:(slot + 1) * PIECE]

        @block.sync
        def _(sp):
            def load(src, n_before, q, i, k, m):
                slot = m % 4
                wait(sp, lo_ready, i * k + (n_before + m - 3))
                sp.dma_start(piece_ap(raw, slot), src[ds(i * k + m, 1)].rearrange("a p n -> (a p) n"))\
                  .then_inc(raw_landed[slot], 16)

            before = 0
            for name, n in (("w_in", 2 * T_BN), ("w_mix", 8 * KT), ("u", 2 * NKEY), ("v", 2 * NKEY)):
                first = 0
                if before == 0:
                    for m in range(4):
                        load(a[name], 0, None, 0, 4, m)
                    first = 1
                with sp.Fori(first, n // 4) as i:
                    for m in range(4):
                        load(a[name], before, None, i, 4, m)
                before += n
                if (name == "w_in" and stop < 4) or (name == "w_mix" and stop < 5) or (name == "u" and stop < 7):
                    break
            if stop >= 7:
                sp.wait_ge(ev("out_ready"), 1)
                sp.dma_start(a["out"].rearrange("k p t -> p k t"),
                             x3[:, :].rearrange("p (k t) -> p k t", k=KT)).then_inc(ev("stored"), 16)
                sp.wait_ge(ev("stored"), 16)

        @block.tensor
        def _(pe):
            def half_tile(T, h, out, hi_rhs, lo_rhs):
                slot = (T.c % 2) * 2 + h
                hi, lo = piece_ap(w_hi, slot), piece_ap(w_lo, slot % 2)
                pe.wait_ge(hi_ready, T.times(2, h + 1))
                for n, (w, x) in enumerate(((hi, hi_rhs), (hi, lo_rhs), (lo, hi_rhs))):
                    if n == 2:
                        pe.wait_ge(lo_ready, T.times(2, h + 1))
                    for k in range(HKT):
                        kt = h * HKT + k
                        mm = pe.matmul(out, w[:, k * P:(k + 1) * P], x[:, kt * S:(kt + 1) * S],
                                       start=(h == 0 and n == 0 and k == 0), stop=(h == 1 and n == 2 and k == HKT - 1))
                mm.then_inc(piece_used, 1)

            def tile(T, hi_rhs, lo_rhs):
                wait(pe, tile_evicted, T.times(1, -1))
                for h in range(2):
                    half_tile(T, h, bank[T.c % 2][:, 0:S], hi_rhs, lo_rhs)

            def stage(T0, n, hi_rhs, lo_rhs):
                first = 0
                if T0 == 0:
                    tile(Tile(0, 2, 0), hi_rhs, lo_rhs)
                    tile(Tile(0, 2, 1), hi_rhs, lo_rhs)
                    first = 1
                with pe.Fori(first, n // 2) as i:
                    for m in range(2):
                        tile(Tile(i, 2, T0 + m), hi_rhs, lo_rhs)

            pe.wait_ge(par_in, 32)
            pe.wait_ge(ev("sq_ready"), 1)
            pe.matmul(bank[2][:, 0:S], ones, ar(A_VTOK, S), start=True, stop=True).then_inc(ev("sum_ready"), 1)
            pe.wait_ge(ev("h_split"), 4)
            stage(T_A, QKV_A, act0_hi, act0_lo)
            stage(T_B, QKV_B, act0_hi, act0_lo)

            pe.wait_ge(tile_evicted, T_ATT)
            pe.wait_ge(phase_in, 16)
            pe.wait_ge(w1_in, 16)
            for n in range(6):
                if n >= 4:
                    pe.wait_ge(ev("krope"), n - 3)
                pe.matmul(bank[2 + n % 4][:, :], rot, ar(A_K + n * 512, 512), start=True, stop=True)\
                  .then_inc(ev("krot"), 1)
            pe.wait_ge(ev("krope"), 6)
            for n in range(4):
                for g in range(GROUPS):
                    b, tt = n // 2, n % 2
                    mm = pe.transpose(bank[2 + n][:, g * P:(g + 1) * P],
                                      ar(A_VT + (b * GROUPS + g) * S + tt * P, P), ident)
                mm.then_inc(ev("v_turned"), 1)
            for n in range(4):
                src = ar(A_GD + (n // 2) * S + (n % 2) * P, P)
                mm = pe.transpose(bank[6][:, n * P:(n + 1) * P], src, ident)
            mm.then_inc(ev("g_turned"), 1)
            for c in range(2):
                src = ar(A_K + (8 + 4 * c) * S, 4 * S).rearrange("p (g t) -> p g t", g=GROUPS)
                w1 = ar(A_XBC + c * CB * P, CB * P)
                if c == 1:
                    pe.wait_ge(ev("hid_used"), 1)
                for l in range(CB):
                    pe.matmul(bank[0][:, 0:GROUPS * NC], w1[:, l * P:(l + 1) * P],
                              src[:, :, l:l + CS * (NC - 1) + 1:CS], start=(l == 0), stop=(l == CB - 1))
                for l in range(CB):
                    mm = pe.matmul(bank[1][:, 0:1], w1[:, l * P:(l + 1) * P],
                                   par[:, V_POS + c * CB + l:V_POS + c * CB + l + 1],
                                   start=(l == 0), stop=(l == CB - 1))
                mm.then_inc(ev("hid_sum"), 1)
            pe.wait_ge(ev("hid_ready"), 2)
            pe.wait_ge(ev("g_kept"), 3)
            w2 = ar(A_XBC + 2 * CB * P, 2 * P)
            hid = [ar(A_MG + 26 * KB + c * 64, GROUPS * NC) for c in range(2)]
            pe.matmul(bank[7][:, 0:GROUPS * NC], w2[:, 0:P], hid[0], start=True, stop=True)
            for g in range(GROUPS):
                mm = pe.matmul(bank[6][0:NC, g * P:(g + 1) * P], hid[1][:, g * NC:(g + 1) * NC], w2[:, P:2 * P],
                               start=True, stop=True)
            mm.then_inc(ev("cmp_out"), 1)
            if stop < 2:
                return

            pe.wait_ge(ev("cmp_kept"), 2)
            pe.wait_ge(ev("v_kept"), 4)
            starts = (0, 2, 5, 7)

            def attention_turn(i, first):
                def n_of(hh):
                    return i * 4 + hh

                def q_rot(hh):
                    if not (first and hh == 0):
                        pe.wait_ge(ev("scored"), n_of(hh))
                    pe.matmul(bank[2][:, 0:S], rot, arena[:, ds(i * 4 * S + hh * S, S)], start=True, stop=True)\
                      .then_inc(ev("q_rot"), 1)

                def scores(hh):
                    pe.wait_ge(ev("q_roped"), n_of(hh) + 1)
                    q = ar(A_MG + 20 * KB + (hh % 2) * S, S)
                    for tt in range(TT):
                        w = P * (tt + 1)
                        for b in range(2):
                            pe.matmul(bank[3 + tt][:, b * w:(b + 1) * w], q[:, tt * P:(tt + 1) * P],
                                      arena[:, ds(A_K + b * 4 * S + i * S, w)], start=True, stop=True)
                    for tt in range(TT):
                        mm = pe.matmul(bank[2][:, tt * NC:(tt + 1) * NC], q[:, tt * P:(tt + 1) * P],
                                       kc_group(i), start=True, stop=True)
                    mm.then_inc(ev("scores"), 1)

                def turn_p(hh):
                    pe.wait_ge(ev("probs"), n_of(hh) + 1)
                    if not (first and hh == 0):
                        pe.wait_ge(ev("p_kept_a"), n_of(hh))
                        pe.wait_ge(ev("p_kept_b"), n_of(hh))
                    pr = ar(A_MG + 8 * KB + (hh % 2) * 800, 798)
                    for b in range(2):
                        pe.transpose(bank[5][:, b * S:b * S + P], pr[:, b * P:(b + 1) * P], ident)
                        pe.transpose(bank[5][:, b * S + P:(b + 1) * S], pr[:, S + b * S:S + b * S + P], ident)
                    for b in range(2):
                        pe.transpose(bank[6][:, b * P:(b + 1) * P], pr[:, S + b * S + P:S + (b + 1) * S], ident)
                    for tt in range(TT):
                        mm = pe.transpose(bank[6][0:NC, S + tt * P:S + (tt + 1) * P],
                                          pr[:, 3 * S + tt * NC:3 * S + (tt + 1) * NC], ident)
                    mm.then_inc(ev("p_turned"), 1)

                def pv(hh):
                    pe.wait_ge(ev("p_kept_a"), n_of(hh) + 1)
                    pe.wait_ge(ev("p_kept_b"), n_of(hh) + 1)
                    pe.wait_ge(ev("v_staged"), i + 1)
                    if not (first and hh == 0):
                        pe.wait_ge(ev("o_lo"), n_of(hh))
                    pt = ar(A_MG + 16 * KB, 4 * S)
                    vs, vcs = ar(A_MG + 23 * KB, 4 * P), ar(A_MG + 25 * KB, P)
                    o = bank[7]
                    pe.matmul(o[:, 0:S], vs[:, 0:P], pt[:, 0:S], start=True, stop=False)
                    pe.matmul(o[:, 0:S], vs[:, 2 * P:3 * P], pt[:, S:2 * S], start=False, stop=False)
                    pe.matmul(o[:, 0:S], vcs[0:NC, :], pt[0:NC, 3 * S:4 * S], start=False, stop=False)
                    pe.matmul(o[:, P:S], vs[:, P:2 * P], pt[:, 2 * S:2 * S + P], start=False, stop=False)
                    pe.matmul(o[:, P:S], vs[:, 3 * P:4 * P], pt[:, 2 * S + P:3 * S], start=False, stop=True)\
                      .then_inc(ev("pv"), 1)

                for m in range(12):
                    if m in starts:
                        q_rot(starts.index(m))
                    tile(Tile(i, 12, T_ATT + m), act0_hi, act0_lo)
                    if m in starts:
                        scores(starts.index(m))
                    if m - 2 in starts:
                        turn_p(starts.index(m - 2))
                    if m - 3 in starts:
                        pv(starts.index(m - 3))

            def kc_group(i):
                return arena[:, ds(A_MG + 26 * KB + 128 + i * NC, NC)]

            attention_turn(0, True)
            with pe.Fori(1, GROUPS) as i:
                attention_turn(i, False)
            if stop < 3:
                return

            pe.wait_ge(ev("o_lo"), HEADS)
            pe.wait_ge(ev("dta_ready"), 1)
            dta = small[:, 96 + 64:96 + 128]
            pe.matmul(bank[2][:, 0:64], tri, dta, start=True, stop=True)
            pe.matmul(bank[2][:, 64:96], ones, dta[:, 0:32], start=True, stop=True).then_inc(ev("acs_sum"), 1)
            pe.wait_ge(ev("acs_kept"), 1)
            pe.wait_ge(ev("dte_in"), 1)

            xs_stage = ar(A_K, 4 * S)
            b_stage, c_stage = ar(A_K + 4 * KB, S), ar(A_K + 5 * KB, S)
            ebuf = [ar(A_K + (6 + 4 * c) * KB, PIECE) for c in range(2)]
            cs_buf = ar(A_K + 14 * KB, PIECE)
            xdt = [ar(A_K + (18 + 2 * c) * KB, 512) for c in range(2)]
            xde = ar(A_K + 22 * KB, 512)
            btok = small[:, 700:828]
            cbm = small[:, 444:700]

            def ssd_turn(i, first):
                T = Tile(i, 6, T_SSD)
                pe.wait_ge(ev("x_staged"), i + 1)
                if not first:
                    pe.wait_ge(ev("g_ready"), i)
                for c in range(2):
                    for t in range(4):
                        mm = pe.transpose(bank[2 + c][:, t * P:(t + 1) * P],
                                          xs_stage[:, t * S + c * P:t * S + (c + 1) * P], ident)
                mm.then_inc(ev("x_turned"), 1)
                pe.transpose(bank[6][:, 0:P], b_stage[:, 0:P], ident)
                for c in range(2):
                    mm = pe.matmul(bank[6][:, (1 + c) * P:(2 + c) * P], b_stage[:, c * P:(c + 1) * P],
                                   c_stage[:, c * P:(c + 1) * P], start=True, stop=True)
                mm.then_inc(ev("b_turned"), 1)
                tile(T, act0_hi, act0_lo)
                for c in range(2):
                    pe.wait_ge(ev("dtatri"), i * 2 + (c + 1))
                    if c == 1:
                        pe.wait_ge(ev("seg_ready"), i * 2 + 1)
                    for n in range(2):
                        mm = pe.matmul(bank[4 + n][:, :], ones, ebuf[c][:, n * 512:(n + 1) * 512],
                                       start=True, stop=True)
                    mm.then_inc(ev("acsb"), 1)
                    tile(T + (1 + c), act0_hi, act0_lo)
                pe.wait_ge(ev("xdt_ready"), i + 1)
                pe.wait_ge(ev("b_kept"), i + 1)
                if not first:
                    pe.wait_ge(ev("gsum_kept"), i)
                pe.matmul(bank[7][:, :], btok, xde, start=True, stop=True).then_inc(ev("state"), 1)
                tile(T + 3, act0_hi, act0_lo)
                pe.wait_ge(ev("m_ready"), i * 2 + 2)
                pe.wait_ge(ev("c_ready"), i + 1)
                pe.wait_ge(ev("state_kept"), i + 1)
                for t in range(4):
                    b, at = bank[2 + t // 2], (t % 2) * S
                    for r in (2 * t, 2 * t + 1):
                        rows = slice((r % 2) * SP_, (r % 2 + 1) * SP_)
                        head = slice(r * SP_, (r + 1) * SP_)
                        pe.matmul(b[rows, at:at + P], xdt[0][:, head], ebuf[0][:, r * P:(r + 1) * P],
                                  start=True, stop=True)
                        pe.matmul(b[rows, at + P:at + S], xdt[1][:, head], ebuf[1][:, r * P:(r + 1) * P],
                                  start=True, stop=False)
                        mm = pe.matmul(b[rows, at + P:at + S], xde[:, head], cs_buf[:, r * P:(r + 1) * P],
                                       start=False, stop=True)
                mm.then_inc(ev("y_sum"), 1)
                tile(T + 4, act0_hi, act0_lo)
                pe.wait_ge(ev("gsq_ready"), i + 1)
                for t in range(4):
                    mm = pe.matmul(bank[7][:, 0:S], ones, cs_buf[:, t * S:(t + 1) * S], start=(t == 0), stop=(t == 3))
                mm.then_inc(ev("gsum"), 1)
                tile(T + 5, act0_hi, act0_lo)

            ssd_turn(0, True)
            with pe.Fori(1, SG) as i:
                ssd_turn(i, False)
            if stop < 4:
                return

            stage(T_BN, KT, act1_hi, act1_lo)
            pe.wait_ge(ev("g_split"), 4)
            stage(T_BS, KT, act0_hi, act0_lo)
            pe.wait_ge(ev("merged_lo"), KT)
            stage(T_WO, KT, act1_hi, act1_lo)
            pe.wait_ge(ev("sumsq"), KT)
            pe.matmul(bank[2][:, 0:S], ones, ar(A_XBC + 16 * KB, S), start=True, stop=True).then_inc(ev("x2sum"), 1)
            pe.wait_ge(ev("x2g_lo"), KT)
            stage(T_WQ, KT, act0_hi, act0_lo)
            if stop < 5:
                return

            pe.wait_ge(tile_evicted, T_U)
            pe.wait_ge(ev("subk_in"), 16)
            qp, subk = ar(A_MG + 16 * KB, KT * S), ar(A_MG, 8 * KB)
            for n in range(8):
                if n >= 4:
                    pe.wait_ge(ev("s_kept"), n - 3)
                for m in range(4):
                    tt, hc = n // 4, (n % 4) * 4 + m
                    mm = pe.matmul(bank[4 + n % 4][:, m * P:(m + 1) * P], qp[:, hc * S + tt * P:hc * S + (tt + 1) * P],
                                   subk[:, hc * P:(hc + 1) * P], start=True, stop=True)
                mm.then_inc(ev("s_sum"), 1)
            stage(T_U, U1_T, act0_hi, act0_lo)
            pe.wait_ge(ev("gate_done"), 1)
            res = ar(A_Z - 3 * KB, 3 * S)
            for n in range(3):
                for tt in range(TT):
                    mm = pe.transpose(bank[2 + n][:, tt * P:(tt + 1) * P],
                                      res[:, n * S + tt * P:n * S + (tt + 1) * P], ident)
                mm.then_inc(ev("i_turned"), 1)
            stage(T_U2, NKEY - U1_T, act0_hi, act0_lo)
            if stop < 6:
                return

            pe.wait_ge(ev("i_kept"), 3)

            def w_turn(i, first):
                for b in range(2):
                    if not first:
                        pe.wait_ge(ev("w_used"), i * 2 + (b - 1))
                    pe.wait_ge(ev("ohi"), i * 8 + 4 * (b + 1))
                    pe.wait_ge(ev("gj"), i * 2 + (b + 1))
                    for t in range(4):
                        at = (b * 4 + t) * P
                        mm = pe.matmul(bank[2 + b][:, t * P:(t + 1) * P], onehot[:, at:at + P],
                                       onehot[:, 8 * P + at:9 * P + at], start=True, stop=True)
                    mm.then_inc(ev("w_sum"), 1)

            w_turn(0, True)
            with pe.Fori(1, S // 8) as i:
                w_turn(i, False)
            if stop < 7:
                return

            pe.wait_ge(ev("v_zero"), 1)

            def v_piece(p, m):
                hi, lo = piece_ap(w_hi, m), piece_ap(w_lo, m % 2)
                ah, al = av_hi[:, m * S:(m + 1) * S], av_lo[:, m * S:(m + 1) * S]
                pe.wait_ge(hi_ready, p + (P_V + 1))
                pe.wait_ge(ev("av_hi_r"), p + 1)
                for n, (w, x) in enumerate(((hi, ah), (hi, al), (lo, ah))):
                    if n == 1:
                        pe.wait_ge(ev("av_lo_r"), p + 1)
                    if n == 2:
                        pe.wait_ge(lo_ready, p + (P_V + 1))
                    for k in range(HKT):
                        mm = pe.matmul(bank[4 + k // 2][:, (k % 2) * S:(k % 2 + 1) * S], w[:, k * P:(k + 1) * P], x,
                                       start=False, stop=False, skip_group_check=True)
                mm.then_inc(piece_used, 1)

            zeros = onehot[:, 0:P]
            for s in range(2):
                if s == 1:
                    pe.wait_ge(ev("sweep_used"), 1)
                for b in range(4):
                    pe.matmul(bank[4 + b][:, :], zeros, onehot[:, 0:512], start=True, stop=False,
                              skip_group_check=True)
                with pe.Fori(s * 32, (s + 1) * 32) as i:
                    for m in range(4):
                        v_piece(i * 4 + m, m)
                for b in range(4):
                    mm = pe.matmul(bank[4 + b][:, :], zeros, onehot[:, 0:512], start=False, stop=True,
                                   skip_group_check=True)
                mm.then_inc(ev("sweep"), 1)
            pe.wait_ge(ev("fsq"), 1)
            for k in range(KT):
                mm = pe.matmul(bank[2][:, 0:S], ones, ar(k * S, S), start=(k == 0), stop=(k == KT - 1))
            mm.then_inc(ev("fsum"), 1)

        @block.scalar
        def _(act):
            st = Steps(act, a_step)
            act.dma_start(ar(A_MG, KT * S).rearrange("p (k t) -> p k t", k=KT), a["x"].rearrange("k p t -> p k t"))\
               .then_inc(x_in, 16)

            def hi(T, h):
                slot = (T.c % 2) * 2 + h
                act.wait_ge(raw_landed[slot], T.half(1) * 16)
                wait(act, piece_used, T.times(2, h - 3))
                act.activation(piece_ap(w_hi, slot), piece_ap(raw, slot), ACT.Copy).then_inc(hi_ready, 1)

            def pair(T):
                hi(T, 0)
                hi(T, 1)

            def stage(T0, n, evict, late=None, per=2):
                def turn(i, first):
                    for m in range(per):
                        pair(Tile(i, per, T0 + m))
                        if not (first and m == 0):
                            evict(Tile(i, per, m - 1))
                turn(0, True)
                with act.Fori(1, n // per) as i:
                    turn(i, False)
                evict(Tile(0, per, n - 1))

            def nothing(T):
                pass

            def keep_in(at, T0):
                def evict(T):
                    act.wait_ge(piece_used, T.times(2, 2 * T0 + 2))
                    act.activation(arena[:, ds(T.times(S, at), S)], bank[T.c % 2 ^ T0 % 2][:, 0:S], ACT.Copy)\
                       .then_inc(tile_evicted, 1)
                return evict

            act.wait_ge(par_in, 32)
            act.wait_ge(x_in, 16)
            act.activation(ar(0, KT * S), ar(A_MG, KT * S), ACT.Square).then_inc(st.sem, 1)
            st.n += 1
            act.wait_ge(ev("var_ready"), 1)
            act.activation(ar(A_K + S, S), ar(A_K, S), ACT.Sqrt).then_inc(ev("root_ready"), 1)
            for c in range(4):
                act.wait_ge(ev("h_ready"), c + 1)
                act.activation(act0_hi[:, c * PIECE:(c + 1) * PIECE], ar(A_MG + (16 + 4 * (c % 2)) * KB, PIECE), ACT.Copy)\
                   .then_inc(ev("h_hi"), 1)
            act.wait_ge(ev("h_hi"), 4)
            stage(T_A, QKV_A, keep_in(0, T_A))
            stage(T_B, QKV_B, keep_in(A_K, T_B))

            act.wait_ge(ev("g_turned"), 1)
            gsig = small[:, 0:96].rearrange("p (h s) -> p h s", s=6)
            for tt in range(TT):
                src = bank[6][:, tt * P:tt * P + 3 * HEADS].rearrange("p (h b) -> p h b", b=3)
                act.activation(gsig[:, :, 2 * tt:2 * tt + 2], src[:, :, 1:3], ACT.Sigmoid).then_inc(ev("g_kept"), 1)
                ins = act.activation(gsig[:, :, 4 + tt:5 + tt], src[:, :, 0:1], ACT.Sigmoid)
                st.mark(ins)
            st.wait()
            hid = [ar(A_MG + 26 * KB + c * 64, GROUPS * NC) for c in range(2)]
            for c in range(2):
                act.wait_ge(ev("hid_used"), c + 1)
                act.activation(hid[c], ar(A_MG + 27 * KB + c * 64, GROUPS * NC), ACT.Gelu).then_inc(ev("hid_ready"), 1)
            act.wait_ge(ev("cmp_out"), 1)
            act.activation(ar(A_MG + 26 * KB + 128, GROUPS * NC), bank[7][:, 0:GROUPS * NC], ACT.Copy)\
               .then_inc(ev("cmp_kept"), 1)
            act.activation(arena[0:NC, A_K + 12 * KB:A_K + 14 * KB], bank[6][0:NC, :], ACT.Copy)\
               .then_inc(ev("cmp_kept"), 1)
            if stop < 2:
                return

            starts = (0, 2, 5, 7)
            att_keep = keep_in(A_XBC, T_ATT)

            def attention_turn(i, first):
                def n_of(hh):
                    return i * 4 + hh

                def exps(hh):
                    act.wait_ge(ev("scored"), n_of(hh) + 1)
                    pr = ar(A_MG + 8 * KB + (hh % 2) * 800, 798)
                    nm, sm = small[:, 360 + (hh % 2) * 24:366 + (hh % 2) * 24], small[:, 366 + (hh % 2) * 24:372 + (hh % 2) * 24]
                    cuts = [(b * P, P) for b in range(2)] + [(S + b * S, S) for b in range(2)] + \
                           [(3 * S + tt * NC, NC) for tt in range(TT)]
                    for n, (at, w) in enumerate(cuts):
                        last = act.activation(pr[:, at:at + w], pr[:, at:at + w], ACT.Exp, bias=nm[:, n:n + 1],
                                              accum_out=sm[:, n:n + 1]).then_inc(ev("exps"), 1)

                def keep_pt(hh):
                    act.wait_ge(ev("p_turned"), n_of(hh) + 1)
                    if not (first and hh == 0):
                        act.wait_ge(ev("pv"), n_of(hh))
                    act.activation(ar(A_MG + 16 * KB, 2 * S), bank[5][:, :], ACT.Copy).then_inc(ev("p_kept_a"), 1)

                def keep_o(hh):
                    act.wait_ge(ev("pv"), n_of(hh) + 1)
                    act.activation(act1_hi[:, ds(i * 4 * S + hh * S, S)], bank[7][:, 0:S], ACT.Copy)\
                       .then_inc(ev("o_hi"), 1)

                for m in range(12):
                    pair(Tile(i, 12, T_ATT + m))
                    if m - 2 in starts:
                        exps(starts.index(m - 2))
                    if not (first and m == 0):
                        att_keep(Tile(i, 12, m - 1))
                    if m - 3 in starts:
                        keep_pt(starts.index(m - 3))
                    if m - 4 in starts:
                        keep_o(starts.index(m - 4))

            attention_turn(0, True)
            with act.Fori(1, GROUPS) as i:
                attention_turn(i, False)
            att_keep(Tile(0, 12, ATT_T - 1))
            if stop < 3:
                return

            tmp = ar(A_MG + 8 * KB, 64 * 12)
            act.wait_ge(ev("dt_in"), 1)
            act.activation(tmp[:, 64:128], tmp[:, 0:64], ACT.Exp, scale=-1.0).then_inc(ev("dt_exp"), 1)
            act.activation(tmp[:, 128:160], par[:, V_AL:V_AL + 32], ACT.Exp).then_inc(ev("dt_exp"), 1)
            act.wait_ge(ev("acs_kept"), 1)
            act.wait_ge(ev("dte_in"), 1)
            act.activation(small[:, 328:360], small[:, 328:360], ACT.Exp).then_inc(ev("dte_ready"), 1)
            act.wait_ge(tile_evicted, T_SSD)
            act.activation(ar(A_Z, Z_T * S), ar(A_Z, Z_T * S), ACT.Silu).then_inc(ev("z_done"), 1)

            def silu_turn(i):
                for m in range(2):
                    act.wait_ge(ev("conv_done"), i * 2 + (m + 1))
                    act.activation(arena[:, ds(A_XBC + i * 2 * S + m * S, S)], ar(A_MG + (12 + m) * KB, S), ACT.Silu)\
                       .then_inc(ev("silu_done"), 1)
            with act.Fori(0, XBC_T // 2) as i:
                silu_turn(i)

            ebuf = [ar(A_K + (6 + 4 * c) * KB, PIECE) for c in range(2)]
            cs_buf = ar(A_K + 14 * KB, PIECE)
            xde = ar(A_K + 22 * KB, 512)
            btok = small[:, 700:828]
            ssd_keep = keep_in(A_MG + 8 * KB, T_SSD)

            def ssd_turn(i, first):
                def evict(m):
                    if not (first and m == 0):
                        ssd_keep(Tile(i, 6, m - 1))
                pair(Tile(i, 6, T_SSD))
                evict(0)
                act.wait_ge(ev("b_turned"), i + 1)
                if not first:
                    act.wait_ge(ev("state"), i)
                act.activation(btok, bank[6][:, 0:P], ACT.Copy).then_inc(ev("b_kept"), 1)
                pair(Tile(i, 6, T_SSD + 1))
                evict(1)
                pair(Tile(i, 6, T_SSD + 2))
                act.wait_ge(ev("seg_ready"), i * 2 + 1)
                act.activation(ebuf[0], ebuf[0], ACT.Exp).then_inc(ev("seg_exp"), 1)
                evict(2)
                pair(Tile(i, 6, T_SSD + 3))
                act.wait_ge(ev("acsb"), i * 2 + 2)
                act.wait_ge(ev("seg_ready"), i * 2 + 2)
                if not first:
                    act.wait_ge(ev("gsum"), i)
                for n in range(2):
                    act.activation(cs_buf[:, n * 512:(n + 1) * 512], bank[4 + n][:, :], ACT.Exp)\
                       .then_inc(ev("c_exp"), 1)
                act.activation(ebuf[1], ebuf[1], ACT.Exp).then_inc(ev("seg_exp"), 1)
                evict(3)
                act.wait_ge(ev("state"), i + 1)
                act.activation(xde, bank[7][:, :], ACT.Copy).then_inc(ev("state_kept"), 1)
                pair(Tile(i, 6, T_SSD + 4))
                evict(4)
                pair(Tile(i, 6, T_SSD + 5))
                act.wait_ge(ev("g_ready"), i + 1)
                act.activation(cs_buf, arena[:, ds(A_Z + i * 4 * S, 4 * S)], ACT.Square).then_inc(ev("gsq_ready"), 1)
                evict(5)

            ssd_turn(0, True)
            with act.Fori(1, SG) as i:
                ssd_turn(i, False)
            ssd_keep(Tile(0, 6, SSD_T - 1))
            if stop < 4:
                return

            act.wait_ge(ev("gvar"), 1)
            act.activation(ar(A_K + 4 * KB, 4 * S), ar(A_K, 4 * S), ACT.Sqrt).then_inc(ev("groot"), 1)

            def gate0(T):
                act.activation(arena[:, ds(T.times(S, A_MG), S)], arena[:, ds(T.times(S, A_MG), S)], ACT.Sigmoid,
                               bias=par[:, ds(T.times(1, V_GB), 1)]).then_inc(ev("gate_ready"), 1)

            def gate1(T):
                act.activation(arena[:, ds(T.times(S, A_MG + KT * S), S)], arena[:, ds(T.times(S, A_MG + KT * S), S)],
                               ACT.Sigmoid, bias=par[:, ds(T.times(1, V_GB + KT), 1)]).then_inc(ev("gate_ready"), 1)

            stage(T_BN, KT, gate0)
            for c in range(4):
                act.wait_ge(ev("gn_ready"), c + 1)
                act.activation(act0_hi[:, c * PIECE:(c + 1) * PIECE], ar(A_Z + c * PIECE, PIECE), ACT.Copy)\
                   .then_inc(ev("gn_hi"), 1)

            def bs(T):
                gate1(T)
                act.wait_ge(ev("merged"), T.times(1, 1))
                act.activation(act1_hi[:, ds(T.times(S), S)], arena[:, ds(T.times(S, A_MG), S)], ACT.Copy)\
                   .then_inc(ev("merged_hi"), 1)

            stage(T_BS, KT, bs)

            def wo(T):
                act.wait_ge(ev("x2_ready"), T.times(1, 1))
                act.activation(act0_hi[:, ds(T.times(S), S)], arena[:, ds(T.times(S, A_MG), S)], ACT.Copy)\
                   .then_inc(ev("x2g_hi"), 1)

            stage(T_WO, KT, wo)
            act.wait_ge(ev("x2var"), 1)
            act.activation(ar(A_XBC + 18 * KB, S), ar(A_XBC + 17 * KB, S), ACT.Sqrt).then_inc(ev("x2root"), 1)
            stage(T_WQ, KT, nothing)
            if stop < 5:
                return

            s_all = ar(A_Z, KT * S)
            for n in range(1, 8, 2):
                act.wait_ge(ev("s_sum"), n + 1)
                act.wait_ge(ev("s_kept"), n)
                act.wait_ge(ev("spilled"), 16)
                act.activation(s_all[:, n * 512:(n + 1) * 512], bank[4 + n % 4][:, :], ACT.Copy).then_inc(ev("s_kept"), 1)

            def gelu(T0):
                def evict(T):
                    act.wait_ge(ev("dots_scaled"), T.times(1, T0 + 1))
                    act.activation(arena[:, ds(T.times(S, T0 * S), S)], arena[:, ds(T.times(S, T0 * S), S)], ACT.Gelu)\
                       .then_inc(ev("g_done"), 1)
                return evict

            stage(T_U, U1_T, gelu(0))
            act.wait_ge(ev("gate_in"), 1)
            gates = ar(A_Z - 3 * KB + 2 * S, S)
            act.activation(gates, gates, ACT.Exp).then_inc(ev("gate_exp"), 1)
            stage(T_U2, NKEY - U1_T, gelu(U1_T))
            if stop < 7:
                return

            def v_pieces(i, first):
                for m in range(4):
                    act.wait_ge(raw_landed[m], (i + (P_V // 4 + 1)) * 16)
                    act.wait_ge(piece_used, i * 4 + (P_V + m - 3))
                    act.activation(piece_ap(w_hi, m), piece_ap(raw, m), ACT.Copy).then_inc(hi_ready, 1)
                    j = arena[:, ds((i if first else i - 32) * 4 * S + m * S, S)]
                    act.activation(av_hi[:, m * S:(m + 1) * S], j, ACT.Copy).then_inc(ev("av_hi_r"), 1)

            act.wait_ge(ev("w_used"), S // 4)
            with act.Fori(0, 32) as i:
                v_pieces(i, True)
            with act.Fori(32, 64) as i:
                v_pieces(i, False)
            act.wait_ge(ev("sweep_used"), 2)
            act.activation(ar(0, KT * S), x3[:, :], ACT.Square).then_inc(ev("fsq"), 1)
            act.wait_ge(ev("fvar"), 1)
            act.activation(ar(A_XBC + S, S), ar(A_XBC, S), ACT.Sqrt).then_inc(ev("froot"), 1)

        @block.vector
        def _(v):
            st = Steps(v, v_step)

            def lo(T, h):
                slot = (T.c % 2) * 2 + h
                v.wait_ge(hi_ready, T.times(2, h + 1))
                wait(v, piece_used, T.times(2, h - 1))
                v.tensor_tensor(piece_ap(w_lo, slot % 2), piece_ap(raw, slot), piece_ap(w_hi, slot).bitcast(F32),
                                ALU.subtract).then_inc(lo_ready, 1)

            def pair(T):
                lo(T, 0)
                lo(T, 1)

            def stage(T0, n, evict=None, steps=0, late=None, per=2):
                def turn(i, first):
                    for m in range(per):
                        pair(Tile(i, per, T0 + m))
                        if late and not (first and m < 2):
                            late(Tile(i, per, m - 2))
                        if evict and not (first and m == 0):
                            evict(Tile(i, per, m - 1))
                turn(0, True)
                st.turns(1, n // per, per * steps, lambda i: turn(i, False))
                if late:
                    late(Tile(0, per, n - 2))
                if evict:
                    evict(Tile(0, per, n - 1))
                if late:
                    late(Tile(0, per, n - 1))

            def rstd(total, n, var, root, t1, out, var_ev, root_ev):
                v.tensor_scalar(var, total, 1.0 / n, EPS, ALU.mult, ALU.add).then_inc(var_ev, 1)
                v.wait_ge(root_ev, 1)
                st(v.reciprocal(out, root))
                st(v.tensor_tensor(t1, out, out, ALU.mult))
                st(v.tensor_tensor(t1, t1, var, ALU.mult))
                st(v.tensor_scalar(t1, t1, -0.5, 1.5, ALU.mult, ALU.add))
                st(v.tensor_tensor(out, out, t1, ALU.mult))

            v.wait_ge(a_step, 1)
            v.wait_ge(par_in, 32)
            v.tensor_reduce(ar(A_VTOK, S), ar(0, KT * S).rearrange("p (k t) -> p t k", k=KT), AX.X, ALU.add)\
             .then_inc(ev("sq_ready"), 1)
            v.wait_ge(ev("sum_ready"), 1)
            r1 = ar(A_K + 2 * S, S)
            rstd(bank[2][:, 0:S], D, ar(A_K, S), ar(A_K + S, S), ar(A_K + 3 * S, S), r1,
                 ev("var_ready"), ev("root_ready"))
            for c in range(4):
                buf = ar(A_MG + (16 + 4 * (c % 2)) * KB, PIECE)
                for k in range(4):
                    kt = 4 * c + k
                    ins = v.scalar_tensor_tensor(buf[:, k * S:(k + 1) * S], ar(A_MG + kt * S, S),
                                                 par[:, V_AN + kt:V_AN + kt + 1], r1, ALU.mult, ALU.mult)
                    st.mark(ins)
                st.wait()
                v.nop().then_inc(ev("h_ready"), 1)
                v.wait_ge(ev("h_hi"), c + 1)
                v.tensor_tensor(act0_lo[:, c * PIECE:(c + 1) * PIECE], buf,
                                act0_hi[:, c * PIECE:(c + 1) * PIECE].bitcast(F32), ALU.subtract)\
                 .then_inc(ev("h_split"), 1)
                v.wait_ge(ev("h_split"), c + 1)
            stage(T_A, QKV_A)
            stage(T_B, QKV_B)

            v.wait_ge(phase_in, 16)
            v.wait_ge(tile_evicted, T_ATT)
            scratch = ar(A_MG + 8 * KB, 512)
            two = lambda x: x.unsqueeze(1).broadcast_to([P, 2, S])
            pair2 = lambda x: x.rearrange("p (b t) -> p b t", b=2)
            for n in range(6):
                k = ar(A_K + n * 512, 512)
                v.wait_ge(ev("krot"), n + 1)
                st(v.tensor_tensor(pair2(scratch), pair2(bank[2 + n % 4][:, :]), two(sin_t), ALU.mult))
                st(v.tensor_tensor(pair2(k), pair2(k), two(cos_t), ALU.mult))
                st(v.tensor_tensor(k, k, scratch, ALU.add))
                v.nop().then_inc(ev("krope"), 1)
            for n in range(4):
                v.wait_ge(ev("v_turned"), n + 1)
                v.tensor_copy(ar(A_VTOK + n * 512, 512), bank[2 + n][:, :]).then_inc(ev("v_kept"), 1)
            v.wait_ge(ev("g_kept"), 2)
            v.wait_ge(a_step, 3)
            dt2 = small[:, 96:160].rearrange("p (c h) -> p c h", c=2)
            v.tensor_tensor(dt2, bank[6][:, 2 * P:4 * P].rearrange("p (c h) -> p c h", c=2)[:, :, 0:SH],
                            par[:, V_DTB:V_DTB + SH].unsqueeze(1).broadcast_to([P, 2, SH]), ALU.add)\
             .then_inc(ev("g_kept"), 1)
            for c in range(2):
                v.wait_ge(ev("hid_sum"), c + 1)
                st(v.tensor_tensor(small[:, 360 + c:361 + c], bank[1][:, 0:1], par[:, V_B1 + c:V_B1 + c + 1], ALU.add))
                v.tensor_scalar(ar(A_MG + 27 * KB + c * 64, GROUPS * NC), bank[0][:, 0:GROUPS * NC],
                                small[:, 360 + c:361 + c], None, ALU.add).then_inc(ev("hid_used"), 1)
            if stop < 2:
                return

            starts = (0, 2, 5, 7)
            gsig = small[:, 0:96]

            def attention_turn(i, first):
                def n_of(hh):
                    return i * 4 + hh

                def bufs(hh):
                    o = 360 + (hh % 2) * 24
                    return (ar(A_MG + 8 * KB + (hh % 2) * 800, 798), small[:, o:o + 6], small[:, o + 6:o + 12],
                            small[:, o + 12:o + 18])

                def rope(hh):
                    v.wait_ge(ev("q_rot"), n_of(hh) + 1)
                    q = ar(A_MG + 20 * KB + (hh % 2) * S, S)
                    t = ar(A_MG + 22 * KB, S)
                    st.mark(v.tensor_tensor(t, bank[2][:, 0:S], sin_t, ALU.mult))
                    st(v.tensor_tensor(q, arena[:, ds(i * 4 * S + hh * S, S)], cos_t, ALU.mult))
                    v.tensor_tensor(q, q, t, ALU.add).then_inc(ev("q_roped"), 1)
                    v.wait_ge(ev("q_roped"), n_of(hh) + 1)

                def score(hh):
                    v.wait_ge(ev("scores"), n_of(hh) + 1)
                    if not (first and hh < 2):
                        v.wait_ge(ev("p_turned"), n_of(hh) - 1)
                    pr, nm, sm, wg = bufs(hh)
                    m0 = mask_t[:, P:S].unsqueeze(1).broadcast_to([P, 2, P])
                    s0 = pr[:, 0:S].rearrange("p (b s) -> p b s", b=2)
                    s1 = pr[:, S:3 * S].rearrange("p (b s) -> p b s", b=2)
                    s2 = pr[:, 3 * S:3 * S + 2 * NC].rearrange("p (b s) -> p b s", b=2)
                    st.mark(v.scalar_tensor_tensor(s0, bank[3][:, 0:S].rearrange("p (b s) -> p b s", b=2), SCALE, m0,
                                                   ALU.mult, ALU.add))
                    st.mark(v.scalar_tensor_tensor(s1, bank[4][:, :].rearrange("p (b s) -> p b s", b=2), SCALE,
                                                   two(mask_t), ALU.mult, ALU.add))
                    st(v.scalar_tensor_tensor(pr[:, 3 * S:3 * S + 2 * NC], bank[2][:, 0:2 * NC], SCALE,
                                              cmp_bias, ALU.mult, ALU.add))
                    st.mark(v.tensor_reduce(nm[:, 0:2], s0, AX.X, ALU.max, negate=True))
                    st.mark(v.tensor_reduce(nm[:, 2:4], s1, AX.X, ALU.max, negate=True))
                    v.tensor_reduce(nm[:, 4:6], s2, AX.X, ALU.max, negate=True).then_inc(ev("scored"), 1)
                    st.wait()

                def probs(hh):
                    v.wait_ge(ev("exps"), i * 24 + 6 * (hh + 1))
                    pr, nm, sm, wg = bufs(hh)
                    st(v.reciprocal(wg, sm))
                    st(v.tensor_tensor(wg, wg, gsig_at(i, hh), ALU.mult))
                    s0 = pr[:, 0:S].rearrange("p (b s) -> p b s", b=2)
                    s1 = pr[:, S:3 * S].rearrange("p (b s) -> p b s", b=2)
                    s2 = pr[:, 3 * S:3 * S + 2 * NC].rearrange("p (b s) -> p b s", b=2)
                    st(v.tensor_tensor(s2, s2, cmp_01.rearrange("p (b s) -> p b s", b=2), ALU.mult))
                    st.mark(v.tensor_tensor(s2, s2, wg[:, 4:6].unsqueeze(2).broadcast_to([P, 2, NC]), ALU.mult))
                    st.mark(v.tensor_tensor(s0, s0, wg[:, 0:2].unsqueeze(2).broadcast_to([P, 2, P]), ALU.mult))
                    st(v.tensor_tensor(s1, s1, wg[:, 2:4].unsqueeze(2).broadcast_to([P, 2, S]), ALU.mult))
                    v.nop().then_inc(ev("probs"), 1)

                def gsig_at(i, hh):
                    return small[:, ds(i * 24 + hh * 6, 6)]

                def keep_pt(hh):
                    v.wait_ge(ev("p_turned"), n_of(hh) + 1)
                    pt = ar(A_MG + 16 * KB, 4 * S)
                    if not (first and hh == 0):
                        v.wait_ge(ev("pv"), n_of(hh))
                    st(v.tensor_copy(pt[:, 2 * S:3 * S], bank[6][:, 0:S]))
                    v.tensor_copy(pt[0:NC, 3 * S:4 * S], bank[6][0:NC, S:2 * S]).then_inc(ev("p_kept_b"), 1)

                def keep_o(hh):
                    v.wait_ge(ev("o_hi"), n_of(hh) + 1)
                    v.tensor_tensor(act1_lo[:, ds(i * 4 * S + hh * S, S)], bank[7][:, 0:S],
                                    act1_hi[:, ds(i * 4 * S + hh * S, S)].bitcast(F32), ALU.subtract)\
                     .then_inc(ev("o_lo"), 1)

                for m in range(12):
                    pair(Tile(i, 12, T_ATT + m))
                    if m in starts:
                        rope(starts.index(m))
                    if m - 1 in starts:
                        score(starts.index(m - 1))
                    if m - 2 in starts:
                        probs(starts.index(m - 2))
                    if m - 3 in starts:
                        keep_pt(starts.index(m - 3))
                    if m - 4 in starts:
                        keep_o(starts.index(m - 4))

            attention_turn(0, True)
            st.turns(1, GROUPS, 4 * 14, lambda i: attention_turn(i, False))
            if stop < 3:
                return

            tmp = ar(A_MG + 8 * KB, 64 * 12)
            x_dt, dta, acs = small[:, 96:160], small[:, 160:224], small[:, 224:288]
            dtdte, dte = small[:, 288:320], small[:, 328:360]
            v.wait_ge(ev("p_turned"), HEADS)
            st(v.tensor_scalar(tmp[:, 192:256], x_dt, -1.0, None, ALU.mult))
            v.tensor_tensor(tmp[:, 0:64], x_dt, tmp[:, 192:256], ALU.max).then_inc(ev("dt_in"), 1)
            v.wait_ge(ev("dt_exp"), 2)
            u, s_, s2, acc = tmp[:, 64:128], tmp[:, 256:320], tmp[:, 320:384], tmp[:, 384:448]
            st(v.tensor_scalar(s_, u, 2.0, None, ALU.add))
            st(v.reciprocal(s_, s_))
            st(v.tensor_tensor(s_, s_, u, ALU.mult))
            st(v.tensor_tensor(s2, s_, s_, ALU.mult))
            st(v.tensor_scalar(acc, s2, 1.0 / 17, 1.0 / 15, ALU.mult, ALU.add))
            for k in (13, 11, 9, 7, 5, 3, 1):
                st(v.tensor_tensor(acc, acc, s2, ALU.mult))
                st(v.tensor_scalar(acc, acc, 1.0 / k, None, ALU.add))
            st(v.tensor_tensor(acc, acc, s_, ALU.mult))
            st(v.tensor_scalar(x_dt, x_dt, 0.0, None, ALU.max))
            st(v.scalar_tensor_tensor(x_dt, acc, 2.0, x_dt, ALU.mult, ALU.add))
            st(v.tensor_scalar(tmp[:, 128:160], tmp[:, 128:160], -1.0, None, ALU.mult))
            v.tensor_tensor(dta.rearrange("p (c h) -> p c h", c=2), x_dt.rearrange("p (c h) -> p c h", c=2),
                            tmp[:, 128:160].unsqueeze(1).broadcast_to([P, 2, SH]), ALU.mult)\
             .then_inc(ev("dta_ready"), 1)
            v.wait_ge(ev("acs_sum"), 1)
            v.tensor_copy(acs, bank[2][:, 0:64]).then_inc(ev("acs_kept"), 1)
            v.wait_ge(ev("acs_kept"), 1)
            v.tensor_tensor(dte, bank[2][:, 64:96], acs[:, 0:32], ALU.subtract).then_inc(ev("dte_in"), 1)
            v.wait_ge(ev("dte_ready"), 1)
            st(v.tensor_tensor(dtdte, dte, x_dt[:, 0:32], ALU.mult))

            v.wait_ge(tile_evicted, T_SSD)

            def conv_turn(i, first):
                for m in range(2):
                    u = arena[:, ds(A_XBC + i * 2 * S + m * S, S)]
                    out = ar(A_MG + (12 + m) * KB, S)
                    if not first:
                        v.wait_ge(ev("silu_done"), i * 2 + (m - 1))
                    cw = lambda k: par[:, ds(i * 8 + (V_CW + m * 4 + k), 1)]
                    st(v.tensor_scalar(out, u, cw(3), par[:, ds(i * 2 + (V_CB + m), 1)], ALU.mult, ALU.add))
                    for n in range(1, CONV):
                        ins = v.scalar_tensor_tensor(
                            out[:, n:S], arena[:, ds(A_XBC + i * 2 * S + m * S, S - n)], cw(3 - n), out[:, n:S],
                            ALU.mult, ALU.add)
                        if n < CONV - 1:
                            st(ins)
                        else:
                            ins.then_inc(ev("conv_done"), 1)
            conv_turn(0, True)
            st.turns(1, XBC_T // 2, 6, lambda i: conv_turn(i, False))

            xs_stage = ar(A_K, 4 * S)
            c_stage = ar(A_K + 5 * KB, S)
            ebuf = [ar(A_K + (6 + 4 * c) * KB, PIECE) for c in range(2)]
            cs_buf = ar(A_K + 14 * KB, PIECE)
            xdt = [ar(A_K + (18 + 2 * c) * KB, 512) for c in range(2)]
            xde = ar(A_K + 22 * KB, 512)
            cbm = small[:, 444:700]
            v.wait_ge(ev("silu_done"), XBC_T)
            v.wait_ge(ev("z_done"), 1)

            def heads(x):
                return x.rearrange("p (r l) -> p r l", r=SHG)

            def over(x, n):
                return x.unsqueeze(2).broadcast_to([P, SHG, n])

            def ssd_turn(i, first):
                def per_head(t, c):
                    return small[:, ds(i * 8 + (t + 32 * c), 8)]
                if not first:
                    v.wait_ge(ev("y_sum"), i)
                for c in range(2):
                    v.tensor_tensor(heads(ebuf[c]), tri.unsqueeze(1).broadcast_to([P, SHG, P]),
                                    over(per_head(160, c), P), ALU.mult).then_inc(ev("dtatri"), 1)
                pair(Tile(i, 6, T_SSD))
                v.wait_ge(ev("x_turned"), i + 1)
                for c in range(2):
                    st.mark(v.tensor_tensor(xdt[c].rearrange("p (r d) -> p r d", r=SHG),
                                            bank[2 + c][:, :].rearrange("p (r d) -> p r d", r=SHG),
                                            over(per_head(96, c), SP_), ALU.mult))
                st(v.tensor_tensor(xde.rearrange("p (r d) -> p r d", r=SHG),
                                   bank[2][:, :].rearrange("p (r d) -> p r d", r=SHG),
                                   over(small[:, ds(i * 8 + 288, 8)], SP_), ALU.mult))
                v.nop().then_inc(ev("xdt_ready"), 1)
                v.wait_ge(ev("b_kept"), i + 1)
                st(v.tensor_tensor(cbm.rearrange("p (c l) -> p c l", c=2),
                                   bank[6][:, P:3 * P].rearrange("p (c l) -> p c l", c=2),
                                   tri.unsqueeze(1).broadcast_to([P, 2, P]), ALU.mult))
                pair(Tile(i, 6, T_SSD + 1))

                def seg(c):
                    v.wait_ge(ev("acsb"), i * 2 + (c + 1))
                    for n in range(2):
                        ins = v.tensor_tensor(
                            ebuf[c][:, n * 512:(n + 1) * 512].rearrange("p (r l) -> p r l", r=4),
                            bank[4 + n][:, :].rearrange("p (r l) -> p r l", r=4),
                            small[:, ds(i * 8 + (224 + 32 * c + 4 * n), 4)].unsqueeze(2).broadcast_to([P, 4, P]),
                            ALU.subtract)
                        st.mark(ins)
                    st.wait()
                    v.tensor_scalar(ebuf[c], ebuf[c], 0.0, None, ALU.min).then_inc(ev("seg_ready"), 1)

                def decay(c):
                    v.wait_ge(ev("seg_exp"), i * 2 + (c + 1))
                    v.tensor_tensor(heads(ebuf[c]), heads(ebuf[c]),
                                    cbm[:, c * P:(c + 1) * P].unsqueeze(1).broadcast_to([P, SHG, P]),
                                    ALU.mult).then_inc(ev("m_ready"), 1)

                seg(0)
                pair(Tile(i, 6, T_SSD + 2))
                seg(1)
                pair(Tile(i, 6, T_SSD + 3))
                decay(0)
                decay(1)
                v.wait_ge(ev("c_exp"), i * 2 + 2)
                v.tensor_tensor(heads(cs_buf), heads(cs_buf), c_stage[:, P:S].unsqueeze(1).broadcast_to([P, SHG, P]),
                                ALU.mult).then_inc(ev("c_ready"), 1)
                pair(Tile(i, 6, T_SSD + 4))
                v.wait_ge(ev("y_sum"), i + 1)
                for t in range(4):
                    st.mark(v.scalar_tensor_tensor(xs_stage[:, t * S:(t + 1) * S], xs_stage[:, t * S:(t + 1) * S],
                                                   par[:, ds(i * 4 + (V_DS + t), 1)],
                                                   bank[2 + t // 2][:, (t % 2) * S:(t % 2 + 1) * S],
                                                   ALU.mult, ALU.add))
                st.wait()
                zt = arena[:, ds(A_Z + i * 4 * S, 4 * S)]
                v.tensor_tensor(zt, zt, xs_stage, ALU.mult).then_inc(ev("g_ready"), 1)
                pair(Tile(i, 6, T_SSD + 5))
                v.wait_ge(ev("gsum"), i + 1)
                v.tensor_copy(arena[:, ds(A_XBC + i * 4 * S, S)], bank[7][:, 0:S]).then_inc(ev("gsum_kept"), 1)

            SSD_STEPS = 3 + 1 + 4 + 4
            ssd_turn(0, True)
            st.turns(1, SG, SSD_STEPS, lambda i: ssd_turn(i, False))
            if stop < 4:
                return

            v.wait_ge(ev("gsum_kept"), SG)
            gs = ar(A_XBC, 16 * S).rearrange("p (g t) -> p g t", g=SG)[:, :, 0:S]
            g4 = lambda x: x.rearrange("p (g t) -> p g t", g=SG)
            gvar, groot, gr, gt = (ar(A_K + 4 * k * KB, 4 * S) for k in range(4))
            v.wait_ge(ev("y_sum"), SG)
            rstd(gs, 4 * P, g4(gvar), g4(groot), g4(gt), g4(gr), ev("gvar"), ev("groot"))

            def bn(T):
                v.wait_ge(ev("gate_ready"), T.times(1, 1))
                v.wait_ge(piece_used, T.times(2, 2 * T_BN + 2))
                m0 = arena[:, ds(T.times(S, A_MG), S)]
                v.tensor_tensor(m0, m0, bank[T.c % 2][:, 0:S], ALU.mult).then_inc(tile_evicted, 1)

            v.wait_ge(piece_used, 2 * T_BN)
            for c in range(4):
                for k in range(4):
                    t = 4 * c + k
                    z = ar(A_Z + t * S, S)
                    st.mark(v.scalar_tensor_tensor(z, z, par[:, V_SN + t:V_SN + t + 1], gr[:, c * S:(c + 1) * S],
                                                   ALU.mult, ALU.mult))
                st.wait()
                v.nop().then_inc(ev("gn_ready"), 1)
            stage(T_BN, KT, bn)
            for c in range(4):
                v.wait_ge(ev("gn_hi"), c + 1)
                v.tensor_tensor(act0_lo[:, c * PIECE:(c + 1) * PIECE], ar(A_Z + c * PIECE, PIECE),
                                act0_hi[:, c * PIECE:(c + 1) * PIECE].bitcast(F32), ALU.subtract)\
                 .then_inc(ev("g_split"), 1)

            def bs(T):
                v.wait_ge(ev("gate_ready"), T.times(1, KT + 1))
                v.wait_ge(piece_used, T.times(2, 2 * T_BS + 2))
                m1 = arena[:, ds(T.times(S, A_MG + KT * S), S)]
                m0 = arena[:, ds(T.times(S, A_MG), S)]
                v.tensor_tensor(m1, m1, bank[T.c % 2][:, 0:S], ALU.mult).then_inc(tile_evicted, 1)
                v.wait_ge(tile_evicted, T.times(1, T_BS + 1))
                v.tensor_tensor(m0, m0, m1, ALU.add).then_inc(ev("merged"), 1)

            def bs_lo(T):
                v.wait_ge(ev("merged_hi"), T.times(1, 1))
                v.tensor_tensor(act1_lo[:, ds(T.times(S), S)], arena[:, ds(T.times(S, A_MG), S)],
                                act1_hi[:, ds(T.times(S), S)].bitcast(F32), ALU.subtract)\
                 .then_inc(ev("merged_lo"), 1)

            stage(T_BS, KT, bs, late=bs_lo)

            def wo(T):
                v.wait_ge(piece_used, T.times(2, 2 * T_WO + 2))
                x2 = arena[:, ds(T.times(S, A_Z), S)]
                v.tensor_tensor(x2, bank[T.c % 2][:, 0:S], arena[:, ds(T.times(S, A_XBC), S)], ALU.add)\
                 .then_inc(tile_evicted, 1)
                v.wait_ge(tile_evicted, T.times(1, T_WO + 1))
                v.tensor_scalar(arena[:, ds(T.times(S, A_MG), S)], x2, par[:, ds(T.times(1, V_FN), 1)], None, ALU.mult)\
                 .then_inc(ev("x2_ready"), 1)

            def wo_lo(T):
                v.wait_ge(ev("x2g_hi"), T.times(1, 1))
                v.tensor_tensor(act0_lo[:, ds(T.times(S), S)], arena[:, ds(T.times(S, A_MG), S)],
                                act0_hi[:, ds(T.times(S), S)].bitcast(F32), ALU.subtract)\
                 .then_inc(ev("x2g_lo"), 1)

            v.wait_ge(ev("res_in"), 16)
            stage(T_WO, KT, wo, late=wo_lo)
            v.wait_ge(ev("x2sum"), 1)
            rstd(bank[2][:, 0:S], D, ar(A_XBC + 17 * KB, S), ar(A_XBC + 18 * KB, S), ar(A_XBC + 19 * KB, S), r2,
                 ev("x2var"), ev("x2root"))

            def wq(T):
                v.wait_ge(piece_used, T.times(2, 2 * T_WQ + 2))
                v.tensor_tensor(arena[:, ds(T.times(S, A_MG + 16 * KB), S)], bank[T.c % 2][:, 0:S], r2, ALU.mult)\
                 .then_inc(tile_evicted, 1)

            stage(T_WQ, KT, wq)
            if stop < 5:
                return

            s_all = ar(A_Z, KT * S)
            v.wait_ge(ev("spilled"), 16)
            for n in range(0, 8, 2):
                v.wait_ge(ev("s_sum"), n + 1)
                v.wait_ge(ev("s_kept"), n)
                v.tensor_copy(s_all[:, n * 512:(n + 1) * 512], bank[4 + n % 4][:, :]).then_inc(ev("s_kept"), 1)
            v.wait_ge(ev("s_kept"), 8)

            top = ar(A_MG, 16 * KB)
            sc, sc2 = top[:, 0:S], top[:, S:2 * S]
            cand, cand2 = top[:, 2 * S:3 * S], top[:, 3 * S:4 * S]
            eq = top[:, 4 * S:5 * S]
            sv, sif = top[:, 5 * S:5 * S + 32], top[:, 5 * S + 32:5 * S + 64]
            si = top[:, 5 * S + 64:5 * S + 96].bitcast(U32)
            pos = top[:, 5 * S + 96:5 * S + 112].bitcast(U32)
            pa, pb = (top[:, 5 * S + k:5 * S + k + 16].bitcast(U32) for k in (112, 128))
            paf, pbf = top[:, 5 * S + 144:5 * S + 160], top[:, 5 * S + 160:5 * S + 176]
            best = top[:, 5 * S + 176:5 * S + 192]
            res_at = A_Z - 3 * KB
            mat = lambda x: x.rearrange("p (k a) -> p k a", k=16)
            rows = lambda x: x.unsqueeze(2).broadcast_to([P, 16, 16])
            cols = lambda x: x.unsqueeze(1).broadcast_to([P, 16, 16])
            FLOOR = -3.0e38

            def dots(T0):
                def evict(T):
                    v.wait_ge(piece_used, T.times(2, 2 * (T_U + T0) + 2))
                    v.tensor_tensor(arena[:, ds(T.times(S, T0 * S), S)], bank[T.c % 2][:, 0:S], r2, ALU.mult)\
                     .then_inc(tile_evicted, 1)
                    v.wait_ge(tile_evicted, T.times(1, T_U + T0 + 1))
                    v.nop().then_inc(ev("dots_scaled"), 1)
                return evict

            def top_parts(i):
                def keys():
                    st.apart(v.tensor_copy(sc, arena[:, ds(A_Z + i * S, S)]))
                    for c in range(2):
                        x, y = sc[:, c * P:(c + 1) * P], sc2[:, c * P:(c + 1) * P]
                        a0, a1 = sv[:, c * 16:c * 16 + 8], sv[:, c * 16 + 8:c * 16 + 16]
                        st.apart(v.max(a0, x))
                        st.mark(v.max_index(si[:, c * 16:c * 16 + 8], a0, x))
                        st.apart(v.match_replace(y, a0, x, FLOOR))
                        st.apart(v.max(a1, y))
                        st.mark(v.max_index(si[:, c * 16 + 8:c * 16 + 16], a1, y))
                    st.wait()
                    st.mark(v.tensor_copy(sif, si))

                def pairs():
                    st.apart(v.tensor_tensor(mat(cand), rows(sv[:, 0:16]), cols(sv[:, 16:32]), ALU.add))
                    st.apart(v.max(best[:, 0:8], cand))
                    st.mark(v.max_index(pos[:, 0:8], best[:, 0:8], cand))
                    st.apart(v.match_replace(cand2, best[:, 0:8], cand, FLOOR))
                    st.apart(v.max(best[:, 8:16], cand2))
                    st(v.max_index(pos[:, 8:16], best[:, 8:16], cand2))
                    st.mark(v.tensor_copy(arena[:, ds(res_at + 2 * S + i * 16, 16)], best))
                    st.mark(v.tensor_scalar(pa, pos, 4, None, ALU.logical_shift_right))
                    st(v.tensor_scalar(pb, pos, 15, None, ALU.bitwise_and))
                    st.mark(v.tensor_copy(paf, pa))
                    st(v.tensor_copy(pbf, pb))

                def index(n, place):
                    st(v.tensor_tensor(mat(eq), rows(place), cols(iota[:, 0:16]), ALU.is_equal))
                    st(v.tensor_tensor(mat(eq), mat(eq), cols(sif[:, n * 16:(n + 1) * 16]), ALU.mult))
                    st(v.tensor_reduce(arena[:, ds(res_at + n * S + i * 16, 16)], mat(eq), AX.X, ALU.add))

                return (keys, pairs, lambda: index(0, paf), lambda: index(1, pbf))

            scale1 = dots(0)

            def top_turn(i, first):
                parts = top_parts(i)
                for m in range(4):
                    pair(Tile(i, 4, T_U + m))
                    if not (first and m == 0):
                        scale1(Tile(i, 4, m - 1))
                    parts[m]()

            top_turn(0, True)
            st.turns(1, U1_T // 4, 12 + 11 + 6, lambda i: top_turn(i, False))
            scale1(Tile(0, 4, U1_T - 1))
            g3 = ar(res_at + 2 * S, S).rearrange("p (h k) -> p h k", k=16)
            mx = small[:, 352:368]
            st(v.tensor_copy(mx.unsqueeze(2), g3[:, :, 0:1]))
            v.tensor_tensor(g3, g3, mx.unsqueeze(2).broadcast_to([P, 16, 16]), ALU.subtract).then_inc(ev("gate_in"), 1)
            v.wait_ge(ev("gate_exp"), 1)
            st(v.tensor_reduce(mx, g3, AX.X, ALU.add))
            st(v.reciprocal(mx, mx))
            v.tensor_tensor(g3, g3, mx.unsqueeze(2).broadcast_to([P, 16, 16]), ALU.mult).then_inc(ev("gate_done"), 1)
            for n in range(3):
                v.wait_ge(ev("i_turned"), n + 1)
                v.tensor_copy(slot_major(n), bank[2 + n][:, 0:S]).then_inc(ev("i_kept"), 1)
            stage(T_U2, NKEY - U1_T, dots(U1_T))
            if stop < 6:
                return

            v.wait_ge(ev("g_done"), NKEY)
            v.wait_ge(piece_used, 2 * T_V)
            a_tj = ar(0, NKEY * S).rearrange("p (j t) -> p t j", t=S)
            tok = lambda x: x.rearrange("p (t j) -> p t j", t=4)

            def w_turn(i, first):
                for b in range(2):
                    out = tok(onehot[:, (8 + 4 * b) * P:(12 + 4 * b) * P])
                    if not first:
                        v.wait_ge(ev("w_sum"), i * 2 + (b - 1))
                    st(v.tensor_tensor(out, iota.unsqueeze(1).broadcast_to([P, 4, P]), gate_cols(1, i, b),
                                       ALU.is_equal))
                    v.tensor_tensor(out, out, gate_cols(2, i, b), ALU.mult).then_inc(ev("gj"), 1)
                for b in range(2):
                    v.wait_ge(ev("w_sum"), i * 2 + (b + 1))
                    av = a_tj[:, ds(i * 8 + 4 * b, 4), :]
                    v.tensor_tensor(av, av, tok(bank[2 + b][:, :]), ALU.mult).then_inc(ev("w_used"), 1)

            w_turn(0, True)
            st.turns(1, S // 8, 2, lambda i: w_turn(i, False))
            if stop < 7:
                return
            v.wait_ge(ev("w_sum"), S // 4)
            v.memset(onehot[:, 0:512], 0.0).then_inc(ev("v_zero"), 1)

            def v_pieces(i, first):
                for m in range(4):
                    v.wait_ge(hi_ready, i * 4 + (P_V + m + 1))
                    v.wait_ge(piece_used, i * 4 + (P_V + m - 1))
                    v.tensor_tensor(piece_ap(w_lo, m % 2), piece_ap(raw, m), piece_ap(w_hi, m).bitcast(F32),
                                    ALU.subtract).then_inc(lo_ready, 1)
                    v.wait_ge(ev("av_hi_r"), i * 4 + (m + 1))
                    j = arena[:, ds((i if first else i - 32) * 4 * S + m * S, S)]
                    v.tensor_tensor(av_lo[:, m * S:(m + 1) * S], j, av_hi[:, m * S:(m + 1) * S].bitcast(F32),
                                    ALU.subtract).then_inc(ev("av_lo_r"), 1)

            def keep_sweep(s):
                v.wait_ge(ev("sweep"), s + 1)
                for b in range(4):
                    x = x3[:, (s * 8 + 2 * b) * S:(s * 8 + 2 * b + 2) * S]
                    st.mark(v.tensor_tensor(x, x, bank[4 + b][:, :], ALU.add))
                st.wait()
                v.nop().then_inc(ev("sweep_used"), 1)

            with v.Fori(0, 32) as i:
                v_pieces(i, True)
            v.wait_ge(ev("back_in"), 16)
            keep_sweep(0)
            with v.Fori(32, 64) as i:
                v_pieces(i, False)
            keep_sweep(1)
            v.wait_ge(ev("fsum"), 1)
            r3 = ar(A_XBC + 2 * S, S)
            rstd(bank[2][:, 0:S], D, ar(A_XBC, S), ar(A_XBC + S, S), ar(A_XBC + 3 * S, S), r3,
                 ev("fvar"), ev("froot"))
            for k in range(KT):
                x = x3[:, k * S:(k + 1) * S]
                st.mark(v.scalar_tensor_tensor(x, x, par[:, V_ON + k:V_ON + k + 1], r3, ALU.mult, ALU.mult))
            st.wait()
            v.nop().then_inc(ev("out_ready"), 1)

        @block.gpsimd
        def _(pool):
            st = Steps(pool, p_step)
            pool.dma_start(const, a["const"]).then_inc(par_in, 16)
            pool.dma_start(par, a["par"]).then_inc(par_in, 16)
            pool.dma_start(ar(phase_at, C_PHASE), a["phase"]).then_inc(phase_in, 16)
            pool.dma_start(ar(A_XBC, 2 * CB * P + 2 * P), a["cmp_w"]).then_inc(w1_in, 16)
            pool.wait_ge(par_in, 32)
            if stop < 2:
                pool.wait_ge(phase_in, 16)
                pool.wait_ge(w1_in, 16)
                return

            pool.wait_ge(ev("v_kept"), 4)
            pool.wait_ge(ev("cmp_kept"), 2)

            def stage_v(i, first):
                if not first:
                    pool.wait_ge(ev("pv"), i * 4)
                vs = ar(A_MG + 23 * KB, 4 * P)
                pool.tensor_copy(vs.rearrange("p (n d) -> p n d", n=4),
                                 ar(A_VTOK, 4 * 512).rearrange("p (n g d) -> p n g d", n=4, g=GROUPS)
                                 [:, :, ds(i, 1), :].rearrange("p n g d -> p n (g d)"))\
                    .then_inc(p_step, 1)
                pool.wait_ge(p_step, i + 1)
                pool.tensor_copy(ar(A_MG + 25 * KB, P)[0:NC, :], arena[0:NC, ds(A_K + 12 * KB + i * P, P)]).then_inc(ev("v_staged"), 1)

            stage_v(0, True)
            with pool.Fori(1, GROUPS) as i:
                stage_v(i, False)
            if stop < 3:
                return
            pool.wait_ge(ev("silu_done"), XBC_T)
            pool.wait_ge(ev("pv"), HEADS)

            def stage_x(i, first):
                if not first:
                    pool.wait_ge(ev("g_ready"), i)
                pool.tensor_copy(ar(A_K, 4 * S), arena[:, ds(A_XBC + i * 4 * S, 4 * S)]).then_inc(p_step, 1)
                pool.tensor_copy(ar(A_K + 4 * KB, S), arena[:, ds(A_XBC + 16 * S + i * S, S)]).then_inc(p_step, 1)
                pool.tensor_copy(ar(A_K + 5 * KB, S), arena[:, ds(A_XBC + 20 * S + i * S, S)]).then_inc(p_step, 1)
                pool.wait_ge(p_step, i * 3 + (GROUPS + 3))
                pool.nop().then_inc(ev("x_staged"), 1)

            stage_x(0, True)
            with pool.Fori(1, SG) as i:
                stage_x(i, False)
            if stop < 4:
                return
            pool.wait_ge(ev("gvar"), 1)
            pool.dma_start(ar(A_XBC, KT * S).rearrange("p (k t) -> p k t", k=KT), a["x"].rearrange("k p t -> p k t"))\
                .then_inc(ev("res_in"), 16)
            acc, sq = ar(A_XBC + 16 * KB, S), ar(A_XBC + 20 * KB, S)
            pool.memset(acc, 0.0).then_inc(p_step, 1)
            n0 = GROUPS + 3 * SG + 1
            with pool.Fori(0, KT) as i:
                pool.wait_ge(ev("x2_ready"), i + 1)
                x2 = arena[:, ds(A_Z + i * S, S)]
                pool.wait_ge(p_step, i * 2 + n0)
                pool.tensor_tensor(sq, x2, x2, ALU.mult).then_inc(p_step, 1)
                pool.wait_ge(p_step, i * 2 + (n0 + 1))
                pool.tensor_tensor(acc, acc, sq, ALU.add).then_inc(p_step, 1)
                pool.wait_ge(p_step, i * 2 + (n0 + 2))
                pool.nop().then_inc(ev("sumsq"), 1)
            pool.dma_start(a["spill"], ar(A_Z, KT * S)).then_inc(ev("spilled"), 16)
            pool.wait_ge(ev("x2g_lo"), KT)
            pool.dma_start(ar(A_MG, 8 * KB), a["subk"]).then_inc(ev("subk_in"), 16)
            pool.wait_ge(ev("spilled"), 16)
            if stop < 6:
                pool.wait_ge(ev("subk_in"), 16)
                return

            pool.wait_ge(ev("i_kept"), 3)
            pool.wait_ge(piece_used, 2 * T_V)

            def w_turn(i, first):
                for b in range(2):
                    if not first:
                        pool.wait_ge(ev("w_sum"), i * 2 + (b - 1))
                    rows = small[:, 784 + 4 * b:788 + 4 * b]
                    pool.tensor_copy(rows, small[:, ds(i * 8 + 4 * b, 4)]).then_inc(ev("rows_ready"), 1)
                    pool.wait_ge(ev("rows_ready"), i * 2 + (b + 1))
                    pool.nop(nofuse=True)
                    for t in range(4):
                        pool.tensor_scalar(onehot[:, (4 * b + t) * P:(4 * b + t + 1) * P], iota, rows[:, t:t + 1],
                                           None, ALU.is_equal).then_inc(ev("ohi"), 1)

            w_turn(0, True)
            with pool.Fori(1, S // 8) as i:
                w_turn(i, False)
            if stop < 7:
                return
            pool.wait_ge(piece_used, 2 * T_V)
            pool.dma_start(x3[:, :], a["spill"]).then_inc(ev("back_in"), 16)


def col_tiles(w):
    n = w.shape[1] // P
    return w.reshape(2, HKT, P, n, P).transpose(3, 0, 2, 1, 4).reshape(2 * n, P, PIECE)


def padded(w):
    return np.concatenate([w, np.zeros((w.shape[0], P - w.shape[1]), w.dtype)], axis=1)


def columns(x):
    return x.reshape(-1, P).T


def lay_out(x, attn_norm, w_in, gate_bias, nsa_cmp_pos, nsa_cmp_w1, nsa_cmp_b1, nsa_cmp_w2, ssm_conv_w, ssm_conv_b,
            ssm_dt_bias, ssm_a_log, ssm_d, ssm_norm, w_branch_nsa, w_branch_ssm, w_out, ffn_norm, peer_w_q,
            peer_sub_keys, peer_u, peer_v, final_norm):
    w = w_in[0]
    at = np.cumsum([0, HEADS * HD, 6 * GROUPS * HD, 3 * HEADS, D, XBC_T * P, SH, 2 * D])
    q, kv, gate, z, xbc, dt, merge = (w[:, at[n]:at[n + 1]] for n in range(7))
    branch = lambda b, c: kv[:, (b * 2 + c) * GROUPS * HD:(b * 2 + c + 1) * GROUPS * HD]
    w_in_t = np.concatenate([q, branch(1, 1), branch(2, 1), padded(gate), padded(dt),
                             branch(1, 0), branch(2, 0), branch(0, 0), branch(0, 1), xbc, z, merge], axis=1)
    keep, phase = shape_constants()
    u = peer_u[0].reshape(NKEY, NKEY, 2, HKT, P)
    v = peer_v[0].reshape(NKEY, NKEY, 2, PIECE)
    cw = ssm_conv_w[0].reshape(CONV, XBC_T, P)
    par = np.concatenate([
        columns(attn_norm[0]), columns(ssm_norm[0]), columns(gate_bias[0]),
        cw.transpose(2, 1, 0).reshape(P, XBC_T * CONV), columns(ffn_norm[0]), columns(final_norm),
        columns(ssm_conv_b[0]), nsa_cmp_b1[0].T, columns(np.repeat(ssm_d[0], SP_)),
        nsa_cmp_pos[0].transpose(2, 0, 1).reshape(P, 2 * CB),
        np.tile(ssm_dt_bias[0], (P, 1)), np.tile(ssm_a_log[0], (P, 1))], axis=1)
    assert par.shape[1] == V_END
    cmp_w = np.concatenate([nsa_cmp_w1[0].reshape(2, CB, P, P).transpose(2, 0, 1, 3).reshape(P, 2 * CB * P),
                            nsa_cmp_w2[0].transpose(1, 0, 2).reshape(P, 2 * P)], axis=1)
    return {
        "x": x[0].T.reshape(KT, P, S),
        "w_in": col_tiles(w_in_t),
        "w_mix": np.concatenate([col_tiles(m[0]) for m in (w_branch_nsa, w_branch_ssm, w_out, peer_w_q)]),
        "u": u.transpose(1, 2, 4, 3, 0).reshape(2 * NKEY, P, PIECE),
        "v": v.transpose(2, 1, 0, 3).reshape(2 * NKEY, P, PIECE),
        "subk": peer_sub_keys[0].transpose(3, 0, 1, 2).reshape(P, 2 * PH * NKEY),
        "cmp_w": cmp_w, "par": par, "const": keep, "phase": phase,
    }


def kernel(**inputs):
    import concourse.bacc as bacc
    from concourse.bass_utils import run_bass_kernel_spmd

    nc = bacc.Bacc("TRN2", target_bir_lowering=False, num_devices=1)
    arrays = {n: np.ascontiguousarray(x) for n, x in lay_out(**{n: np.asarray(x) for n, x in inputs.items()}).items()}
    a = {n: nc.dram_tensor(n, x.shape, F32, kind="ExternalInput").ap() for n, x in arrays.items()}
    a["out"] = nc.dram_tensor("out", (KT, P, S), F32, kind="ExternalOutput").ap()
    a["spill"] = nc.dram_tensor("spill", (P, KT * S), F32, kind="Internal").ap()
    build(nc, a)
    r = run_bass_kernel_spmd(nc, [arrays], core_ids=[0])
    return np.ascontiguousarray(r.results[0]["out"].reshape(D, S).T)[None]
```

```python
from contextlib import ExitStack

import numpy as np

import concourse.bass as bass
from concourse import mybir
from concourse.alu_op_type import AluOpType as ALU

ACT = mybir.ActivationFunctionType
AX = mybir.AxisListType
F32 = mybir.dt.float32
F32R = mybir.dt.float32r
U32 = mybir.dt.uint32
BF16 = mybir.dt.bfloat16
ds = bass.ds

P = 128
D = 2048
KT = D // P
S = 256
TT = S // P
EPS = 1e-6
NEG = -1e30
PIECE = 1024
HKT = KT // 2

HEADS, GROUPS, RPG, HD = 16, 4, 4, 128
SCALE = HD ** -0.5
CB, CS = 32, 16
NC = S // CS - CB // CS + 1
ROPE = HD // 4
THETA = 500000.0

SH, SG, SHG, SP_, SN, CHUNK = 32, 4, 8, 64, 128, 128
CONV = 4
XT_T, XBC_T, Z_T, MG_T = 16, 24, 16, 32

PH, TOPK, NKEY = 8, 16, 128

QKV_A = HEADS + 2 * GROUPS + 2
QKV_B = 4 * GROUPS
ATT_T = XBC_T + Z_T + 8
SSD_T = MG_T - 8
T_A, T_B = 0, QKV_A
T_ATT = T_B + QKV_B
T_SSD = T_ATT + ATT_T
T_BN = T_SSD + SSD_T
T_BS, T_WO, T_WQ = T_BN + KT, T_BN + 2 * KT, T_BN + 3 * KT
T_U = T_BN + 4 * KT
U1_T = 64
T_U2 = T_U + U1_T
WT = 8
JH = NKEY // 2
W_STEPS = S // WT
W_TILES, W_TURN = 14, 8
W_AT = [n * 2 * W_TILES // W_TURN for n in range(W_TURN)]
U3_T = NKEY - U1_T - W_TILES * W_STEPS // W_TURN
T_U3 = T_U + NKEY - U3_T
SWEEP = NKEY // 2 // 8
T_V = T_U + NKEY
P_V = 2 * T_V

KB = 256
A_Q, A_VT, A_GD, A_K, A_VTOK, A_XBC, A_Z, A_MG = (k * KB for k in (0, 16, 24, 32, 48, 56, 80, 96))
A_END = 128 * KB

C_ONES, C_IOTA, C_IDENT, C_TRI = 0, P, 2 * P, 3 * P
C_KEEP = 4 * P
C_ROT, C_COS, C_SIN, C_MASK, C_CB, C_C01 = 0, P, P + S, P + 2 * S, P + 3 * S, P + 3 * S + 2 * NC
C_PHASE = P + 3 * S + 4 * NC

V_ON, V_AN, V_SN, V_GB, V_CW, V_FN, V_CB, V_B1, V_DS, V_POS, V_DTB, V_AL = (
    0, 16, 32, 48, 80, 176, 192, 216, 218, 234, 298, 330)
V_END = 362


def shape_constants():
    keep = np.zeros((P, C_KEEP), np.float32)
    r = np.arange(P)
    keep[:, C_IDENT:C_IDENT + P] = np.eye(P)
    keep[:, C_IOTA:C_IOTA + P] = r[None, :]
    keep[:, C_ONES:C_ONES + P] = 1
    keep[:, C_TRI:C_TRI + P] = r[:, None] <= r[None, :]
    phase = np.zeros((P, C_PHASE), np.float32)
    half = ROPE // 2
    for d in range(half):
        phase[d + half, C_ROT + d] = -1
        phase[d, C_ROT + d + half] = 1
    inv = np.float32(THETA) ** (-np.arange(half, dtype=np.float32) / np.float32(half))
    ang = np.arange(S, dtype=np.float32)[None, :] * inv.astype(np.float32)[:, None]
    phase[:, C_COS:C_COS + S] = 1
    phase[0:half, C_COS:C_COS + S] = phase[half:ROPE, C_COS:C_COS + S] = np.cos(ang)
    phase[0:half, C_SIN:C_SIN + S] = phase[half:ROPE, C_SIN:C_SIN + S] = np.sin(ang)
    phase[:, C_MASK + P:C_MASK + S] = np.where(r[None, :] <= r[:, None], 0, NEG)
    for tt in range(TT):
        ok = np.arange(NC)[None, :] * CS + CB - 1 <= (r + tt * P)[:, None]
        phase[:, C_CB + tt * NC:C_CB + (tt + 1) * NC] = np.where(ok, 0, NEG)
        phase[:, C_C01 + tt * NC:C_C01 + (tt + 1) * NC] = ok
    return keep, phase


class Tile:

    def __init__(self, i, k, c):
        self.i, self.k, self.c = i, k, c

    def times(self, m, a=0):
        return self.i * (self.k * m) + (self.c * m + a)

    def half(self, a=0):
        return self.i * (self.k // 2) + (self.c // 2 + a)

    def __add__(self, n):
        return Tile(self.i, self.k, self.c + n)


def wait(eng, sem, value):
    if not isinstance(value, int) or value > 0:
        eng.wait_ge(sem, value)


class Steps:

    def __init__(self, eng, sem):
        self.eng, self.sem, self.base, self.n, self.at = eng, sem, 0, 0, 0

    def mark(self, ins):
        self.n += 1
        ins.then_inc(self.sem, 1)

    def wait(self):
        self.eng.wait_ge(self.sem, self.base + self.n)

    def __call__(self, ins):
        self.mark(ins)
        self.wait()

    def apart(self, ins):
        self(ins)
        self.eng.nop(nofuse=True)

    def turns(self, first, end, per, body):
        start = self.n
        with self.eng.Fori(first, end) as i:
            self.base, self.n = i * per + (start - first * per), 0
            body(i)
            assert self.n == per, (self.n, per)
        self.base, self.n = 0, start + (end - first) * per


def build(nc, a, stop=99):
    with ExitStack() as ctx:
        def sb(name, shape, dt=F32, stack=ctx):
            return stack.enter_context(nc.sbuf_tensor(name, shape, dt))

        def sem(name):
            return ctx.enter_context(nc.semaphore(name))

        with ExitStack() as early:
            act1_hi = sb("act1_hi", [P, KT * S], F32R, early)
            act1_lo = sb("act1_lo", [P, KT * S], F32R, early)
        arena = sb("arena", [P, A_END])
        with ExitStack() as early:
            act0_hi = sb("act0_hi", [P, KT * S], F32R, early)
            act0_lo = sb("act0_lo", [P, KT * S], F32R, early)
        onehot_late = sb("onehot_late", [P, 16 * KB], BF16)
        av_hi = sb("av_hi", [P, 4 * S], F32R)
        av_lo = sb("av_lo", [P, 4 * S], F32R)
        x3 = sb("x3", [P, KT * S])
        raw = sb("raw", [P, 4 * PIECE])
        w_hi = sb("w_hi", [P, 4 * PIECE], F32R)
        w_lo = sb("w_lo", [P, 2 * PIECE], F32R)
        kept = sb("kept", [P, C_KEEP + V_END])
        const, par = kept[:, 0:C_KEEP], kept[:, C_KEEP:C_KEEP + V_END]
        r2 = par[:, V_AN:V_AN + S]
        zeros = par[:, V_AN + S:V_AN + S + P // 2].bitcast(BF16)
        gate_rest = kept[:, C_IDENT:C_IDENT + S]
        small = sb("small", [P, 872])

        bank = [ctx.enter_context(nc.psum_tensor(f"bank{i}", [P, 512], F32)) for i in range(8)]

        def ar(at, n):
            return arena[:, at:at + n]

        onehot_early = arena[:, A_END - 8 * KB:A_END].bitcast(BF16)
        rows_i = small[:, 0:S]
        cols_j, iota_j = small[:, S:S + P].bitcast(BF16), small[:, S + P:S + P + JH].bitcast(BF16)
        gate_part = [small[:, 448 + k * P:448 + (k + 1) * P].bitcast(BF16) for k in range(3)]
        row_now = small[:, 840:840 + WT]

        def oh_rows(store):
            return store[:, 0:WT * P]

        def oh_cols(store, part):
            return store[:, WT * P + part * WT * JH:WT * P + (part + 1) * WT * JH]

        def over_j(x, step):
            return x[:, ds(step.times(WT), WT)].unsqueeze(2).broadcast_to([P, WT, JH])

        ident, iota, ones, tri = (const[:, k:k + P] for k in (C_IDENT, C_IOTA, C_ONES, C_TRI))
        phase_at = A_MG + 28 * KB
        rot = ar(phase_at + C_ROT, P)
        cos_t, sin_t = ar(phase_at + C_COS, S), ar(phase_at + C_SIN, S)
        mask_t = ar(phase_at + C_MASK, S)
        cmp_bias = ar(phase_at + C_CB, 2 * NC)
        cmp_01 = ar(phase_at + C_C01, 2 * NC)

        raw_landed = [sem(f"raw_landed{k}") for k in range(4)]
        hi_ready, lo_ready = sem("hi_ready"), sem("lo_ready")
        piece_used, tile_evicted = sem("piece_used"), sem("tile_evicted")
        v_step, a_step, p_step = sem("v_step"), sem("a_step"), sem("p_step")
        par_in, x_in, w1_in, phase_in = sem("par_in"), sem("x_in"), sem("w1_in"), sem("phase_in")
        E = {}

        def ev(name):
            if name not in E:
                E[name] = sem(name)
            return E[name]

        for name in ("sq_ready", "sum_ready", "var_ready", "root_ready", "h_ready", "h_hi", "h_split",
                     "krot", "krot_used", "krope", "v_turned", "v_kept", "g_turned", "g_kept", "hid_sum", "hid_used",
                     "hid_ready", "cmp_out", "cmp_kept",
                     "q_rot", "q_roped", "scores", "scored", "exps", "probs", "p_turned", "p_kept_a",
                     "p_kept_b", "pv", "o_hi", "o_lo", "v_staged",
                     "conv_done", "silu_done", "z_done", "dt_in", "dt_exp", "dta_ready", "acs_sum", "acs_kept",
                     "dte_in", "dte_ready", "dtdte_ready",
                     "x_staged", "x_turned", "b_turned", "b_kept", "xdt_ready", "cbm_ready", "dtatri", "acsb",
                     "seg_ready", "seg_exp", "m_ready", "c_exp", "c_ready", "state", "state_kept", "y_sum",
                     "y_used", "g_ready", "gsq_ready", "gsum", "gsum_kept",
                     "gvar", "groot", "gn_ready", "gn_hi", "g_split",
                     "gate_ready", "merged", "merged_hi", "merged_lo", "res_in", "x2_ready", "x2g_hi", "x2g_lo",
                     "sumsq", "x2sum", "x2var", "x2root", "rstd2", "spilled", "subk_in", "s_sum", "s_kept",
                     "top_done", "gate_in", "gate_exp", "gate_done", "i_turned", "i_kept",
                     "g_done", "rows_ready", "ohi", "gj", "w_sum", "w_used", "v_zero", "av_hi_r", "av_lo_r", "back_in",
                     "sweep", "sweep_used", "last_kept", "fsq", "fsum", "fvar", "froot", "out_ready", "stored"):
            ev(name)

        def expert_col(s, i, m):
            return arena[:, ds(i * 8 * S + (m - 8 * SWEEP * (s - s // 2)) * S, S)]

        block = ctx.enter_context(nc.Block())

        def piece_ap(ring, slot):
            return ring[:, slot * PIECE:(slot + 1) * PIECE]

        @block.sync
        def _(sp):
            def load(src, n_before, q, i, k, m):
                slot = m % 4
                wait(sp, lo_ready, i * k + (n_before + m - 3))
                sp.dma_start(piece_ap(raw, slot), src[ds(i * k + m, 1)].rearrange("a p n -> (a p) n"))\
                  .then_inc(raw_landed[slot], 16)

            before = 0
            for name, n in (("w_in", 2 * T_BN), ("w_mix", 8 * KT), ("u", 2 * NKEY), ("v", 2 * NKEY)):
                first = 0
                if before == 0:
                    for m in range(4):
                        load(a[name], 0, None, 0, 4, m)
                    first = 1
                with sp.Fori(first, n // 4) as i:
                    for m in range(4):
                        load(a[name], before, None, i, 4, m)
                before += n
                if (name == "w_in" and stop < 4) or (name == "w_mix" and stop < 5) or (name == "u" and stop < 7):
                    break
            if stop >= 7:
                for c in range(4):
                    sp.wait_ge(ev("out_ready"), 4 * c + 4)
                    sp.dma_start(a["out"][4 * c:4 * c + 4].rearrange("k p t -> p k t"),
                                 x3[:, c * PIECE:(c + 1) * PIECE].rearrange("p (k t) -> p k t", k=4))\
                      .then_inc(ev("stored"), 16)
                sp.wait_ge(ev("stored"), 64)

        @block.tensor
        def _(pe):
            def half_tile(T, h, out, hi_rhs, lo_rhs):
                slot = (T.c % 2) * 2 + h
                hi, lo = piece_ap(w_hi, slot), piece_ap(w_lo, slot % 2)
                pe.wait_ge(hi_ready, T.times(2, h + 1))
                for n, (w, x) in enumerate(((hi, hi_rhs), (hi, lo_rhs), (lo, hi_rhs))):
                    if n == 2:
                        pe.wait_ge(lo_ready, T.times(2, h + 1))
                    for k in range(HKT):
                        kt = h * HKT + k
                        mm = pe.matmul(out, w[:, k * P:(k + 1) * P], x[:, kt * S:(kt + 1) * S],
                                       start=(h == 0 and n == 0 and k == 0), stop=(h == 1 and n == 2 and k == HKT - 1))
                mm.then_inc(piece_used, 1)

            def tile(T, hi_rhs, lo_rhs):
                wait(pe, tile_evicted, T.times(1, -1))
                for h in range(2):
                    half_tile(T, h, bank[T.c % 2][:, 0:S], hi_rhs, lo_rhs)

            def stage(T0, n, hi_rhs, lo_rhs, first=0):
                with pe.Fori(first, n // 2) as i:
                    for m in range(2):
                        tile(Tile(i, 2, T0 + m), hi_rhs, lo_rhs)

            pe.wait_ge(par_in, 32)
            pe.wait_ge(ev("sq_ready"), 1)
            pe.matmul(bank[2][:, 0:S], ones, ar(A_VTOK, S), start=True, stop=True).then_inc(ev("sum_ready"), 1)
            pe.wait_ge(ev("h_split"), 4)
            for m in range(2):
                tile(Tile(0, 2, T_A + m), act0_hi, act0_lo)
            stage(T_A, QKV_A, act0_hi, act0_lo, first=1)
            stage(T_B, QKV_B, act0_hi, act0_lo)

            pe.wait_ge(tile_evicted, T_ATT)
            pe.wait_ge(phase_in, 16)
            pe.wait_ge(w1_in, 16)
            for n in range(6):
                if n >= 4:
                    pe.wait_ge(ev("krope"), n - 3)
                pe.matmul(bank[2 + n % 4][:, :], rot, ar(A_K + n * 512, 512), start=True, stop=True)\
                  .then_inc(ev("krot"), 1)
            pe.wait_ge(ev("krope"), 6)
            for n in range(4):
                for g in range(GROUPS):
                    b, tt = n // 2, n % 2
                    mm = pe.transpose(bank[2 + n][:, g * P:(g + 1) * P],
                                      ar(A_VT + (b * GROUPS + g) * S + tt * P, P), ident)
                mm.then_inc(ev("v_turned"), 1)
            for n in range(4):
                src = ar(A_GD + (n // 2) * S + (n % 2) * P, P)
                mm = pe.transpose(bank[6][:, n * P:(n + 1) * P], src, ident)
            mm.then_inc(ev("g_turned"), 1)
            for c in range(2):
                src = ar(A_K + (8 + 4 * c) * S, 4 * S).rearrange("p (g t) -> p g t", g=GROUPS)
                w1 = ar(A_XBC + c * CB * P, CB * P)
                if c == 1:
                    pe.wait_ge(ev("hid_used"), 1)
                for l in range(CB):
                    pe.matmul(bank[0][:, 0:GROUPS * NC], w1[:, l * P:(l + 1) * P],
                              src[:, :, l:l + CS * (NC - 1) + 1:CS], start=(l == 0), stop=(l == CB - 1))
                for l in range(CB):
                    mm = pe.matmul(bank[1][:, 0:1], w1[:, l * P:(l + 1) * P],
                                   par[:, V_POS + c * CB + l:V_POS + c * CB + l + 1],
                                   start=(l == 0), stop=(l == CB - 1))
                mm.then_inc(ev("hid_sum"), 1)
            pe.wait_ge(ev("hid_ready"), 2)
            pe.wait_ge(ev("g_kept"), 3)
            w2 = ar(A_XBC + 2 * CB * P, 2 * P)
            hid = [ar(A_MG + 26 * KB + c * 64, GROUPS * NC) for c in range(2)]
            pe.matmul(bank[7][:, 0:GROUPS * NC], w2[:, 0:P], hid[0], start=True, stop=True)
            for g in range(GROUPS):
                mm = pe.matmul(bank[6][0:NC, g * P:(g + 1) * P], hid[1][:, g * NC:(g + 1) * NC], w2[:, P:2 * P],
                               start=True, stop=True)
            mm.then_inc(ev("cmp_out"), 1)
            pe.wait_ge(ev("dta_ready"), 1)
            pe.wait_ge(ev("v_kept"), 4)
            dta = small[:, 96 + 64:96 + 128]
            pe.matmul(bank[2][:, 0:64], tri, dta, start=True, stop=True)
            pe.matmul(bank[2][:, 64:96], ones, dta[:, 0:32], start=True, stop=True).then_inc(ev("acs_sum"), 1)
            if stop < 2:
                return

            pe.wait_ge(ev("cmp_kept"), 2)
            pe.wait_ge(ev("dte_in"), 1)
            starts = (0, 2, 5, 7)

            def attention_turn(i, first):
                def n_of(hh):
                    return i * 4 + hh

                def q_rot(hh):
                    if not (first and hh == 0):
                        pe.wait_ge(ev("scored"), n_of(hh))
                    pe.matmul(bank[2][:, 0:S], rot, arena[:, ds(i * 4 * S + hh * S, S)], start=True, stop=True)\
                      .then_inc(ev("q_rot"), 1)

                def scores(hh):
                    pe.wait_ge(ev("q_roped"), n_of(hh) + 1)
                    q = ar(A_MG + 20 * KB + (hh % 2) * S, S)
                    for tt in range(TT):
                        w = P * (tt + 1)
                        for b in range(2):
                            pe.matmul(bank[3 + tt][:, b * w:(b + 1) * w], q[:, tt * P:(tt + 1) * P],
                                      arena[:, ds(A_K + b * 4 * S + i * S, w)], start=True, stop=True)
                    for tt in range(TT):
                        mm = pe.matmul(bank[2][:, tt * NC:(tt + 1) * NC], q[:, tt * P:(tt + 1) * P],
                                       kc_group(i), start=True, stop=True)
                    mm.then_inc(ev("scores"), 1)

                def turn_p(hh):
                    pe.wait_ge(ev("probs"), n_of(hh) + 1)
                    if not (first and hh == 0):
                        pe.wait_ge(ev("p_kept_a"), n_of(hh))
                        pe.wait_ge(ev("p_kept_b"), n_of(hh))
                    pr = ar(A_MG + 8 * KB + (hh % 2) * 800, 798)
                    for b in range(2):
                        pe.transpose(bank[5][:, b * S:b * S + P], pr[:, b * P:(b + 1) * P], ident)
                        pe.transpose(bank[5][:, b * S + P:(b + 1) * S], pr[:, S + b * S:S + b * S + P], ident)
                    for b in range(2):
                        pe.transpose(bank[6][:, b * P:(b + 1) * P], pr[:, S + b * S + P:S + (b + 1) * S], ident)
                    for tt in range(TT):
                        mm = pe.transpose(bank[6][0:NC, S + tt * P:S + (tt + 1) * P],
                                          pr[:, 3 * S + tt * NC:3 * S + (tt + 1) * NC], ident)
                    mm.then_inc(ev("p_turned"), 1)

                def pv(hh):
                    pe.wait_ge(ev("p_kept_a"), n_of(hh) + 1)
                    pe.wait_ge(ev("p_kept_b"), n_of(hh) + 1)
                    pe.wait_ge(ev("v_staged"), i + 1)
                    if not (first and hh == 0):
                        pe.wait_ge(ev("o_lo"), n_of(hh))
                    pt = ar(A_MG + 16 * KB, 4 * S)
                    vs, vcs = ar(A_MG + 23 * KB, 4 * P), ar(A_MG + 25 * KB, P)
                    o = bank[7]
                    pe.matmul(o[:, 0:S], vs[:, 0:P], pt[:, 0:S], start=True, stop=False)
                    pe.matmul(o[:, 0:S], vs[:, 2 * P:3 * P], pt[:, S:2 * S], start=False, stop=False)
                    pe.matmul(o[:, 0:S], vcs[0:NC, :], pt[0:NC, 3 * S:4 * S], start=False, stop=False)
                    pe.matmul(o[:, P:S], vs[:, P:2 * P], pt[:, 2 * S:2 * S + P], start=False, stop=False)
                    pe.matmul(o[:, P:S], vs[:, 3 * P:4 * P], pt[:, 2 * S + P:3 * S], start=False, stop=True)\
                      .then_inc(ev("pv"), 1)

                for m in range(12):
                    if m in starts:
                        q_rot(starts.index(m))
                    tile(Tile(i, 12, T_ATT + m), act0_hi, act0_lo)
                    if m in starts:
                        scores(starts.index(m))
                    if m - 2 in starts:
                        turn_p(starts.index(m - 2))
                    if m - 3 in starts:
                        pv(starts.index(m - 3))

            def kc_group(i):
                return arena[:, ds(A_MG + 26 * KB + 128 + i * NC, NC)]

            attention_turn(0, True)
            with pe.Fori(1, GROUPS) as i:
                attention_turn(i, False)
            if stop < 3:
                return

            pe.wait_ge(ev("o_lo"), HEADS)
            pe.wait_ge(ev("dtdte_ready"), 1)

            xs_stage = ar(A_K, 4 * S)
            b_stage, c_stage = ar(A_K + 4 * KB, S), ar(A_K + 5 * KB, S)
            ebuf = [ar(A_K + (6 + 4 * c) * KB, PIECE) for c in range(2)]
            cs_buf = ar(A_K + 14 * KB, PIECE)
            xdt = [ar(A_K + (18 + 2 * c) * KB, 512) for c in range(2)]
            xde = ar(A_K + 22 * KB, 512)
            btok = small[:, 700:828]
            cbm = small[:, 444:700]

            def ssd_turn(i, first):
                T = Tile(i, 6, T_SSD)
                pe.wait_ge(ev("x_staged"), i + 1)
                if not first:
                    pe.wait_ge(ev("g_ready"), i)
                for c in range(2):
                    for t in range(4):
                        mm = pe.transpose(bank[2 + c][:, t * P:(t + 1) * P],
                                          xs_stage[:, t * S + c * P:t * S + (c + 1) * P], ident)
                mm.then_inc(ev("x_turned"), 1)
                pe.transpose(bank[6][:, 0:P], b_stage[:, 0:P], ident)
                for c in range(2):
                    mm = pe.matmul(bank[6][:, (1 + c) * P:(2 + c) * P], b_stage[:, c * P:(c + 1) * P],
                                   c_stage[:, c * P:(c + 1) * P], start=True, stop=True)
                mm.then_inc(ev("b_turned"), 1)
                tile(T, act0_hi, act0_lo)
                for c in range(2):
                    pe.wait_ge(ev("dtatri"), i * 2 + (c + 1))
                    if c == 1:
                        pe.wait_ge(ev("seg_ready"), i * 2 + 1)
                    for n in range(2):
                        mm = pe.matmul(bank[4 + n][:, :], ones, ebuf[c][:, n * 512:(n + 1) * 512],
                                       start=True, stop=True)
                    mm.then_inc(ev("acsb"), 1)
                    tile(T + (1 + c), act0_hi, act0_lo)
                pe.wait_ge(ev("xdt_ready"), i + 1)
                pe.wait_ge(ev("b_kept"), i + 1)
                if not first:
                    pe.wait_ge(ev("gsum_kept"), i)
                pe.matmul(bank[7][:, :], btok, xde, start=True, stop=True).then_inc(ev("state"), 1)
                tile(T + 3, act0_hi, act0_lo)
                pe.wait_ge(ev("m_ready"), i * 2 + 2)
                pe.wait_ge(ev("c_ready"), i + 1)
                pe.wait_ge(ev("state_kept"), i + 1)
                for t in range(4):
                    b, at = bank[2 + t // 2], (t % 2) * S
                    for r in (2 * t, 2 * t + 1):
                        rows = slice((r % 2) * SP_, (r % 2 + 1) * SP_)
                        head = slice(r * SP_, (r + 1) * SP_)
                        pe.matmul(b[rows, at:at + P], xdt[0][:, head], ebuf[0][:, r * P:(r + 1) * P],
                                  start=True, stop=True)
                        pe.matmul(b[rows, at + P:at + S], xdt[1][:, head], ebuf[1][:, r * P:(r + 1) * P],
                                  start=True, stop=False)
                        mm = pe.matmul(b[rows, at + P:at + S], xde[:, head], cs_buf[:, r * P:(r + 1) * P],
                                       start=False, stop=True)
                mm.then_inc(ev("y_sum"), 1)
                tile(T + 4, act0_hi, act0_lo)
                pe.wait_ge(ev("gsq_ready"), i + 1)
                for t in range(4):
                    mm = pe.matmul(bank[7][:, 0:S], ones, cs_buf[:, t * S:(t + 1) * S], start=(t == 0), stop=(t == 3))
                mm.then_inc(ev("gsum"), 1)
                tile(T + 5, act0_hi, act0_lo)

            ssd_turn(0, True)
            with pe.Fori(1, SG) as i:
                ssd_turn(i, False)
            if stop < 4:
                return

            def joined_stage(T0, hi_rhs, lo_rhs, made, n, between=None):
                pe.wait_ge(tile_evicted, T0 - 1)
                for h in range(2):
                    pe.wait_ge(made, n * (h + 1) // 2)
                    half_tile(Tile(0, 2, T0), h, bank[0][:, 0:S], hi_rhs, lo_rhs)
                if between:
                    between()
                tile(Tile(0, 2, T0 + 1), hi_rhs, lo_rhs)
                stage(T0, KT, hi_rhs, lo_rhs, first=1)

            def residual_sum():
                pe.wait_ge(ev("sumsq"), KT)
                pe.matmul(bank[2][:, 0:S], ones, ar(A_XBC + 16 * KB, S), start=True, stop=True)\
                  .then_inc(ev("x2sum"), 1)

            stage(T_BN, KT, act1_hi, act1_lo)
            joined_stage(T_BS, act0_hi, act0_lo, ev("g_split"), 4)
            joined_stage(T_WO, act1_hi, act1_lo, ev("merged_lo"), KT)
            joined_stage(T_WQ, act0_hi, act0_lo, ev("x2g_lo"), KT, residual_sum)
            if stop < 5:
                return

            for m in range(2):
                tile(Tile(0, 2, T_U + m), act0_hi, act0_lo)
            pe.wait_ge(tile_evicted, T_U)
            pe.wait_ge(ev("subk_in"), 16)
            qp, subk = ar(A_MG + 16 * KB, KT * S), ar(A_MG, 8 * KB)
            for n in range(8):
                if n >= 4:
                    pe.wait_ge(ev("s_kept"), n - 3)
                for m in range(4):
                    tt, hc = n // 4, (n % 4) * 4 + m
                    mm = pe.matmul(bank[4 + n % 4][:, m * P:(m + 1) * P], qp[:, hc * S + tt * P:hc * S + (tt + 1) * P],
                                   subk[:, hc * P:(hc + 1) * P], start=True, stop=True)
                mm.then_inc(ev("s_sum"), 1)
            stage(T_U, U1_T, act0_hi, act0_lo, first=1)
            pe.wait_ge(ev("gate_done"), 1)
            res = ar(A_Z - 3 * KB, 3 * S)
            for n in range(3):
                for tt in range(TT):
                    mm = pe.transpose(bank[2 + n][:, tt * P:(tt + 1) * P],
                                      res[:, n * S + tt * P:n * S + (tt + 1) * P], ident)
                mm.then_inc(ev("i_turned"), 1)

            pe.wait_ge(ev("i_kept"), 2)

            def w_step(step, store, first=False):
                n = step.c % 2
                if not first:
                    pe.wait_ge(ev("w_used"), step.times(1, -1))
                pe.wait_ge(ev("ohi"), step.times(WT, WT))
                pe.wait_ge(ev("gj"), step.times(1, 1))
                rows = oh_rows(store)
                for t in range(WT):
                    for part in range(1, 4):
                        mm = pe.matmul(bank[2 + n][:, t * JH:(t + 1) * JH], rows[:, t * P:(t + 1) * P],
                                       oh_cols(store, part)[:, t * JH:(t + 1) * JH], start=part == 1, stop=part == 3)
                mm.then_inc(ev("w_sum"), 1)

            def u2_turn(i, first):
                for m in range(W_TILES):
                    T = Tile(i, W_TILES, T_U2 + m)
                    wait(pe, tile_evicted, T.times(1, -1))
                    for h in range(2):
                        half_tile(T, h, bank[T.c % 2][:, 0:S], act0_hi, act0_lo)
                        if 2 * m + h - 2 in W_AT:
                            n = W_AT.index(2 * m + h - 2)
                            w_step(Tile(i, W_TURN, n), onehot_early, first and n < 2)

            u2_turn(0, True)
            with pe.Fori(1, W_STEPS // W_TURN) as i:
                u2_turn(i, False)
            stage(T_U3, U3_T, act0_hi, act0_lo)
            if stop < 7:
                return

            pe.wait_ge(ev("v_zero"), 1)

            def v_piece(i, m):
                slot = m % 4
                hi, lo = piece_ap(w_hi, slot), piece_ap(w_lo, slot % 2)
                ah, al = av_hi[:, slot * S:(slot + 1) * S], av_lo[:, slot * S:(slot + 1) * S]
                pe.wait_ge(hi_ready, i * 8 + (P_V + m + 1))
                pe.wait_ge(ev("av_hi_r"), i * 8 + (m + 1))
                for n, (w, x) in enumerate(((hi, ah), (hi, al), (lo, ah))):
                    if n == 1:
                        pe.wait_ge(ev("av_lo_r"), i * 8 + (m + 1))
                    if n == 2:
                        pe.wait_ge(lo_ready, i * 8 + (P_V + m + 1))
                    for k in range(HKT):
                        mm = pe.matmul(bank[4 + k // 2][:, (k % 2) * S:(k % 2 + 1) * S], w[:, k * P:(k + 1) * P], x,
                                       start=False, stop=False, skip_group_check=True)
                mm.then_inc(piece_used, 1)

            def rim(start):
                for b in range(4):
                    mm = pe.matmul(bank[4 + b][:, :], zeros, const[:, 0:S].bitcast(BF16), start=start, stop=not start,
                                   skip_group_check=True)
                return mm

            for s in range(4):
                if s > 0:
                    pe.wait_ge(ev("sweep_used"), s)
                rim(True)
                with pe.Fori(s * SWEEP, (s + 1) * SWEEP) as i:
                    for m in range(8):
                        v_piece(i, m)
                        if s < 2 and m % 4 == 2:
                            w_step(Tile(i, 2, W_STEPS + m // 4), onehot_late)
                rim(False).then_inc(ev("sweep"), 1)
            for k in range(KT):
                pe.wait_ge(ev("fsq"), k // 2 + 1)
                mm = pe.matmul(bank[2][:, 0:S], ones, ar(k * S, S), start=(k == 0), stop=(k == KT - 1))
            mm.then_inc(ev("fsum"), 1)

        @block.scalar
        def _(act):
            st = Steps(act, a_step)
            act.dma_start(ar(A_MG, KT * S).rearrange("p (k t) -> p k t", k=KT), a["x"].rearrange("k p t -> p k t"))\
               .then_inc(x_in, 16)

            def hi(T, h):
                slot = (T.c % 2) * 2 + h
                act.wait_ge(raw_landed[slot], T.half(1) * 16)
                wait(act, piece_used, T.times(2, h - 3))
                act.activation(piece_ap(w_hi, slot), piece_ap(raw, slot), ACT.Copy).then_inc(hi_ready, 1)

            def pair(T):
                hi(T, 0)
                hi(T, 1)

            def stage(T0, n, evict, per=2, beside=None, begun=False, goes_on=False):
                def turn(i, first):
                    for m in range(per):
                        if not (first and m == 0 and begun):
                            pair(Tile(i, per, T0 + m))
                        if beside:
                            beside(i, m, first)
                        if not (first and m == 0):
                            evict(Tile(i, per, m - 1))
                turn(0, True)
                with act.Fori(1, n // per) as i:
                    turn(i, False)
                if goes_on:
                    pair(Tile(0, per, T0 + n))
                evict(Tile(0, per, n - 1))

            def nothing(T):
                pass

            def keep_in(at, T0):
                def evict(T):
                    act.wait_ge(piece_used, T.times(2, 2 * T0 + 2))
                    act.activation(arena[:, ds(T.times(S, at), S)], bank[T.c % 2 ^ T0 % 2][:, 0:S], ACT.Copy)\
                       .then_inc(tile_evicted, 1)
                return evict

            act.wait_ge(par_in, 32)
            act.wait_ge(x_in, 16)
            act.activation(ar(0, KT * S), ar(A_MG, KT * S), ACT.Square).then_inc(st.sem, 1)
            st.n += 1
            act.wait_ge(ev("var_ready"), 1)
            act.activation(ar(A_K + S, S), ar(A_K, S), ACT.Sqrt).then_inc(ev("root_ready"), 1)
            for c in range(4):
                act.wait_ge(ev("h_ready"), c + 1)
                act.activation(act0_hi[:, c * PIECE:(c + 1) * PIECE], ar(A_MG + (16 + 4 * (c % 2)) * KB, PIECE), ACT.Copy)\
                   .then_inc(ev("h_hi"), 1)
            act.wait_ge(ev("h_hi"), 4)
            stage(T_A, QKV_A, keep_in(0, T_A))
            stage(T_B, QKV_B, keep_in(A_K, T_B))

            act.wait_ge(ev("g_turned"), 1)
            gsig = small[:, 0:96].rearrange("p (h s) -> p h s", s=6)
            for tt in range(TT):
                src = bank[6][:, tt * P:tt * P + 3 * HEADS].rearrange("p (h b) -> p h b", b=3)
                act.activation(gsig[:, :, 2 * tt:2 * tt + 2], src[:, :, 1:3], ACT.Sigmoid).then_inc(ev("g_kept"), 1)
                ins = act.activation(gsig[:, :, 4 + tt:5 + tt], src[:, :, 0:1], ACT.Sigmoid)
                st.mark(ins)
            st.wait()
            tmp = ar(A_MG + 8 * KB, 64 * 12)
            act.wait_ge(ev("dt_in"), 1)
            act.activation(tmp[:, 64:128], tmp[:, 0:64], ACT.Exp, scale=-1.0).then_inc(ev("dt_exp"), 1)
            act.activation(tmp[:, 128:160], par[:, V_AL:V_AL + 32], ACT.Exp).then_inc(ev("dt_exp"), 1)
            hid = [ar(A_MG + 26 * KB + c * 64, GROUPS * NC) for c in range(2)]
            for c in range(2):
                act.wait_ge(ev("hid_used"), c + 1)
                act.activation(hid[c], ar(A_MG + 27 * KB + c * 64, GROUPS * NC), ACT.Gelu).then_inc(ev("hid_ready"), 1)
            act.wait_ge(ev("cmp_out"), 1)
            act.activation(ar(A_MG + 26 * KB + 128, GROUPS * NC), bank[7][:, 0:GROUPS * NC], ACT.Copy)\
               .then_inc(ev("cmp_kept"), 1)
            act.activation(arena[0:NC, A_K + 12 * KB:A_K + 14 * KB], bank[6][0:NC, :], ACT.Copy)\
               .then_inc(ev("cmp_kept"), 1)
            act.wait_ge(ev("dte_in"), 1)
            act.activation(small[:, 328:360], small[:, 328:360], ACT.Exp).then_inc(ev("dte_ready"), 1)
            if stop < 2:
                return

            starts = (0, 2, 5, 7)
            att_keep = keep_in(A_XBC, T_ATT)

            def attention_turn(i, first):
                def n_of(hh):
                    return i * 4 + hh

                def exps(hh):
                    act.wait_ge(ev("scored"), n_of(hh) + 1)
                    pr = ar(A_MG + 8 * KB + (hh % 2) * 800, 798)
                    nm, sm = small[:, 360 + (hh % 2) * 24:366 + (hh % 2) * 24], small[:, 366 + (hh % 2) * 24:372 + (hh % 2) * 24]
                    cuts = [(b * P, P) for b in range(2)] + [(S + b * S, S) for b in range(2)] + \
                           [(3 * S + tt * NC, NC) for tt in range(TT)]
                    for n, (at, w) in enumerate(cuts):
                        last = act.activation(pr[:, at:at + w], pr[:, at:at + w], ACT.Exp, bias=nm[:, n:n + 1],
                                              accum_out=sm[:, n:n + 1]).then_inc(ev("exps"), 1)

                def keep_pt(hh):
                    act.wait_ge(ev("p_turned"), n_of(hh) + 1)
                    if not (first and hh == 0):
                        act.wait_ge(ev("pv"), n_of(hh))
                    act.activation(ar(A_MG + 16 * KB, 2 * S), bank[5][:, :], ACT.Copy).then_inc(ev("p_kept_a"), 1)

                def keep_o(hh):
                    act.wait_ge(ev("pv"), n_of(hh) + 1)
                    act.activation(act1_hi[:, ds(i * 4 * S + hh * S, S)], bank[7][:, 0:S], ACT.Copy)\
                       .then_inc(ev("o_hi"), 1)

                def silu(b):
                    act.wait_ge(ev("conv_done"), i * 2 + (b - 1))
                    act.activation(arena[:, ds(i * 8 * S + (A_XBC + (b * 4 - 8) * S), 4 * S)], ar(A_K + 8 * KB, 4 * S),
                                   ACT.Silu).then_inc(ev("silu_done"), 1)

                for m in range(12):
                    pair(Tile(i, 12, T_ATT + m))
                    if not first and m in (4, 9):
                        silu(m // 5)
                    if m - 2 in starts:
                        exps(starts.index(m - 2))
                    if not (first and m == 0):
                        att_keep(Tile(i, 12, m - 1))
                    if m - 3 in starts:
                        keep_pt(starts.index(m - 3))
                    if m - 4 in starts:
                        keep_o(starts.index(m - 4))

            attention_turn(0, True)
            act.wait_ge(ev("cmp_kept"), 2)
            act.nop().then_inc(ev("silu_done"), 1)
            with act.Fori(1, GROUPS) as i:
                attention_turn(i, False)
            att_keep(Tile(0, 12, ATT_T - 1))
            if stop < 3:
                return

            act.wait_ge(tile_evicted, T_SSD)
            ebuf = [ar(A_K + (6 + 4 * c) * KB, PIECE) for c in range(2)]
            cs_buf = ar(A_K + 14 * KB, PIECE)
            xde = ar(A_K + 22 * KB, 512)
            btok = small[:, 700:828]
            ssd_keep = keep_in(A_MG + 8 * KB, T_SSD)

            def ssd_turn(i, first):
                def evict(m):
                    if not (first and m == 0):
                        ssd_keep(Tile(i, 6, m - 1))
                pair(Tile(i, 6, T_SSD))
                evict(0)
                act.wait_ge(ev("b_turned"), i + 1)
                if not first:
                    act.wait_ge(ev("state"), i)
                act.activation(btok, bank[6][:, 0:P], ACT.Copy).then_inc(ev("b_kept"), 1)
                pair(Tile(i, 6, T_SSD + 1))
                evict(1)
                zt = arena[:, ds(A_Z + i * 4 * S, 4 * S)]
                act.activation(zt, zt, ACT.Silu).then_inc(ev("z_done"), 1)
                pair(Tile(i, 6, T_SSD + 2))
                act.wait_ge(ev("seg_ready"), i * 2 + 1)
                act.activation(ebuf[0], ebuf[0], ACT.Exp).then_inc(ev("seg_exp"), 1)
                evict(2)
                pair(Tile(i, 6, T_SSD + 3))
                act.wait_ge(ev("acsb"), i * 2 + 2)
                act.wait_ge(ev("seg_ready"), i * 2 + 2)
                if not first:
                    act.wait_ge(ev("gsum"), i)
                for n in range(2):
                    act.activation(cs_buf[:, n * 512:(n + 1) * 512], bank[4 + n][:, :], ACT.Exp)\
                       .then_inc(ev("c_exp"), 1)
                act.activation(ebuf[1], ebuf[1], ACT.Exp).then_inc(ev("seg_exp"), 1)
                evict(3)
                act.wait_ge(ev("state"), i + 1)
                act.activation(xde, bank[7][:, :], ACT.Copy).then_inc(ev("state_kept"), 1)
                pair(Tile(i, 6, T_SSD + 4))
                evict(4)
                pair(Tile(i, 6, T_SSD + 5))
                act.wait_ge(ev("g_ready"), i + 1)
                act.nop(nofuse=True)
                act.activation(cs_buf, arena[:, ds(A_Z + i * 4 * S, 4 * S)], ACT.Square).then_inc(ev("gsq_ready"), 1)
                evict(5)

            ssd_turn(0, True)
            with act.Fori(1, SG) as i:
                ssd_turn(i, False)
            ssd_keep(Tile(0, 6, SSD_T - 1))
            if stop < 4:
                return

            def gate0(T):
                act.activation(arena[:, ds(T.times(S, A_MG), S)], arena[:, ds(T.times(S, A_MG), S)], ACT.Sigmoid,
                               bias=par[:, ds(T.times(1, V_GB), 1)]).then_inc(ev("gate_ready"), 1)

            def gate1(T):
                act.activation(arena[:, ds(T.times(S, A_MG + KT * S), S)], arena[:, ds(T.times(S, A_MG + KT * S), S)],
                               ACT.Sigmoid, bias=par[:, ds(T.times(1, V_GB + KT), 1)]).then_inc(ev("gate_ready"), 1)

            def y_norm(i, m, first):
                if m == 1:
                    act.wait_ge(ev("gvar"), i + 1)
                    act.activation(ar(A_K + S, S), ar(A_K, S), ACT.Sqrt).then_inc(ev("groot"), 1)
                if m == 3:
                    act.wait_ge(ev("gn_ready"), i + 1)
                    act.wait_ge(piece_used, 2 * T_BN)
                    act.activation(act0_hi[:, ds(i * PIECE, PIECE)], arena[:, ds(A_Z + i * PIECE, PIECE)], ACT.Copy)\
                       .then_inc(ev("gn_hi"), 1)

            stage(T_BN, KT, gate0, per=4, beside=y_norm, goes_on=True)

            def bs(T):
                gate1(T)
                act.wait_ge(ev("merged"), T.times(1, 1))
                act.activation(act1_hi[:, ds(T.times(S), S)], arena[:, ds(T.times(S, A_MG), S)], ACT.Copy)\
                   .then_inc(ev("merged_hi"), 1)

            stage(T_BS, KT, bs, begun=True, goes_on=True)

            def wo(T):
                act.wait_ge(ev("x2_ready"), T.times(1, 1))
                act.activation(act0_hi[:, ds(T.times(S), S)], arena[:, ds(T.times(S, A_MG), S)], ACT.Copy)\
                   .then_inc(ev("x2g_hi"), 1)

            stage(T_WO, KT, wo, begun=True, goes_on=True)

            def root(i, m, first):
                if first and m == 1:
                    act.wait_ge(ev("x2var"), 1)
                    act.activation(ar(A_XBC + 18 * KB, S), ar(A_XBC + 17 * KB, S), ACT.Sqrt)\
                       .then_inc(ev("x2root"), 1)

            stage(T_WQ, KT, nothing, beside=root, begun=True, goes_on=True)
            if stop < 5:
                return

            s_all = ar(A_Z, KT * S)

            def keep_scores(i, m, first):
                if not (first and m == 1):
                    return
                for n in range(1, 8, 2):
                    act.wait_ge(ev("s_sum"), n + 1)
                    act.wait_ge(ev("s_kept"), n)
                    act.wait_ge(ev("spilled"), 16)
                    act.activation(s_all[:, n * 512:(n + 1) * 512], bank[4 + n % 4][:, :], ACT.Copy)\
                       .then_inc(ev("s_kept"), 1)

            def gelu(T0):
                def evict(T):
                    act.wait_ge(tile_evicted, T.times(1, T_U + T0 + 1))
                    act.activation(arena[:, ds(T.times(S, T0 * S), S)], arena[:, ds(T.times(S, T0 * S), S)], ACT.Gelu)\
                       .then_inc(ev("g_done"), 1)
                return evict

            stage(T_U, U1_T, gelu(0), beside=keep_scores, begun=True)
            act.wait_ge(ev("gate_in"), 1)
            gates = ar(A_Z - 3 * KB + 2 * S, S)
            act.activation(gates, gates, ACT.Exp).then_inc(ev("gate_exp"), 1)
            u2_gelu = gelu(U1_T)

            def u2_turn(i, first):
                for m in range(W_TILES):
                    pair(Tile(i, W_TILES, T_U2 + m))
                    if not (first and m == 0):
                        u2_gelu(Tile(i, W_TILES, m - 1))

            u2_turn(0, True)
            with act.Fori(1, W_STEPS // W_TURN) as i:
                u2_turn(i, False)
            u2_gelu(Tile(0, 2, NKEY - U1_T - U3_T - 1))
            stage(T_U3, U3_T, gelu(NKEY - U3_T))
            if stop < 7:
                return

            act.wait_ge(ev("w_used"), W_STEPS)
            act.wait_ge(piece_used, P_V)
            for s in range(4):
                if s == 2:
                    act.wait_ge(ev("w_used"), 2 * W_STEPS)
                with act.Fori(s * SWEEP, (s + 1) * SWEEP) as i:
                    for m in range(8):
                        slot = m % 4
                        act.wait_ge(raw_landed[slot], i * 32 + (P_V // 4 + m // 4 + 1) * 16)
                        act.wait_ge(piece_used, i * 8 + (P_V + m - 3))
                        act.activation(piece_ap(w_hi, slot), piece_ap(raw, slot), ACT.Copy).then_inc(hi_ready, 1)
                        act.activation(av_hi[:, slot * S:(slot + 1) * S], expert_col(s, i, m), ACT.Copy)\
                           .then_inc(ev("av_hi_r"), 1)
            act.wait_ge(ev("sweep_used"), 3)
            for b in range(8):
                if b >= 4:
                    act.wait_ge(ev("last_kept"), b - 3)
                act.activation(ar(b * 512, 512), x3[:, b * 512:(b + 1) * 512], ACT.Square).then_inc(ev("fsq"), 1)
            act.wait_ge(ev("fvar"), 1)
            act.activation(ar(A_XBC + S, S), ar(A_XBC, S), ACT.Sqrt).then_inc(ev("froot"), 1)

        @block.vector
        def _(v):
            st = Steps(v, v_step)

            def lo(T, h):
                slot = (T.c % 2) * 2 + h
                v.wait_ge(hi_ready, T.times(2, h + 1))
                wait(v, piece_used, T.times(2, h - 1))
                v.tensor_tensor(piece_ap(w_lo, slot % 2), piece_ap(raw, slot), piece_ap(w_hi, slot).bitcast(F32),
                                ALU.subtract).then_inc(lo_ready, 1)

            def pair(T):
                lo(T, 0)
                lo(T, 1)

            def stage(T0, n, evict=None, steps=0, late=None, per=2, beside=None, begun=False, goes_on=False):
                def turn(i, first):
                    for m in range(per):
                        if not (first and m == 0 and begun):
                            lo(Tile(i, per, T0 + m), 0)
                        lo(Tile(i, per, T0 + m), 1)
                        if beside:
                            beside(i, m, first)
                        if late and not (first and m < 2):
                            late(Tile(i, per, m - 2))
                        if evict and not (first and m == 0):
                            evict(Tile(i, per, m - 1))
                turn(0, True)
                st.turns(1, n // per, steps, lambda i: turn(i, False))
                if goes_on:
                    lo(Tile(0, per, T0 + n), 0)
                if late:
                    late(Tile(0, per, n - 2))
                if evict:
                    evict(Tile(0, per, n - 1))
                if late:
                    late(Tile(0, per, n - 1))

            def rstd(total, n, var, root, t1, out, var_ev, root_ev):
                v.tensor_scalar(var, total, 1.0 / n, EPS, ALU.mult, ALU.add).then_inc(var_ev, 1)
                v.wait_ge(root_ev, 1)
                inverse_root(var, root, t1, out)

            def inverse_root(var, root, t1, out):
                st(v.reciprocal(out, root))
                st(v.tensor_tensor(t1, out, out, ALU.mult))
                st(v.tensor_tensor(t1, t1, var, ALU.mult))
                st(v.tensor_scalar(t1, t1, -0.5, 1.5, ALU.mult, ALU.add))
                st(v.tensor_tensor(out, out, t1, ALU.mult))

            v.wait_ge(a_step, 1)
            v.wait_ge(par_in, 32)
            v.tensor_reduce(ar(A_VTOK, S), ar(0, KT * S).rearrange("p (k t) -> p t k", k=KT), AX.X, ALU.add)\
             .then_inc(ev("sq_ready"), 1)
            v.wait_ge(ev("sum_ready"), 1)
            r1 = ar(A_K + 2 * S, S)
            rstd(bank[2][:, 0:S], D, ar(A_K, S), ar(A_K + S, S), ar(A_K + 3 * S, S), r1,
                 ev("var_ready"), ev("root_ready"))
            for c in range(4):
                buf = ar(A_MG + (16 + 4 * (c % 2)) * KB, PIECE)
                for k in range(4):
                    kt = 4 * c + k
                    ins = v.scalar_tensor_tensor(buf[:, k * S:(k + 1) * S], ar(A_MG + kt * S, S),
                                                 par[:, V_AN + kt:V_AN + kt + 1], r1, ALU.mult, ALU.mult)
                    st.mark(ins)
                st.wait()
                v.nop().then_inc(ev("h_ready"), 1)
                v.wait_ge(ev("h_hi"), c + 1)
                v.tensor_tensor(act0_lo[:, c * PIECE:(c + 1) * PIECE], buf,
                                act0_hi[:, c * PIECE:(c + 1) * PIECE].bitcast(F32), ALU.subtract)\
                 .then_inc(ev("h_split"), 1)
                v.wait_ge(ev("h_split"), c + 1)
            stage(T_A, QKV_A)
            stage(T_B, QKV_B)

            v.wait_ge(phase_in, 16)
            v.wait_ge(tile_evicted, T_ATT)
            scratch = ar(A_MG + 8 * KB, 512)
            two = lambda x: x.unsqueeze(1).broadcast_to([P, 2, S])
            pair2 = lambda x: x.rearrange("p (b t) -> p b t", b=2)
            for n in range(6):
                k = ar(A_K + n * 512, 512)
                v.wait_ge(ev("krot"), n + 1)
                st(v.tensor_tensor(pair2(scratch), pair2(bank[2 + n % 4][:, :]), two(sin_t), ALU.mult))
                st(v.tensor_tensor(pair2(k), pair2(k), two(cos_t), ALU.mult))
                st(v.tensor_tensor(k, k, scratch, ALU.add))
                v.nop().then_inc(ev("krope"), 1)
            for n in range(4):
                v.wait_ge(ev("v_turned"), n + 1)
                v.tensor_copy(ar(A_VTOK + n * 512, 512), bank[2 + n][:, :]).then_inc(ev("v_kept"), 1)
            v.wait_ge(ev("g_kept"), 2)
            v.wait_ge(a_step, 3)
            dt2 = small[:, 96:160].rearrange("p (c h) -> p c h", c=2)
            v.tensor_tensor(dt2, bank[6][:, 2 * P:4 * P].rearrange("p (c h) -> p c h", c=2)[:, :, 0:SH],
                            par[:, V_DTB:V_DTB + SH].unsqueeze(1).broadcast_to([P, 2, SH]), ALU.add)\
             .then_inc(ev("g_kept"), 1)
            tmp = ar(A_MG + 8 * KB, 64 * 12)
            x_dt, dta, acs = small[:, 96:160], small[:, 160:224], small[:, 224:288]
            dtdte, dte = small[:, 288:320], small[:, 328:360]
            v.wait_ge(ev("g_kept"), 3)
            st(v.tensor_scalar(tmp[:, 192:256], x_dt, -1.0, None, ALU.mult))
            v.tensor_tensor(tmp[:, 0:64], x_dt, tmp[:, 192:256], ALU.max).then_inc(ev("dt_in"), 1)
            v.wait_ge(ev("dt_exp"), 2)
            u, s_, s2, acc = tmp[:, 64:128], tmp[:, 256:320], tmp[:, 320:384], tmp[:, 384:448]
            st(v.tensor_scalar(s_, u, 2.0, None, ALU.add))
            st(v.reciprocal(s_, s_))
            st(v.tensor_tensor(s_, s_, u, ALU.mult))
            st(v.tensor_tensor(s2, s_, s_, ALU.mult))
            st(v.tensor_scalar(acc, s2, 1.0 / 17, 1.0 / 15, ALU.mult, ALU.add))
            for k in (13, 11, 9, 7, 5, 3, 1):
                st(v.tensor_tensor(acc, acc, s2, ALU.mult))
                st(v.tensor_scalar(acc, acc, 1.0 / k, None, ALU.add))
            st(v.tensor_tensor(acc, acc, s_, ALU.mult))
            st(v.tensor_scalar(x_dt, x_dt, 0.0, None, ALU.max))
            st(v.scalar_tensor_tensor(x_dt, acc, 2.0, x_dt, ALU.mult, ALU.add))
            st(v.tensor_scalar(tmp[:, 128:160], tmp[:, 128:160], -1.0, None, ALU.mult))
            v.tensor_tensor(dta.rearrange("p (c h) -> p c h", c=2), x_dt.rearrange("p (c h) -> p c h", c=2),
                            tmp[:, 128:160].unsqueeze(1).broadcast_to([P, 2, SH]), ALU.mult)\
             .then_inc(ev("dta_ready"), 1)
            for c in range(2):
                v.wait_ge(ev("hid_sum"), c + 1)
                st(v.tensor_tensor(small[:, 360 + c:361 + c], bank[1][:, 0:1], par[:, V_B1 + c:V_B1 + c + 1], ALU.add))
                v.tensor_scalar(ar(A_MG + 27 * KB + c * 64, GROUPS * NC), bank[0][:, 0:GROUPS * NC],
                                small[:, 360 + c:361 + c], None, ALU.add).then_inc(ev("hid_used"), 1)
            v.wait_ge(ev("acs_sum"), 1)
            v.tensor_copy(acs, bank[2][:, 0:64]).then_inc(ev("acs_kept"), 1)
            v.wait_ge(ev("acs_kept"), 1)
            v.tensor_tensor(dte, bank[2][:, 64:96], acs[:, 0:32], ALU.subtract).then_inc(ev("dte_in"), 1)
            if stop < 2:
                return

            starts = (0, 2, 5, 7)
            gsig = small[:, 0:96]

            def attention_turn(i, first):
                def n_of(hh):
                    return i * 4 + hh

                def bufs(hh):
                    o = 360 + (hh % 2) * 24
                    return (ar(A_MG + 8 * KB + (hh % 2) * 800, 798), small[:, o:o + 6], small[:, o + 6:o + 12],
                            small[:, o + 12:o + 18])

                def rope(hh):
                    v.wait_ge(ev("q_rot"), n_of(hh) + 1)
                    q = ar(A_MG + 20 * KB + (hh % 2) * S, S)
                    t = ar(A_MG + 22 * KB, S)
                    st.mark(v.tensor_tensor(t, bank[2][:, 0:S], sin_t, ALU.mult))
                    st(v.tensor_tensor(q, arena[:, ds(i * 4 * S + hh * S, S)], cos_t, ALU.mult))
                    v.tensor_tensor(q, q, t, ALU.add).then_inc(ev("q_roped"), 1)
                    v.wait_ge(ev("q_roped"), n_of(hh) + 1)

                def score(hh):
                    v.wait_ge(ev("scores"), n_of(hh) + 1)
                    if not (first and hh < 2):
                        v.wait_ge(ev("p_turned"), n_of(hh) - 1)
                    pr, nm, sm, wg = bufs(hh)
                    m0 = mask_t[:, P:S].unsqueeze(1).broadcast_to([P, 2, P])
                    s0 = pr[:, 0:S].rearrange("p (b s) -> p b s", b=2)
                    s1 = pr[:, S:3 * S].rearrange("p (b s) -> p b s", b=2)
                    s2 = pr[:, 3 * S:3 * S + 2 * NC].rearrange("p (b s) -> p b s", b=2)
                    st.mark(v.scalar_tensor_tensor(s0, bank[3][:, 0:S].rearrange("p (b s) -> p b s", b=2), SCALE, m0,
                                                   ALU.mult, ALU.add))
                    st.mark(v.scalar_tensor_tensor(s1, bank[4][:, :].rearrange("p (b s) -> p b s", b=2), SCALE,
                                                   two(mask_t), ALU.mult, ALU.add))
                    st(v.scalar_tensor_tensor(pr[:, 3 * S:3 * S + 2 * NC], bank[2][:, 0:2 * NC], SCALE,
                                              cmp_bias, ALU.mult, ALU.add))
                    st.mark(v.tensor_reduce(nm[:, 0:2], s0, AX.X, ALU.max, negate=True))
                    st.mark(v.tensor_reduce(nm[:, 2:4], s1, AX.X, ALU.max, negate=True))
                    v.tensor_reduce(nm[:, 4:6], s2, AX.X, ALU.max, negate=True).then_inc(ev("scored"), 1)
                    st.wait()

                def probs(hh):
                    v.wait_ge(ev("exps"), i * 24 + 6 * (hh + 1))
                    pr, nm, sm, wg = bufs(hh)
                    st(v.reciprocal(wg, sm))
                    st(v.tensor_tensor(wg, wg, gsig_at(i, hh), ALU.mult))
                    s0 = pr[:, 0:S].rearrange("p (b s) -> p b s", b=2)
                    s1 = pr[:, S:3 * S].rearrange("p (b s) -> p b s", b=2)
                    s2 = pr[:, 3 * S:3 * S + 2 * NC].rearrange("p (b s) -> p b s", b=2)
                    st(v.tensor_tensor(s2, s2, cmp_01.rearrange("p (b s) -> p b s", b=2), ALU.mult))
                    st.mark(v.tensor_tensor(s2, s2, wg[:, 4:6].unsqueeze(2).broadcast_to([P, 2, NC]), ALU.mult))
                    st.mark(v.tensor_tensor(s0, s0, wg[:, 0:2].unsqueeze(2).broadcast_to([P, 2, P]), ALU.mult))
                    v.tensor_tensor(s1, s1, wg[:, 2:4].unsqueeze(2).broadcast_to([P, 2, S]), ALU.mult)\
                     .then_inc(ev("probs"), 1)

                def gsig_at(i, hh):
                    return small[:, ds(i * 24 + hh * 6, 6)]

                def keep_pt(hh):
                    v.wait_ge(ev("p_turned"), n_of(hh) + 1)
                    pt = ar(A_MG + 16 * KB, 4 * S)
                    if not (first and hh == 0):
                        v.wait_ge(ev("pv"), n_of(hh))
                    st(v.tensor_copy(pt[:, 2 * S:3 * S], bank[6][:, 0:S]))
                    v.tensor_copy(pt[0:NC, 3 * S:4 * S], bank[6][0:NC, S:2 * S]).then_inc(ev("p_kept_b"), 1)

                def keep_o(hh):
                    v.wait_ge(ev("o_hi"), n_of(hh) + 1)
                    v.tensor_tensor(act1_lo[:, ds(i * 4 * S + hh * S, S)], bank[7][:, 0:S],
                                    act1_hi[:, ds(i * 4 * S + hh * S, S)].bitcast(F32), ALU.subtract)\
                     .then_inc(ev("o_lo"), 1)

                def conv(b, n):
                    if n == 0:
                        v.wait_ge(tile_evicted, i * 8 + T_ATT)
                        v.wait_ge(ev("silu_done"), i * 2 + (b - 1))
                    for t in range(4):
                        out = ar(A_K + 8 * KB + t * S, S)
                        w = par[:, ds(i * 32 + (V_CW + (b * 4 - 8 + t) * 4 + 3 - n), 1)]
                        u = arena[:, ds(i * 8 * S + (A_XBC + (b * 4 - 8 + t) * S), S - n)]
                        if n == 0:
                            ins = v.tensor_scalar(out, u, w, par[:, ds(i * 8 + (V_CB + b * 4 - 8 + t), 1)],
                                                  ALU.mult, ALU.add)
                        else:
                            ins = v.scalar_tensor_tensor(out[:, n:S], u, w, out[:, n:S], ALU.mult, ALU.add)
                        if n < CONV - 1:
                            st.mark(ins)
                    if n < CONV - 1:
                        st.wait()
                    else:
                        ins.then_inc(ev("conv_done"), 1)

                for m in range(12):
                    T = Tile(i, 12, T_ATT + m)
                    lo(T, 0)
                    if not first and m < 10 and m % 5 < CONV:
                        conv(m // 5, m % 5)
                    lo(T, 1)
                    if m in starts:
                        rope(starts.index(m))
                    if m - 1 in starts:
                        score(starts.index(m - 1))
                    if m - 2 in starts:
                        probs(starts.index(m - 2))
                    if m - 3 in starts:
                        keep_pt(starts.index(m - 3))
                    if m - 4 in starts:
                        keep_o(starts.index(m - 4))

            attention_turn(0, True)
            st.turns(1, GROUPS, 4 * 13 + 2 * 4 * (CONV - 1), lambda i: attention_turn(i, False))
            if stop < 3:
                return

            v.wait_ge(ev("dte_ready"), 1)
            x_dt, dtdte, dte = small[:, 96:160], small[:, 288:320], small[:, 328:360]
            v.tensor_tensor(dtdte, dte, x_dt[:, 0:32], ALU.mult).then_inc(ev("dtdte_ready"), 1)
            v.wait_ge(ev("dtdte_ready"), 1)

            xs_stage = ar(A_K, 4 * S)
            c_stage = ar(A_K + 5 * KB, S)
            ebuf = [ar(A_K + (6 + 4 * c) * KB, PIECE) for c in range(2)]
            cs_buf = ar(A_K + 14 * KB, PIECE)
            xdt = [ar(A_K + (18 + 2 * c) * KB, 512) for c in range(2)]
            xde = ar(A_K + 22 * KB, 512)
            cbm = small[:, 444:700]
            v.wait_ge(ev("silu_done"), XBC_T // 4 + 1)

            def heads(x):
                return x.rearrange("p (r l) -> p r l", r=SHG)

            def over(x, n):
                return x.unsqueeze(2).broadcast_to([P, SHG, n])

            def ssd_turn(i, first):
                def per_head(t, c):
                    return small[:, ds(i * 8 + (t + 32 * c), 8)]
                if not first:
                    v.wait_ge(ev("y_sum"), i)
                for c in range(2):
                    v.tensor_tensor(heads(ebuf[c]), tri.unsqueeze(1).broadcast_to([P, SHG, P]),
                                    over(per_head(160, c), P), ALU.mult).then_inc(ev("dtatri"), 1)
                pair(Tile(i, 6, T_SSD))
                v.wait_ge(ev("x_turned"), i + 1)
                for c in range(2):
                    st.mark(v.tensor_tensor(xdt[c].rearrange("p (r d) -> p r d", r=SHG),
                                            bank[2 + c][:, :].rearrange("p (r d) -> p r d", r=SHG),
                                            over(per_head(96, c), SP_), ALU.mult))
                v.tensor_tensor(xde.rearrange("p (r d) -> p r d", r=SHG),
                                bank[2][:, :].rearrange("p (r d) -> p r d", r=SHG),
                                over(small[:, ds(i * 8 + 288, 8)], SP_), ALU.mult).then_inc(ev("xdt_ready"), 1)
                v.wait_ge(ev("b_kept"), i + 1)
                st(v.tensor_tensor(cbm.rearrange("p (c l) -> p c l", c=2),
                                   bank[6][:, P:3 * P].rearrange("p (c l) -> p c l", c=2),
                                   tri.unsqueeze(1).broadcast_to([P, 2, P]), ALU.mult))
                pair(Tile(i, 6, T_SSD + 1))

                def seg(c):
                    v.wait_ge(ev("acsb"), i * 2 + (c + 1))
                    for n in range(2):
                        ins = v.tensor_tensor(
                            ebuf[c][:, n * 512:(n + 1) * 512].rearrange("p (r l) -> p r l", r=4),
                            bank[4 + n][:, :].rearrange("p (r l) -> p r l", r=4),
                            small[:, ds(i * 8 + (224 + 32 * c + 4 * n), 4)].unsqueeze(2).broadcast_to([P, 4, P]),
                            ALU.subtract)
                        st.mark(ins)
                    st.wait()
                    v.tensor_scalar(ebuf[c], ebuf[c], 0.0, None, ALU.min).then_inc(ev("seg_ready"), 1)

                def decay(c):
                    v.wait_ge(ev("seg_exp"), i * 2 + (c + 1))
                    v.tensor_tensor(heads(ebuf[c]), heads(ebuf[c]),
                                    cbm[:, c * P:(c + 1) * P].unsqueeze(1).broadcast_to([P, SHG, P]),
                                    ALU.mult).then_inc(ev("m_ready"), 1)

                seg(0)
                pair(Tile(i, 6, T_SSD + 2))
                seg(1)
                pair(Tile(i, 6, T_SSD + 3))
                decay(0)
                decay(1)
                v.wait_ge(ev("c_exp"), i * 2 + 2)
                v.tensor_tensor(heads(cs_buf), heads(cs_buf), c_stage[:, P:S].unsqueeze(1).broadcast_to([P, SHG, P]),
                                ALU.mult).then_inc(ev("c_ready"), 1)
                pair(Tile(i, 6, T_SSD + 4))
                v.wait_ge(ev("y_sum"), i + 1)
                for t in range(4):
                    st.mark(v.scalar_tensor_tensor(xs_stage[:, t * S:(t + 1) * S], xs_stage[:, t * S:(t + 1) * S],
                                                   par[:, ds(i * 4 + (V_DS + t), 1)],
                                                   bank[2 + t // 2][:, (t % 2) * S:(t % 2 + 1) * S],
                                                   ALU.mult, ALU.add))
                st.wait()
                zt = arena[:, ds(A_Z + i * 4 * S, 4 * S)]
                v.wait_ge(ev("z_done"), i + 1)
                v.tensor_tensor(zt, zt, xs_stage, ALU.mult).then_inc(ev("g_ready"), 1)
                pair(Tile(i, 6, T_SSD + 5))
                v.wait_ge(ev("gsum"), i + 1)
                v.tensor_copy(arena[:, ds(A_XBC + i * 4 * S, S)], bank[7][:, 0:S]).then_inc(ev("gsum_kept"), 1)

            SSD_STEPS = 2 + 1 + 4 + 4
            ssd_turn(0, True)
            st.turns(1, SG, SSD_STEPS, lambda i: ssd_turn(i, False))
            if stop < 4:
                return

            v.wait_ge(ev("gsum_kept"), SG)
            gr = ar(A_K + 2 * S, S)

            def bn(T):
                v.wait_ge(ev("gate_ready"), T.times(1, 1))
                v.wait_ge(piece_used, T.times(2, 2 * T_BN + 2))
                m0 = arena[:, ds(T.times(S, A_MG), S)]
                v.tensor_tensor(m0, m0, bank[T.c % 2][:, 0:S], ALU.mult).then_inc(tile_evicted, 1)

            def y_norm(i, m, first):
                if m == 0:
                    v.tensor_scalar(ar(A_K, S), arena[:, ds(A_XBC + i * 4 * S, S)], 1.0 / (4 * P), EPS,
                                    ALU.mult, ALU.add).then_inc(ev("gvar"), 1)
                if m == 1:
                    v.wait_ge(ev("groot"), i + 1)
                    inverse_root(ar(A_K, S), ar(A_K + S, S), ar(A_K + 3 * S, S), gr)
                if m == 2:
                    for k in range(4):
                        z = arena[:, ds(A_Z + i * PIECE + k * S, S)]
                        ins = v.scalar_tensor_tensor(z, z, par[:, ds(i * 4 + (V_SN + k), 1)], gr, ALU.mult, ALU.mult)
                    ins.then_inc(ev("gn_ready"), 1)
                if m == 3:
                    v.wait_ge(ev("gn_hi"), i + 1)
                    v.tensor_tensor(act0_lo[:, ds(i * PIECE, PIECE)], arena[:, ds(A_Z + i * PIECE, PIECE)],
                                    act0_hi[:, ds(i * PIECE, PIECE)].bitcast(F32), ALU.subtract)\
                     .then_inc(ev("g_split"), 1)

            stage(T_BN, KT, bn, steps=5, per=4, beside=y_norm, goes_on=True)

            def bs(T):
                v.wait_ge(ev("gate_ready"), T.times(1, KT + 1))
                v.wait_ge(piece_used, T.times(2, 2 * T_BS + 2))
                m1 = arena[:, ds(T.times(S, A_MG + KT * S), S)]
                m0 = arena[:, ds(T.times(S, A_MG), S)]
                v.tensor_tensor(m1, m1, bank[T.c % 2][:, 0:S], ALU.mult).then_inc(tile_evicted, 1)
                v.wait_ge(tile_evicted, T.times(1, T_BS + 1))
                v.tensor_tensor(m0, m0, m1, ALU.add).then_inc(ev("merged"), 1)

            def bs_lo(T):
                v.wait_ge(ev("merged_hi"), T.times(1, 1))
                v.tensor_tensor(act1_lo[:, ds(T.times(S), S)], arena[:, ds(T.times(S, A_MG), S)],
                                act1_hi[:, ds(T.times(S), S)].bitcast(F32), ALU.subtract)\
                 .then_inc(ev("merged_lo"), 1)

            stage(T_BS, KT, bs, late=bs_lo, begun=True, goes_on=True)

            def wo(T):
                v.wait_ge(piece_used, T.times(2, 2 * T_WO + 2))
                x2 = arena[:, ds(T.times(S, A_Z), S)]
                v.tensor_tensor(x2, bank[T.c % 2][:, 0:S], arena[:, ds(T.times(S, A_XBC), S)], ALU.add)\
                 .then_inc(tile_evicted, 1)
                v.wait_ge(tile_evicted, T.times(1, T_WO + 1))
                v.tensor_scalar(arena[:, ds(T.times(S, A_MG), S)], x2, par[:, ds(T.times(1, V_FN), 1)], None, ALU.mult)\
                 .then_inc(ev("x2_ready"), 1)

            def wo_lo(T):
                v.wait_ge(ev("x2g_hi"), T.times(1, 1))
                v.tensor_tensor(act0_lo[:, ds(T.times(S), S)], arena[:, ds(T.times(S, A_MG), S)],
                                act0_hi[:, ds(T.times(S), S)].bitcast(F32), ALU.subtract)\
                 .then_inc(ev("x2g_lo"), 1)

            v.wait_ge(ev("res_in"), 16)
            stage(T_WO, KT, wo, late=wo_lo, begun=True, goes_on=True)

            def residual_rstd(i, m, first):
                if first and m == 1:
                    v.wait_ge(ev("x2sum"), 1)
                    rstd(bank[2][:, 0:S], D, ar(A_XBC + 17 * KB, S), ar(A_XBC + 18 * KB, S), ar(A_XBC + 19 * KB, S), r2,
                         ev("x2var"), ev("x2root"))

            def wq(T):
                v.wait_ge(piece_used, T.times(2, 2 * T_WQ + 2))
                v.tensor_tensor(arena[:, ds(T.times(S, A_MG + 16 * KB), S)], bank[T.c % 2][:, 0:S], r2, ALU.mult)\
                 .then_inc(tile_evicted, 1)

            stage(T_WQ, KT, wq, beside=residual_rstd, begun=True, goes_on=True)
            if stop < 5:
                return

            s_all = ar(A_Z, KT * S)

            def keep_scores():
                v.wait_ge(ev("spilled"), 16)
                for n in range(0, 8, 2):
                    v.wait_ge(ev("s_sum"), n + 1)
                    v.wait_ge(ev("s_kept"), n)
                    v.tensor_copy(s_all[:, n * 512:(n + 1) * 512], bank[4 + n % 4][:, :]).then_inc(ev("s_kept"), 1)
                v.wait_ge(ev("s_kept"), 8)

            top = ar(A_MG, 16 * KB)
            sc, sc2 = top[:, 0:S], top[:, S:2 * S]
            cand, cand2 = top[:, 2 * S:3 * S], top[:, 3 * S:4 * S]
            eq = top[:, 4 * S:5 * S]
            sv, sif = top[:, 5 * S:5 * S + 32], top[:, 5 * S + 32:5 * S + 64]
            si = top[:, 5 * S + 64:5 * S + 96].bitcast(U32)
            pos = top[:, 5 * S + 96:5 * S + 112].bitcast(U32)
            pa, pb = (top[:, 5 * S + k:5 * S + k + 16].bitcast(U32) for k in (112, 128))
            paf, pbf = top[:, 5 * S + 144:5 * S + 160], top[:, 5 * S + 160:5 * S + 176]
            best = top[:, 5 * S + 176:5 * S + 192]
            res_at = A_Z - 3 * KB
            mat = lambda x: x.rearrange("p (k a) -> p k a", k=16)
            rows = lambda x: x.unsqueeze(2).broadcast_to([P, 16, 16])
            cols = lambda x: x.unsqueeze(1).broadcast_to([P, 16, 16])
            FLOOR = -3.0e38

            def dots(T0):
                def evict(T):
                    v.wait_ge(piece_used, T.times(2, 2 * (T_U + T0) + 2))
                    v.tensor_tensor(arena[:, ds(T.times(S, T0 * S), S)], bank[T.c % 2][:, 0:S], r2, ALU.mult)\
                     .then_inc(tile_evicted, 1)
                return evict

            def top_parts(i):
                halves = [(sc[:, c * P:(c + 1) * P], sc2[:, c * P:(c + 1) * P], sv[:, c * 16:(c + 1) * 16],
                           si[:, c * 16:(c + 1) * 16]) for c in range(2)]

                def keys():
                    st.apart(v.tensor_copy(sc, arena[:, ds(A_Z + i * S, S)]))
                    for x, y, top, at in halves:
                        st.mark(v.max(top[:, 0:8], x))
                    st.wait()
                    v.nop(nofuse=True)
                    for x, y, top, at in halves:
                        st.mark(v.max_index(at[:, 0:8], top[:, 0:8], x))
                        st.mark(v.match_replace(y, top[:, 0:8], x, FLOOR))
                    st.wait()
                    v.nop(nofuse=True)
                    for x, y, top, at in halves:
                        st.mark(v.max(top[:, 8:16], y))
                    st.wait()
                    v.nop(nofuse=True)
                    for x, y, top, at in halves:
                        st.mark(v.max_index(at[:, 8:16], top[:, 8:16], y))

                def pairs():
                    st.apart(v.tensor_tensor(mat(cand), rows(sv[:, 0:16]), cols(sv[:, 16:32]), ALU.add))
                    st.mark(v.tensor_copy(sif, si))
                    st.apart(v.max(best[:, 0:8], cand))
                    st.mark(v.max_index(pos[:, 0:8], best[:, 0:8], cand))
                    st.apart(v.match_replace(cand2, best[:, 0:8], cand, FLOOR))

                def places():
                    st.apart(v.max(best[:, 8:16], cand2))
                    st(v.max_index(pos[:, 8:16], best[:, 8:16], cand2))
                    st.mark(v.tensor_copy(arena[:, ds(res_at + 2 * S + i * 16, 16)], best))
                    st.mark(v.tensor_scalar(pa, pos, 4, None, ALU.logical_shift_right))
                    st(v.tensor_scalar(pb, pos, 15, None, ALU.bitwise_and))
                    st.mark(v.tensor_copy(paf, pa))
                    st.mark(v.tensor_copy(pbf, pb))
                    st.wait()

                def index():
                    both = ((paf, eq), (pbf, cand))
                    for n, (place, e) in enumerate(both):
                        st.mark(v.tensor_tensor(mat(e), rows(place), cols(iota[:, 0:16]), ALU.is_equal))
                    st.wait()
                    for n, (place, e) in enumerate(both):
                        st.mark(v.tensor_tensor(mat(e), mat(e), cols(sif[:, n * 16:(n + 1) * 16]), ALU.mult))
                    st.wait()
                    for n, (place, e) in enumerate(both):
                        st.mark(v.tensor_reduce(arena[:, ds(res_at + n * S + i * 16, 16)], mat(e), AX.X, ALU.add))
                    st.wait()

                return keys, pairs, places, index

            scale1 = dots(0)

            def top_turn(i, first):
                parts = top_parts(i)
                for m in range(4):
                    if not (first and m == 0):
                        lo(Tile(i, 4, T_U + m), 0)
                    lo(Tile(i, 4, T_U + m), 1)
                    if not (first and m == 0):
                        scale1(Tile(i, 4, m - 1))
                    if first and m == 1:
                        keep_scores()
                        parts[0]()
                    if not (first and m == 0):
                        parts[m]()

            top_turn(0, True)
            st.turns(1, U1_T // 4, 11 + 5 + 7 + 6, lambda i: top_turn(i, False))
            scale1(Tile(0, 4, U1_T - 1))
            g3 = ar(res_at + 2 * S, S).rearrange("p (h k) -> p h k", k=16)
            mx = small[:, 352:368]
            st(v.tensor_copy(mx.unsqueeze(2), g3[:, :, 0:1]))
            v.tensor_tensor(g3, g3, mx.unsqueeze(2).broadcast_to([P, 16, 16]), ALU.subtract).then_inc(ev("gate_in"), 1)
            v.wait_ge(ev("gate_exp"), 1)
            st(v.tensor_reduce(mx, g3, AX.X, ALU.add))
            st(v.reciprocal(mx, mx))
            v.tensor_tensor(g3, g3, mx.unsqueeze(2).broadcast_to([P, 16, 16]), ALU.mult).then_inc(ev("gate_done"), 1)
            v.memset(zeros, 0.0).then_inc(ev("v_zero"), 1)
            v.wait_ge(ev("i_turned"), 3)
            v.tensor_copy(rows_i, bank[2][:, 0:S]).then_inc(ev("i_kept"), 1)
            st.mark(v.tensor_copy(cols_j, bank[3][:, 0:S]))
            st.mark(v.tensor_copy(iota_j, iota))
            st(v.tensor_copy(gate_part[0], bank[4][:, 0:S]))
            st(v.tensor_tensor(gate_rest, bank[4][:, 0:S], gate_part[0], ALU.subtract))
            st(v.tensor_copy(gate_part[1], gate_rest))
            st(v.tensor_tensor(gate_rest, gate_rest, gate_part[1], ALU.subtract))
            v.tensor_copy(gate_part[2], gate_rest).then_inc(ev("i_kept"), 1)
            v.wait_ge(ev("i_kept"), 2)
            v.wait_ge(ev("g_done"), U1_T)
            a_tj = ar(0, NKEY * S).rearrange("p (j t) -> p t j", t=S)
            tok = lambda x: x.rearrange("p (t j) -> p t j", t=WT)

            def cols(step, half, store, first=False):
                if not first:
                    v.wait_ge(ev("w_sum"), step.times(1, half * W_STEPS))
                st(v.tensor_tensor(tok(oh_cols(store, 0)),
                                   iota_j[:, half * JH:(half + 1) * JH].unsqueeze(1).broadcast_to([P, WT, JH]),
                                   over_j(cols_j, step), ALU.is_equal))

            def gated(step, store):
                for k in range(3):
                    ins = v.tensor_tensor(tok(oh_cols(store, k + 1)), tok(oh_cols(store, 0)),
                                          over_j(gate_part[k], step), ALU.mult)
                ins.then_inc(ev("gj"), 1)

            def gate_acts(step, half):
                v.wait_ge(ev("w_sum"), step.times(1, half * W_STEPS + 1))
                av = a_tj[:, ds(step.times(WT), WT), half * JH:(half + 1) * JH]
                v.tensor_tensor(av, av, tok(bank[2 + step.c % 2][:, :]), ALU.mult).then_inc(ev("w_used"), 1)

            u2_dots = dots(U1_T)

            def u2_turn(i, first):
                for m in range(W_TILES):
                    for h in range(2):
                        lo(Tile(i, W_TILES, T_U2 + m), h)
                        if h == 1 and not (first and m == 0):
                            u2_dots(Tile(i, W_TILES, m - 1))
                        at = 2 * m + h
                        if at - 3 in W_AT:
                            gate_acts(Tile(i, W_TURN, W_AT.index(at - 3)), 0)
                        if at in W_AT:
                            n = W_AT.index(at)
                            cols(Tile(i, W_TURN, n), 0, onehot_early, first and n == 0)
                        if at - 1 in W_AT:
                            gated(Tile(i, W_TURN, W_AT.index(at - 1)), onehot_early)

            u2_turn(0, True)
            st.turns(1, W_STEPS // W_TURN, 8, lambda i: u2_turn(i, False))
            u2_dots(Tile(0, 2, NKEY - U1_T - U3_T - 1))
            stage(T_U3, U3_T, dots(NKEY - U3_T))
            if stop < 7:
                return

            v.wait_ge(ev("g_done"), NKEY)
            v.wait_ge(piece_used, P_V)

            def v_turn(s, i):
                for m in range(8):
                    slot = m % 4
                    v.wait_ge(hi_ready, i * 8 + (P_V + m + 1))
                    v.wait_ge(piece_used, i * 8 + (P_V + m - 1))
                    v.tensor_tensor(piece_ap(w_lo, slot % 2), piece_ap(raw, slot), piece_ap(w_hi, slot).bitcast(F32),
                                    ALU.subtract).then_inc(lo_ready, 1)
                    v.wait_ge(ev("av_hi_r"), i * 8 + (m + 1))
                    v.tensor_tensor(av_lo[:, slot * S:(slot + 1) * S], expert_col(s, i, m),
                                    av_hi[:, slot * S:(slot + 1) * S].bitcast(F32), ALU.subtract)\
                     .then_inc(ev("av_lo_r"), 1)
                    if s < 2 and m % 4 == 0:
                        cols(Tile(i, 2, m // 4), 1, onehot_late)
                    if s < 2 and m % 4 == 1:
                        gated(Tile(i, 2, m // 4), onehot_late)
                    if s < 2 and m % 4 == 3:
                        gate_acts(Tile(i, 2, m // 4), 1)

            for s in range(4):
                st.turns(s * SWEEP, (s + 1) * SWEEP, 2 if s < 2 else 0, lambda i: v_turn(s, i))
                v.wait_ge(ev("back_in"), 16)
                v.wait_ge(ev("sweep"), s + 1)
                for b in range(4):
                    x = x3[:, ((s % 2) * 8 + 2 * b) * S:((s % 2) * 8 + 2 * b + 2) * S]
                    ins = v.tensor_tensor(x, x, bank[4 + b][:, :], ALU.add)
                    if s < 3:
                        st.mark(ins)
                    else:
                        ins.then_inc(ev("last_kept"), 1)
                if s < 3:
                    st.wait()
                    v.nop().then_inc(ev("sweep_used"), 1)
            v.wait_ge(ev("fsum"), 1)
            r3 = ar(A_XBC + 2 * S, S)
            rstd(bank[2][:, 0:S], D, ar(A_XBC, S), ar(A_XBC + S, S), ar(A_XBC + 3 * S, S), r3,
                 ev("fvar"), ev("froot"))
            for k in range(KT):
                x = x3[:, k * S:(k + 1) * S]
                v.scalar_tensor_tensor(x, x, par[:, V_ON + k:V_ON + k + 1], r3, ALU.mult, ALU.mult)\
                 .then_inc(ev("out_ready"), 1)

        @block.gpsimd
        def _(pool):
            st = Steps(pool, p_step)
            pool.dma_start(const, a["const"]).then_inc(par_in, 16)
            pool.dma_start(par, a["par"]).then_inc(par_in, 16)
            pool.dma_start(ar(phase_at, C_PHASE), a["phase"]).then_inc(phase_in, 16)
            pool.dma_start(ar(A_XBC, 2 * CB * P + 2 * P), a["cmp_w"]).then_inc(w1_in, 16)
            pool.wait_ge(par_in, 32)
            if stop < 2:
                pool.wait_ge(phase_in, 16)
                pool.wait_ge(w1_in, 16)
                return

            pool.wait_ge(ev("v_kept"), 4)
            pool.wait_ge(ev("cmp_kept"), 2)

            def stage_v(i, first):
                if not first:
                    pool.wait_ge(ev("pv"), i * 4)
                vs = ar(A_MG + 23 * KB, 4 * P)
                pool.tensor_copy(vs.rearrange("p (n d) -> p n d", n=4),
                                 ar(A_VTOK, 4 * 512).rearrange("p (n g d) -> p n g d", n=4, g=GROUPS)
                                 [:, :, ds(i, 1), :].rearrange("p n g d -> p n (g d)"))\
                    .then_inc(p_step, 1)
                pool.wait_ge(p_step, i + 1)
                pool.tensor_copy(ar(A_MG + 25 * KB, P)[0:NC, :], arena[0:NC, ds(A_K + 12 * KB + i * P, P)]).then_inc(ev("v_staged"), 1)

            stage_v(0, True)
            with pool.Fori(1, GROUPS) as i:
                stage_v(i, False)
            if stop < 3:
                return
            pool.wait_ge(ev("silu_done"), XBC_T // 4 + 1)
            pool.wait_ge(ev("pv"), HEADS)

            def stage_x(i, first):
                if not first:
                    pool.wait_ge(ev("g_ready"), i)
                pool.tensor_copy(ar(A_K, 4 * S), arena[:, ds(A_XBC + i * 4 * S, 4 * S)]).then_inc(p_step, 1)
                pool.tensor_copy(ar(A_K + 4 * KB, S), arena[:, ds(A_XBC + 16 * S + i * S, S)]).then_inc(p_step, 1)
                pool.tensor_copy(ar(A_K + 5 * KB, S), arena[:, ds(A_XBC + 20 * S + i * S, S)]).then_inc(p_step, 1)
                pool.wait_ge(p_step, i * 3 + (GROUPS + 3))
                pool.nop().then_inc(ev("x_staged"), 1)

            stage_x(0, True)
            with pool.Fori(1, SG) as i:
                stage_x(i, False)
            if stop < 4:
                return
            pool.wait_ge(ev("gvar"), SG)
            pool.dma_start(ar(A_XBC, KT * S).rearrange("p (k t) -> p k t", k=KT), a["x"].rearrange("k p t -> p k t"))\
                .then_inc(ev("res_in"), 16)
            acc, sq = ar(A_XBC + 16 * KB, S), ar(A_XBC + 20 * KB, S)
            pool.memset(acc, 0.0).then_inc(p_step, 1)
            n0 = GROUPS + 3 * SG + 1
            with pool.Fori(0, KT) as i:
                pool.wait_ge(ev("x2_ready"), i + 1)
                x2 = arena[:, ds(A_Z + i * S, S)]
                pool.wait_ge(p_step, i * 2 + n0)
                pool.tensor_tensor(sq, x2, x2, ALU.mult).then_inc(p_step, 1)
                pool.wait_ge(p_step, i * 2 + (n0 + 1))
                pool.tensor_tensor(acc, acc, sq, ALU.add).then_inc(p_step, 1)
                pool.wait_ge(p_step, i * 2 + (n0 + 2))
                pool.nop().then_inc(ev("sumsq"), 1)
            pool.dma_start(a["spill"], ar(A_Z, KT * S)).then_inc(ev("spilled"), 16)
            pool.wait_ge(ev("x2g_lo"), KT)
            pool.dma_start(ar(A_MG, 8 * KB), a["subk"]).then_inc(ev("subk_in"), 16)
            pool.wait_ge(ev("spilled"), 16)
            if stop < 6:
                pool.wait_ge(ev("subk_in"), 16)
                return

            pool.wait_ge(ev("i_kept"), 2)

            def onehot_rows(step, half, store, first=False):
                if not first:
                    pool.wait_ge(ev("w_sum"), step.times(1, half * W_STEPS))
                pool.tensor_copy(row_now, rows_i[:, ds(step.times(WT), WT)]).then_inc(ev("rows_ready"), 1)
                pool.wait_ge(ev("rows_ready"), step.times(1, half * W_STEPS + 1))
                pool.nop(nofuse=True)
                for t in range(WT):
                    pool.tensor_scalar(oh_rows(store)[:, t * P:(t + 1) * P], iota, row_now[:, t:t + 1],
                                       None, ALU.is_equal).then_inc(ev("ohi"), 1)

            onehot_rows(Tile(0, 1, 0), 0, onehot_early, True)
            with pool.Fori(1, W_STEPS) as i:
                onehot_rows(Tile(i, 1, 0), 0, onehot_early)
            if stop < 7:
                return
            pool.wait_ge(piece_used, P_V)
            pool.dma_start(x3[:, :], a["spill"]).then_inc(ev("back_in"), 16)
            with pool.Fori(0, W_STEPS) as i:
                onehot_rows(Tile(i, 1, 0), 1, onehot_late)


def col_tiles(w):
    n = w.shape[1] // P
    return w.reshape(2, HKT, P, n, P).transpose(3, 0, 2, 1, 4).reshape(2 * n, P, PIECE)


def padded(w):
    return np.concatenate([w, np.zeros((w.shape[0], P - w.shape[1]), w.dtype)], axis=1)


def columns(x):
    return x.reshape(-1, P).T


def lay_out(x, attn_norm, w_in, gate_bias, nsa_cmp_pos, nsa_cmp_w1, nsa_cmp_b1, nsa_cmp_w2, ssm_conv_w, ssm_conv_b,
            ssm_dt_bias, ssm_a_log, ssm_d, ssm_norm, w_branch_nsa, w_branch_ssm, w_out, ffn_norm, peer_w_q,
            peer_sub_keys, peer_u, peer_v, final_norm):
    w = w_in[0]
    at = np.cumsum([0, HEADS * HD, 6 * GROUPS * HD, 3 * HEADS, D, XBC_T * P, SH, 2 * D])
    q, kv, gate, z, xbc, dt, merge = (w[:, at[n]:at[n + 1]] for n in range(7))
    branch = lambda b, c: kv[:, (b * 2 + c) * GROUPS * HD:(b * 2 + c + 1) * GROUPS * HD]
    w_in_t = np.concatenate([q, branch(1, 1), branch(2, 1), padded(gate), padded(dt),
                             branch(1, 0), branch(2, 0), branch(0, 0), branch(0, 1), xbc, z, merge], axis=1)
    keep, phase = shape_constants()
    u = peer_u[0].reshape(NKEY, NKEY, 2, HKT, P)
    v = peer_v[0].reshape(NKEY, 2, JH, 2, PIECE)
    cw = ssm_conv_w[0].reshape(CONV, XBC_T, P)
    par = np.concatenate([
        columns(final_norm), columns(attn_norm[0]), columns(ssm_norm[0]), columns(gate_bias[0]),
        cw.transpose(2, 1, 0).reshape(P, XBC_T * CONV), columns(ffn_norm[0]),
        columns(ssm_conv_b[0]), nsa_cmp_b1[0].T, columns(np.repeat(ssm_d[0], SP_)),
        nsa_cmp_pos[0].transpose(2, 0, 1).reshape(P, 2 * CB),
        np.tile(ssm_dt_bias[0], (P, 1)), np.tile(ssm_a_log[0], (P, 1))], axis=1)
    assert par.shape[1] == V_END
    cmp_w = np.concatenate([nsa_cmp_w1[0].reshape(2, CB, P, P).transpose(2, 0, 1, 3).reshape(P, 2 * CB * P),
                            nsa_cmp_w2[0].transpose(1, 0, 2).reshape(P, 2 * P)], axis=1)
    return {
        "x": x[0].T.reshape(KT, P, S),
        "w_in": col_tiles(w_in_t),
        "w_mix": np.concatenate([col_tiles(m[0]) for m in (w_branch_nsa, w_branch_ssm, w_out, peer_w_q)]),
        "u": u.transpose(1, 2, 4, 3, 0).reshape(2 * NKEY, P, PIECE),
        "v": v.transpose(1, 3, 2, 0, 4).reshape(2 * NKEY, P, PIECE),
        "subk": peer_sub_keys[0].transpose(3, 0, 1, 2).reshape(P, 2 * PH * NKEY),
        "cmp_w": cmp_w, "par": par, "const": keep, "phase": phase,
    }


def kernel(**inputs):
    import concourse.bacc as bacc
    from concourse.bass_utils import run_bass_kernel_spmd

    nc = bacc.Bacc("TRN2", target_bir_lowering=False, num_devices=1)
    arrays = {n: np.ascontiguousarray(x) for n, x in lay_out(**{n: np.asarray(x) for n, x in inputs.items()}).items()}
    a = {n: nc.dram_tensor(n, x.shape, F32, kind="ExternalInput").ap() for n, x in arrays.items()}
    a["out"] = nc.dram_tensor("out", (KT, P, S), F32, kind="ExternalOutput").ap()
    a["spill"] = nc.dram_tensor("spill", (P, KT * S), F32, kind="Internal").ap()
    build(nc, a)
    r = run_bass_kernel_spmd(nc, [arrays], core_ids=[0])
    return np.ascontiguousarray(r.results[0]["out"].reshape(D, S).T)[None]
```

```python
from contextlib import ExitStack

import numpy as np

import concourse.bass as bass
from concourse import mybir
from concourse.alu_op_type import AluOpType as ALU

ACT = mybir.ActivationFunctionType
AX = mybir.AxisListType
F32 = mybir.dt.float32
F32R = mybir.dt.float32r
U32 = mybir.dt.uint32
BF16 = mybir.dt.bfloat16
ds = bass.ds

P = 128
D = 2048
KT = D // P
S = 256
TT = S // P
EPS = 1e-6
NEG = -1e30
PIECE = 1024
HKT = KT // 2

HEADS, GROUPS, HD = 16, 4, 128
SCALE = HD ** -0.5
CB, CS = 32, 16
NC = S // CS - CB // CS + 1
ROPE = HD // 4
THETA = 500000.0

SH, SG, SHG, SP_ = 32, 4, 8, 64
CONV = 4
XBC_T, Z_T, MG_T = 24, 16, 32

PH, NKEY = 8, 128

K_T = 4 * GROUPS
V_T = 2 * GROUPS + 2
ATT_T = XBC_T + Z_T + 8
SSD_T = MG_T - 8
T_K, T_VG = 0, K_T
T_Q = T_VG + V_T
T_ATT = T_Q + HEADS
T_SSD = T_ATT + ATT_T
T_BN = T_SSD + SSD_T
T_BS, T_WO, T_WQ = T_BN + KT, T_BN + 2 * KT, T_BN + 3 * KT
T_U = T_BN + 4 * KT
U1_T = 64
G_T = 2
T_U2 = T_U + U1_T + G_T
WT = 8
JH = NKEY // 2
W_STEPS = S // WT
W_TILES, W_TURN = 14, 8
W_AT = [n * 2 * W_TILES // W_TURN for n in range(W_TURN)]
U3_T = NKEY - U1_T - G_T - W_TILES * W_STEPS // W_TURN
T_U3 = T_U + NKEY - U3_T
SWEEP = NKEY // 2 // 8
SWEEP_BANKS = (4, 5, 6, 7), (0, 1, 4, 5), (6, 7, 0, 1), (4, 5, 6, 7)
T_V = T_U + NKEY
P_V = 2 * T_V

KB = 256
A_Q, A_VT, A_GD, A_K, A_VTOK, A_XBC, A_Z, A_MG = (k * KB for k in (0, 16, 24, 32, 48, 56, 80, 96))
A_END = 128 * KB

C_ONES, C_IOTA, C_IDENT, C_TRI = 0, P, 2 * P, 3 * P
C_KEEP = 4 * P
C_ROT, C_COS, C_SIN, C_MASK, C_CB, C_C01 = 0, P, P + S, P + 2 * S, P + 3 * S, P + 3 * S + 2 * NC
C_PHASE = P + 3 * S + 4 * NC

V_ON, V_AN, V_SN, V_GB, V_CW, V_FN, V_CB, V_B1, V_DS, V_POS, V_DTB, V_AL = (
    0, 16, 32, 48, 80, 176, 192, 216, 218, 234, 298, 330)
V_END = 362


def shape_constants():
    keep = np.zeros((P, C_KEEP), np.float32)
    r = np.arange(P)
    keep[:, C_IDENT:C_IDENT + P] = np.eye(P)
    keep[:, C_IOTA:C_IOTA + P] = r[None, :]
    keep[:, C_ONES:C_ONES + P] = 1
    keep[:, C_TRI:C_TRI + P] = r[:, None] <= r[None, :]
    phase = np.zeros((P, C_PHASE), np.float32)
    half = ROPE // 2
    for d in range(half):
        phase[d + half, C_ROT + d] = -1
        phase[d, C_ROT + d + half] = 1
    inv = np.float32(THETA) ** (-np.arange(half, dtype=np.float32) / np.float32(half))
    ang = np.arange(S, dtype=np.float32)[None, :] * inv.astype(np.float32)[:, None]
    phase[:, C_COS:C_COS + S] = 1
    phase[0:half, C_COS:C_COS + S] = phase[half:ROPE, C_COS:C_COS + S] = np.cos(ang)
    phase[0:half, C_SIN:C_SIN + S] = phase[half:ROPE, C_SIN:C_SIN + S] = np.sin(ang)
    phase[:, C_MASK + P:C_MASK + S] = np.where(r[None, :] <= r[:, None], 0, NEG)
    for tt in range(TT):
        ok = np.arange(NC)[None, :] * CS + CB - 1 <= (r + tt * P)[:, None]
        phase[:, C_CB + tt * NC:C_CB + (tt + 1) * NC] = np.where(ok, 0, NEG)
        phase[:, C_C01 + tt * NC:C_C01 + (tt + 1) * NC] = ok
    return keep, phase


class Tile:

    def __init__(self, i, k, c):
        self.i, self.k, self.c = i, k, c

    def times(self, m, a=0):
        return self.i * (self.k * m) + (self.c * m + a)

    def half(self, a=0):
        return self.i * (self.k // 2) + (self.c // 2 + a)

    def __add__(self, n):
        return Tile(self.i, self.k, self.c + n)


def wait(eng, sem, value):
    if not isinstance(value, int) or value > 0:
        eng.wait_ge(sem, value)


class Steps:

    def __init__(self, eng, sem):
        self.eng, self.sem, self.base, self.n, self.at = eng, sem, 0, 0, 0

    def mark(self, ins):
        self.n += 1
        ins.then_inc(self.sem, 1)

    def wait(self):
        self.eng.wait_ge(self.sem, self.base + self.n)

    def __call__(self, ins):
        self.mark(ins)
        self.wait()

    def apart(self, ins):
        self(ins)
        self.eng.nop(nofuse=True)

    def turns(self, first, end, per, body):
        start = self.n
        with self.eng.Fori(first, end) as i:
            self.base, self.n = i * per + (start - first * per), 0
            body(i)
            assert self.n == per, (self.n, per)
        self.base, self.n = 0, start + (end - first) * per


def build(nc, a):
    with ExitStack() as ctx:
        def sb(name, shape, dt=F32, stack=ctx):
            return stack.enter_context(nc.sbuf_tensor(name, shape, dt))

        def sem(name):
            return ctx.enter_context(nc.semaphore(name))

        with ExitStack() as early:
            act1_hi = sb("act1_hi", [P, KT * S], F32R, early)
            act1_lo = sb("act1_lo", [P, KT * S], F32R, early)
        arena = sb("arena", [P, A_END])
        with ExitStack() as early:
            act0_hi = sb("act0_hi", [P, KT * S], F32R, early)
            act0_lo = sb("act0_lo", [P, KT * S], F32R, early)
        onehot_late = sb("onehot_late", [P, 16 * KB], BF16)
        av_hi = sb("av_hi", [P, 4 * S], F32R)
        av_lo = sb("av_lo", [P, 4 * S], F32R)
        x3 = sb("x3", [P, KT * S])
        raw = sb("raw", [P, 4 * PIECE])
        w_hi = sb("w_hi", [P, 4 * PIECE], F32R)
        w_lo = sb("w_lo", [P, 2 * PIECE], F32R)
        kept = sb("kept", [P, C_KEEP + V_END])
        const, par = kept[:, 0:C_KEEP], kept[:, C_KEEP:C_KEEP + V_END]
        r2 = par[:, V_AN:V_AN + S]
        zeros = par[:, V_AN + S:V_AN + S + P // 2].bitcast(BF16)
        gate_rest = kept[:, C_IDENT:C_IDENT + S]
        small = sb("small", [P, 872])

        bank = [ctx.enter_context(nc.psum_tensor(f"bank{i}", [P, 512], F32)) for i in range(8)]

        def ar(at, n):
            return arena[:, at:at + n]

        onehot_early = arena[:, A_END - U3_T * KB:A_END].bitcast(BF16)
        rows_i = small[:, 0:S]
        cols_j, iota_j = small[:, S:S + P].bitcast(BF16), small[:, S + P:S + P + JH].bitcast(BF16)
        gate_part = [small[:, 448 + k * P:448 + (k + 1) * P].bitcast(BF16) for k in range(3)]
        row_now = small[:, 840:840 + WT]

        def oh_rows(store):
            return store[:, 0:WT * P]

        def oh_cols(store, part):
            return store[:, WT * P + part * WT * JH:WT * P + (part + 1) * WT * JH]

        def over_j(x, step):
            return x[:, ds(step.times(WT), WT)].unsqueeze(2).broadcast_to([P, WT, JH])

        ident, iota, ones, tri = (const[:, k:k + P] for k in (C_IDENT, C_IOTA, C_ONES, C_TRI))
        phase_at = A_MG + 28 * KB
        rot = ar(phase_at + C_ROT, P)
        cos_t, sin_t = ar(phase_at + C_COS, S), ar(phase_at + C_SIN, S)
        mask_t = ar(phase_at + C_MASK, S)
        cmp_bias = ar(phase_at + C_CB, 2 * NC)
        cmp_01 = ar(phase_at + C_C01, 2 * NC)

        raw_landed = [sem(f"raw_landed{k}") for k in range(4)]
        hi_ready, lo_ready = sem("hi_ready"), sem("lo_ready")
        piece_used, tile_evicted = sem("piece_used"), sem("tile_evicted")
        v_step, a_step, p_step = sem("v_step"), sem("a_step"), sem("p_step")
        par_in, w1_in, phase_in = sem("par_in"), sem("w1_in"), sem("phase_in")
        x_in = [sem(f"x_in{c}") for c in range(4)]
        E = {}

        def ev(name):
            if name not in E:
                E[name] = sem(name)
            return E[name]

        for name in ("sq_ready", "sq_added", "sum_ready", "var_ready", "root_ready", "h_ready", "h_hi",
                     "h_split", "krot", "krope", "v_turned", "v_kept", "g_turned", "g_kept", "hid_sum",
                     "rows_placed", "hid_ready", "cmp_out", "cmp_kept", "q_rot", "q_roped", "scores", "scored",
                     "exps", "probs", "p_turned", "p_kept_a", "p_kept_b", "pv", "o_hi", "o_lo", "v_staged",
                     "conv_done", "silu_done", "z_done", "dt_in", "dt_exp", "dta_ready", "acs_sum", "acs_kept",
                     "dte_in", "dte_ready", "dtdte_ready", "x_staged", "x_turned", "b_turned", "b_kept",
                     "xdt_ready", "dtatri", "acsb", "seg_ready", "seg_exp", "m_ready", "c_exp", "c_ready",
                     "state", "state_kept", "y_sum", "g_ready", "gsq_ready", "gsum", "gsum_kept", "gvar",
                     "groot", "gn_ready", "gn_hi", "g_split", "gate_ready", "merged", "merged_hi", "merged_lo",
                     "res_in", "x2_ready", "x2g_hi", "x2g_lo", "sumsq", "x2sum", "x2var", "x2root", "spilled",
                     "subk_in", "s_sum", "s_kept", "gate_in", "gate_exp", "gate_done", "i_turned", "i_kept",
                     "g_done", "rows_ready", "ohi", "gj", "w_sum", "w_used", "v_zero", "av_hi_r", "av_lo_r",
                     "back_in", "sweep", "sweep_used", "last_kept", "fsq", "fadd", "fsum", "fvar", "froot",
                     "out_ready", "stored"):
            ev(name)

        def expert_col(s, i, m):
            return arena[:, ds(i * 8 * S + (m - 8 * SWEEP * (s - s // 2)) * S, S)]

        block = ctx.enter_context(nc.Block())

        def piece_ap(ring, slot):
            return ring[:, slot * PIECE:(slot + 1) * PIECE]

        @block.sync
        def _(sp):
            def load(src, n_before, i, k, m):
                slot = m % 4
                wait(sp, lo_ready, i * k + (n_before + m - 3))
                sp.dma_start(piece_ap(raw, slot), src[ds(i * k + m, 1)].rearrange("a p n -> (a p) n"))\
                  .then_inc(raw_landed[slot], 16)

            for c in range(4):
                sp.dma_start(ar(A_MG + c * PIECE, PIECE).rearrange("p (k t) -> p k t", k=4),
                             a["x"][4 * c:4 * c + 4].rearrange("k p t -> p k t")).then_inc(x_in[c], 16)
            before = 0
            for name, n in (("w_in", 2 * T_BN), ("w_mix", 8 * KT), ("u", 2 * NKEY), ("v", 2 * NKEY)):
                first = 0
                if before == 0:
                    for m in range(4):
                        load(a[name], 0, 0, 4, m)
                    first = 1
                with sp.Fori(first, n // 4) as i:
                    for m in range(4):
                        load(a[name], before, i, 4, m)
                before += n
            for c in range(4):
                sp.wait_ge(ev("out_ready"), 4 * c + 4)
                sp.dma_start(a["out"][4 * c:4 * c + 4].rearrange("k p t -> p k t"),
                             x3[:, c * PIECE:(c + 1) * PIECE].rearrange("p (k t) -> p k t", k=4))\
                  .then_inc(ev("stored"), 16)
            sp.wait_ge(ev("stored"), 64)

        @block.tensor
        def _(pe):
            def half_tile(T, h, out, hi_rhs, lo_rhs, made=()):
                slot = (T.c % 2) * 2 + h
                hi, lo = piece_ap(w_hi, slot), piece_ap(w_lo, slot % 2)
                pe.wait_ge(hi_ready, T.times(2, h + 1))
                for n, (w, x) in enumerate(((hi, hi_rhs), (hi, lo_rhs), (lo, hi_rhs))):
                    if n == 2:
                        pe.wait_ge(lo_ready, T.times(2, h + 1))
                    elif made:
                        pe.wait_ge(made[n], 2 * h + 2)
                    for k in range(HKT):
                        kt = h * HKT + k
                        mm = pe.matmul(out, w[:, k * P:(k + 1) * P], x[:, kt * S:(kt + 1) * S],
                                       start=(h == 0 and n == 0 and k == 0), stop=(h == 1 and n == 2 and k == HKT - 1))
                mm.then_inc(piece_used, 1)

            def tile(T, hi_rhs, lo_rhs):
                wait(pe, tile_evicted, T.times(1, -1))
                for h in range(2):
                    half_tile(T, h, bank[T.c % 2][:, 0:S], hi_rhs, lo_rhs)

            def stage(T0, n, hi_rhs, lo_rhs, done=0):
                per = 4 if n % 4 == 0 else 2
                start = -(-done // per)
                for m in range(done, start * per):
                    tile(Tile(0, 2, T0 + m), hi_rhs, lo_rhs)
                with pe.Fori(start, n // per) as i:
                    for m in range(per):
                        tile(Tile(i, per, T0 + m), hi_rhs, lo_rhs)

            pe.wait_ge(par_in, 32)
            for c in range(4):
                pe.wait_ge(ev("sq_added"), c + 1)
                mm = pe.matmul(bank[2][:, 0:S], ones, ar(A_K + (4 + c) * S, S), start=(c == 0), stop=(c == 3))
            mm.then_inc(ev("sum_ready"), 1)
            for h in range(2):
                half_tile(Tile(0, 2, T_K), h, bank[0][:, 0:S], act0_hi, act0_lo, (ev("h_hi"), ev("h_split")))
            tile(Tile(0, 2, T_K + 1), act0_hi, act0_lo)
            stage(T_K, K_T, act0_hi, act0_lo, done=2)
            stage(T_VG, V_T, act0_hi, act0_lo)

            def rotate(numbers):
                for n in numbers:
                    if n >= 4:
                        pe.wait_ge(ev("krope"), n - 3)
                    pe.matmul(bank[2 + n % 4][:, :], rot, ar(A_K + n * 512, 512), start=True, stop=True)\
                      .then_inc(ev("krot"), 1)

            def turn_gates():
                for n in range(4):
                    src = ar(A_GD + (n // 2) * S + (n % 2) * P, P)
                    mm = pe.transpose(bank[6][:, n * P:(n + 1) * P], src, ident)
                mm.then_inc(ev("g_turned"), 1)

            def turn_v(numbers):
                for n in numbers:
                    for g in range(GROUPS):
                        b, tt = n // 2, n % 2
                        mm = pe.transpose(bank[2 + n][:, g * P:(g + 1) * P],
                                          ar(A_VT + (b * GROUPS + g) * S + tt * P, P), ident)
                    mm.then_inc(ev("v_turned"), 1)

            def compress(c, b):
                pe.wait_ge(ev("rows_placed"), 2 - c)
                w1 = ar(A_XBC + c * CB * P, CB * P)
                for l in range(CB):
                    mm = pe.matmul(bank[b][:, 0:GROUPS * NC], w1[:, l * P:(l + 1) * P],
                                   ar(A_MG + 16 * KB + l * GROUPS * NC, GROUPS * NC), start=(l == 0), stop=(l == CB - 1))
                mm.then_inc(ev("hid_sum"), 1)

            for m in range(HEADS):
                tile(Tile(0, 2, T_Q + m), act0_hi, act0_lo)
                if m == 0:
                    pe.wait_ge(phase_in, 16)
                    rotate(range(4))
                if m == 1:
                    turn_gates()
                if m == 2:
                    pe.wait_ge(w1_in, 64)
                    compress(1, 7)
                if m == 4:
                    rotate(range(4, 6))
                if m == 5:
                    pe.wait_ge(ev("krope"), 4)
                    turn_v((2, 3))
                if m == 7:
                    pe.wait_ge(ev("krope"), 6)
                    turn_v((0, 1))
                if m == 8:
                    pe.wait_ge(ev("v_kept"), 2)
                    compress(0, 5)
                if m == 11:
                    pe.wait_ge(ev("dta_ready"), 1)
                    pe.wait_ge(ev("v_kept"), 4)
                    dta = small[:, 96 + 64:96 + 128]
                    pe.matmul(bank[2][:, 0:64], tri, dta, start=True, stop=True)
                    pe.matmul(bank[2][:, 64:96], ones, dta[:, 0:32], start=True, stop=True)\
                      .then_inc(ev("acs_sum"), 1)
                if m == 12:
                    pe.wait_ge(ev("hid_ready"), 2)
                    pe.wait_ge(ev("g_kept"), 3)
                    w2 = ar(A_XBC + 2 * CB * P, 2 * P)
                    hid = [ar(A_MG + 26 * KB + c * 64, GROUPS * NC) for c in range(2)]
                    pe.matmul(bank[7][:, 0:GROUPS * NC], w2[:, 0:P], hid[0], start=True, stop=True)
                    for g in range(GROUPS):
                        mm = pe.matmul(bank[6][0:NC, g * P:(g + 1) * P], hid[1][:, g * NC:(g + 1) * NC],
                                       w2[:, P:2 * P], start=True, stop=True)
                    mm.then_inc(ev("cmp_out"), 1)

            pe.wait_ge(ev("cmp_kept"), 2)
            pe.wait_ge(ev("dte_in"), 1)
            starts = (0, 2, 5, 7)

            def attention_turn(i, first):
                def n_of(hh):
                    return i * 4 + hh

                def q_rot(hh):
                    if not (first and hh == 0):
                        pe.wait_ge(ev("scored"), n_of(hh))
                    pe.matmul(bank[2][:, 0:S], rot, arena[:, ds(i * 4 * S + hh * S, S)], start=True, stop=True)\
                      .then_inc(ev("q_rot"), 1)

                def scores(hh):
                    pe.wait_ge(ev("q_roped"), n_of(hh) + 1)
                    q = ar(A_MG + 20 * KB + (hh % 2) * S, S)
                    for tt in range(TT):
                        w = P * (tt + 1)
                        for b in range(2):
                            pe.matmul(bank[3 + tt][:, b * w:(b + 1) * w], q[:, tt * P:(tt + 1) * P],
                                      arena[:, ds(A_K + b * 4 * S + i * S, w)], start=True, stop=True)
                    for tt in range(TT):
                        mm = pe.matmul(bank[2][:, tt * NC:(tt + 1) * NC], q[:, tt * P:(tt + 1) * P],
                                       kc_group(i), start=True, stop=True)
                    mm.then_inc(ev("scores"), 1)

                def turn_p(hh):
                    pe.wait_ge(ev("probs"), n_of(hh) + 1)
                    if not (first and hh == 0):
                        pe.wait_ge(ev("p_kept_a"), n_of(hh))
                        pe.wait_ge(ev("p_kept_b"), n_of(hh))
                    pr = ar(A_MG + 8 * KB + (hh % 2) * 800, 798)
                    for b in range(2):
                        pe.transpose(bank[5][:, b * S:b * S + P], pr[:, b * P:(b + 1) * P], ident)
                        pe.transpose(bank[5][:, b * S + P:(b + 1) * S], pr[:, S + b * S:S + b * S + P], ident)
                    for b in range(2):
                        pe.transpose(bank[6][:, b * P:(b + 1) * P], pr[:, S + b * S + P:S + (b + 1) * S], ident)
                    for tt in range(TT):
                        mm = pe.transpose(bank[6][0:NC, S + tt * P:S + (tt + 1) * P],
                                          pr[:, 3 * S + tt * NC:3 * S + (tt + 1) * NC], ident)
                    mm.then_inc(ev("p_turned"), 1)

                def pv(hh):
                    pe.wait_ge(ev("p_kept_a"), n_of(hh) + 1)
                    pe.wait_ge(ev("p_kept_b"), n_of(hh) + 1)
                    pe.wait_ge(ev("v_staged"), i + 1)
                    if not (first and hh == 0):
                        pe.wait_ge(ev("o_lo"), n_of(hh))
                    pt = ar(A_MG + 16 * KB, 4 * S)
                    vs, vcs = ar(A_MG + 23 * KB, 4 * P), ar(A_MG + 25 * KB, P)
                    o = bank[7]
                    pe.matmul(o[:, 0:S], vs[:, 0:P], pt[:, 0:S], start=True, stop=False)
                    pe.matmul(o[:, 0:S], vs[:, 2 * P:3 * P], pt[:, S:2 * S], start=False, stop=False)
                    pe.matmul(o[:, 0:S], vcs[0:NC, :], pt[0:NC, 3 * S:4 * S], start=False, stop=False)
                    pe.matmul(o[:, P:S], vs[:, P:2 * P], pt[:, 2 * S:2 * S + P], start=False, stop=False)
                    pe.matmul(o[:, P:S], vs[:, 3 * P:4 * P], pt[:, 2 * S + P:3 * S], start=False, stop=True)\
                      .then_inc(ev("pv"), 1)

                for m in range(12):
                    if m in starts:
                        q_rot(starts.index(m))
                    tile(Tile(i, 12, T_ATT + m), act0_hi, act0_lo)
                    if m in starts:
                        scores(starts.index(m))
                    if m - 2 in starts:
                        turn_p(starts.index(m - 2))
                    if m - 3 in starts:
                        pv(starts.index(m - 3))

            def kc_group(i):
                return arena[:, ds(A_MG + 26 * KB + 128 + i * NC, NC)]

            attention_turn(0, True)
            with pe.Fori(1, GROUPS) as i:
                attention_turn(i, False)

            pe.wait_ge(ev("o_lo"), HEADS)
            pe.wait_ge(ev("dtdte_ready"), 1)

            xs_stage = ar(A_K, 4 * S)
            b_stage, c_stage = ar(A_K + 4 * KB, S), ar(A_K + 5 * KB, S)
            ebuf = [ar(A_K + (6 + 4 * c) * KB, PIECE) for c in range(2)]
            cs_buf = ar(A_K + 14 * KB, PIECE)
            xdt = [ar(A_K + (18 + 2 * c) * KB, 512) for c in range(2)]
            xde = ar(A_K + 22 * KB, 512)
            btok = small[:, 700:828]

            def ssd_turn(i, first):
                T = Tile(i, 6, T_SSD)
                pe.wait_ge(ev("x_staged"), i + 1)
                if not first:
                    pe.wait_ge(ev("g_ready"), i)
                for c in range(2):
                    for t in range(4):
                        mm = pe.transpose(bank[2 + c][:, t * P:(t + 1) * P],
                                          xs_stage[:, t * S + c * P:t * S + (c + 1) * P], ident)
                mm.then_inc(ev("x_turned"), 1)
                pe.transpose(bank[6][:, 0:P], b_stage[:, 0:P], ident)
                for c in range(2):
                    mm = pe.matmul(bank[6][:, (1 + c) * P:(2 + c) * P], b_stage[:, c * P:(c + 1) * P],
                                   c_stage[:, c * P:(c + 1) * P], start=True, stop=True)
                mm.then_inc(ev("b_turned"), 1)
                tile(T, act0_hi, act0_lo)
                for c in range(2):
                    pe.wait_ge(ev("dtatri"), i * 2 + (c + 1))
                    if c == 1:
                        pe.wait_ge(ev("seg_ready"), i * 2 + 1)
                    for n in range(2):
                        mm = pe.matmul(bank[4 + n][:, :], ones, ebuf[c][:, n * 512:(n + 1) * 512],
                                       start=True, stop=True)
                    mm.then_inc(ev("acsb"), 1)
                    tile(T + (1 + c), act0_hi, act0_lo)
                pe.wait_ge(ev("xdt_ready"), i + 1)
                pe.wait_ge(ev("b_kept"), i + 1)
                if not first:
                    pe.wait_ge(ev("gsum_kept"), i)
                pe.matmul(bank[7][:, :], btok, xde, start=True, stop=True).then_inc(ev("state"), 1)
                tile(T + 3, act0_hi, act0_lo)
                pe.wait_ge(ev("m_ready"), i * 2 + 2)
                pe.wait_ge(ev("c_ready"), i + 1)
                pe.wait_ge(ev("state_kept"), i + 1)
                for t in range(4):
                    b, at = bank[2 + t // 2], (t % 2) * S
                    for r in (2 * t, 2 * t + 1):
                        rows = slice((r % 2) * SP_, (r % 2 + 1) * SP_)
                        head = slice(r * SP_, (r + 1) * SP_)
                        pe.matmul(b[rows, at:at + P], xdt[0][:, head], ebuf[0][:, r * P:(r + 1) * P],
                                  start=True, stop=True)
                        pe.matmul(b[rows, at + P:at + S], xdt[1][:, head], ebuf[1][:, r * P:(r + 1) * P],
                                  start=True, stop=False)
                        mm = pe.matmul(b[rows, at + P:at + S], xde[:, head], cs_buf[:, r * P:(r + 1) * P],
                                       start=False, stop=True)
                mm.then_inc(ev("y_sum"), 1)
                tile(T + 4, act0_hi, act0_lo)
                pe.wait_ge(ev("gsq_ready"), i + 1)
                for t in range(4):
                    mm = pe.matmul(bank[7][:, 0:S], ones, cs_buf[:, t * S:(t + 1) * S], start=(t == 0), stop=(t == 3))
                mm.then_inc(ev("gsum"), 1)
                tile(T + 5, act0_hi, act0_lo)

            ssd_turn(0, True)
            with pe.Fori(1, SG) as i:
                ssd_turn(i, False)

            def joined_stage(T0, hi_rhs, lo_rhs, made, n, between=None):
                pe.wait_ge(tile_evicted, T0 - 1)
                for h in range(2):
                    pe.wait_ge(made, n * (h + 1) // 2)
                    half_tile(Tile(0, 2, T0), h, bank[0][:, 0:S], hi_rhs, lo_rhs)
                if between:
                    between()
                tile(Tile(0, 2, T0 + 1), hi_rhs, lo_rhs)
                stage(T0, KT, hi_rhs, lo_rhs, done=2)

            def residual_sum():
                pe.wait_ge(ev("sumsq"), KT)
                pe.matmul(bank[2][:, 0:S], ones, ar(A_XBC + 16 * KB, S), start=True, stop=True)\
                  .then_inc(ev("x2sum"), 1)

            stage(T_BN, KT, act1_hi, act1_lo)
            joined_stage(T_BS, act0_hi, act0_lo, ev("g_split"), 4)
            joined_stage(T_WO, act1_hi, act1_lo, ev("merged_lo"), KT)
            joined_stage(T_WQ, act0_hi, act0_lo, ev("x2g_lo"), KT, residual_sum)

            for m in range(2):
                tile(Tile(0, 2, T_U + m), act0_hi, act0_lo)
            pe.wait_ge(tile_evicted, T_U)
            pe.wait_ge(ev("subk_in"), 16)
            qp, subk = ar(A_MG + 16 * KB, KT * S), ar(A_MG, 8 * KB)
            for n in range(8):
                if n >= 4:
                    pe.wait_ge(ev("s_kept"), n - 3)
                for m in range(4):
                    tt, hc = n // 4, (n % 4) * 4 + m
                    mm = pe.matmul(bank[4 + n % 4][:, m * P:(m + 1) * P], qp[:, hc * S + tt * P:hc * S + (tt + 1) * P],
                                   subk[:, hc * P:(hc + 1) * P], start=True, stop=True)
                mm.then_inc(ev("s_sum"), 1)
            stage(T_U, U1_T, act0_hi, act0_lo, done=2)
            for m in range(G_T):
                tile(Tile(0, 2, T_U + U1_T + m), act0_hi, act0_lo)
            pe.wait_ge(ev("gate_done"), 1)
            res = ar(A_Z - 3 * KB, 3 * S)
            for n in range(3):
                for tt in range(TT):
                    mm = pe.transpose(bank[2 + n][:, tt * P:(tt + 1) * P],
                                      res[:, n * S + tt * P:n * S + (tt + 1) * P], ident)
                mm.then_inc(ev("i_turned"), 1)

            def w_step(step, store, first=False):
                n = step.c % 2
                if not first:
                    pe.wait_ge(ev("w_used"), step.times(1, -1))
                pe.wait_ge(ev("ohi"), step.times(WT, WT))
                pe.wait_ge(ev("gj"), step.times(1, 1))
                rows = oh_rows(store)
                for t in range(WT):
                    for part in range(1, 4):
                        mm = pe.matmul(bank[2 + n][:, t * JH:(t + 1) * JH], rows[:, t * P:(t + 1) * P],
                                       oh_cols(store, part)[:, t * JH:(t + 1) * JH], start=part == 1, stop=part == 3)
                mm.then_inc(ev("w_sum"), 1)

            def u2_turn(i, first):
                for m in range(W_TILES):
                    T = Tile(i, W_TILES, T_U2 + m)
                    wait(pe, tile_evicted, T.times(1, -1))
                    for h in range(2):
                        half_tile(T, h, bank[T.c % 2][:, 0:S], act0_hi, act0_lo)
                        if 2 * m + h - 2 in W_AT:
                            n = W_AT.index(2 * m + h - 2)
                            w_step(Tile(i, W_TURN, n), onehot_early, first and n < 2)

            u2_turn(0, True)
            with pe.Fori(1, W_STEPS // W_TURN) as i:
                u2_turn(i, False)
            stage(T_U3, U3_T, act0_hi, act0_lo)

            pe.wait_ge(ev("v_zero"), 1)

            def v_piece(i, m, banks, between=None):
                slot = m % 4
                hi, lo = piece_ap(w_hi, slot), piece_ap(w_lo, slot % 2)
                ah, al = av_hi[:, slot * S:(slot + 1) * S], av_lo[:, slot * S:(slot + 1) * S]
                pe.wait_ge(hi_ready, i * 8 + (P_V + m + 1))
                pe.wait_ge(ev("av_hi_r"), i * 8 + (m + 1))
                parts = (range(HKT),) if between is None else (range(HKT // 2), range(HKT // 2, HKT))
                for part, row_tiles in enumerate(parts):
                    if part == 1:
                        between()
                    for n, (w, x) in enumerate(((hi, ah), (hi, al), (lo, ah))):
                        if n == 1 and part == 0:
                            pe.wait_ge(ev("av_lo_r"), i * 8 + (m + 1))
                        if n == 2 and part == 0:
                            pe.wait_ge(lo_ready, i * 8 + (P_V + m + 1))
                        for k in row_tiles:
                            mm = pe.matmul(bank[banks[k // 2]][:, (k % 2) * S:(k % 2 + 1) * S],
                                           w[:, k * P:(k + 1) * P], x, start=False, stop=False, skip_group_check=True)
                mm.then_inc(piece_used, 1)

            def rim(banks, start):
                for b in banks:
                    mm = pe.matmul(bank[b][:, :], zeros, const[:, 0:S].bitcast(BF16), start=start, stop=not start,
                                   skip_group_check=True)
                return mm

            def v_turn(s, i, first):
                banks = SWEEP_BANKS[s]

                def second_half():
                    if s > 0:
                        pe.wait_ge(ev("sweep_used"), 4 * s - 2)
                    rim(banks[2:], True)

                for m in range(8):
                    v_piece(i, m, banks, second_half if first and m == 0 else None)
                    if s < 2 and m % 4 == 2:
                        w_step(Tile(i, 2, W_STEPS + m // 4), onehot_late)

            pe.wait_ge(tile_evicted, T_V)
            for s in range(4):
                if s > 1:
                    pe.wait_ge(ev("sweep_used"), 4 * s - 4)
                rim(SWEEP_BANKS[s][:2], True)
                v_turn(s, s * SWEEP, True)
                with pe.Fori(s * SWEEP + 1, (s + 1) * SWEEP) as i:
                    v_turn(s, i, False)
                rim(SWEEP_BANKS[s], False).then_inc(ev("sweep"), 1)
            pe.wait_ge(ev("fadd"), 1)
            pe.matmul(bank[2][:, 0:S], ones, ar(A_XBC + 4 * S, S), start=True, stop=False)
            for k in range(8, KT):
                pe.wait_ge(ev("fsq"), k // 2 - 3)
                mm = pe.matmul(bank[2][:, 0:S], ones, ar(k * S, S), start=False, stop=(k == KT - 1))
            mm.then_inc(ev("fsum"), 1)

        @block.scalar
        def _(act):
            st = Steps(act, a_step)
            act.dma_start(const, a["const"]).then_inc(par_in, 16)
            act.dma_start(par, a["par"]).then_inc(par_in, 16)

            def hi(T, h):
                slot = (T.c % 2) * 2 + h
                act.wait_ge(raw_landed[slot], T.half(1) * 16)
                wait(act, piece_used, T.times(2, h - 3))
                act.activation(piece_ap(w_hi, slot), piece_ap(raw, slot), ACT.Copy).then_inc(hi_ready, 1)

            def pair(T):
                hi(T, 0)
                hi(T, 1)

            def stage(T0, n, evict, per=2, beside=None, begun=False, goes_on=False):
                def turn(i, first):
                    for m in range(per):
                        if not (first and m == 0 and begun):
                            pair(Tile(i, per, T0 + m))
                        if beside:
                            beside(i, m, first)
                        if not (first and m == 0):
                            evict(Tile(i, per, m - 1))
                turn(0, True)
                with act.Fori(1, n // per) as i:
                    turn(i, False)
                if goes_on:
                    pair(Tile(0, per, T0 + n))
                evict(Tile(0, per, n - 1))

            def nothing(T):
                pass

            def keep_in(at, T0):
                def evict(T):
                    act.wait_ge(piece_used, T.times(2, 2 * T0 + 2))
                    act.activation(arena[:, ds(T.times(S, at), S)], bank[T.c % 2 ^ T0 % 2][:, 0:S], ACT.Copy)\
                       .then_inc(tile_evicted, 1)
                return evict

            for c in range(4):
                act.wait_ge(x_in[c], 16)
                act.activation(ar(c * PIECE, PIECE), ar(A_MG + c * PIECE, PIECE), ACT.Square).then_inc(ev("sq_ready"), 1)
            pair(Tile(0, 2, T_K))
            act.wait_ge(ev("var_ready"), 1)
            act.activation(ar(A_K + S, S), ar(A_K, S), ACT.Sqrt).then_inc(ev("root_ready"), 1)
            for c in range(4):
                act.wait_ge(ev("h_ready"), c + 1)
                act.activation(act0_hi[:, c * PIECE:(c + 1) * PIECE], ar(A_MG + (16 + 4 * (c % 2)) * KB, PIECE), ACT.Copy)\
                   .then_inc(ev("h_hi"), 1)
            stage(T_K, K_T, keep_in(A_K, T_K), begun=True)
            stage(T_VG, V_T, keep_in(A_VT, T_VG))

            tmp = ar(A_MG + 12 * KB, 64 * 12)

            def keep_gates():
                act.wait_ge(ev("g_turned"), 1)
                gsig = small[:, 0:96].rearrange("p (h s) -> p h s", s=6)
                for tt in range(TT):
                    src = bank[6][:, tt * P:tt * P + 3 * HEADS].rearrange("p (h b) -> p h b", b=3)
                    act.activation(gsig[:, :, 4 + tt:5 + tt], src[:, :, 0:1], ACT.Sigmoid)
                    act.activation(gsig[:, :, 2 * tt:2 * tt + 2], src[:, :, 1:3], ACT.Sigmoid).then_inc(ev("g_kept"), 1)

            def keep_v(numbers, count):
                for n in numbers:
                    act.wait_ge(ev("v_turned"), count + 1)
                    count += 1
                    act.activation(ar(A_VTOK + n * 512, 512), bank[2 + n][:, :], ACT.Copy).then_inc(ev("v_kept"), 1)

            q_keep = keep_in(A_Q, T_Q)
            for m in range(HEADS):
                pair(Tile(0, 2, T_Q + m))
                if m > 0:
                    q_keep(Tile(0, 2, m - 1))
                if m == 3:
                    keep_gates()
                if m == 6:
                    keep_v((2, 3), 0)
                if m == 8:
                    keep_v((0, 1), 2)
                    act.wait_ge(ev("dt_in"), 1)
                    act.activation(tmp[:, 64:128], tmp[:, 0:64], ACT.Exp, scale=-1.0).then_inc(ev("dt_exp"), 1)
                    act.activation(tmp[:, 128:160], par[:, V_AL:V_AL + 32], ACT.Exp).then_inc(ev("dt_exp"), 1)
                if m == 11:
                    for c in (1, 0):
                        act.wait_ge(ev("hid_sum"), 2 - c)
                        act.activation(ar(A_MG + 26 * KB + c * 64, GROUPS * NC), bank[7 - 2 * (1 - c)][:, 0:GROUPS * NC],
                                       ACT.Gelu, bias=par[:, V_B1 + c:V_B1 + c + 1]).then_inc(ev("hid_ready"), 1)
                if m == 13:
                    act.wait_ge(ev("cmp_out"), 1)
                    act.activation(ar(A_MG + 26 * KB + 128, GROUPS * NC), bank[7][:, 0:GROUPS * NC], ACT.Copy)\
                       .then_inc(ev("cmp_kept"), 1)
                    act.activation(arena[0:NC, A_K + 12 * KB:A_K + 14 * KB], bank[6][0:NC, :], ACT.Copy)\
                       .then_inc(ev("cmp_kept"), 1)
                    act.wait_ge(ev("dte_in"), 1)
                    act.activation(small[:, 328:360], small[:, 328:360], ACT.Exp).then_inc(ev("dte_ready"), 1)
            q_keep(Tile(0, 2, HEADS - 1))

            starts = (0, 2, 5, 7)
            att_keep = keep_in(A_XBC, T_ATT)

            def attention_turn(i, first):
                def n_of(hh):
                    return i * 4 + hh

                def exps(hh):
                    act.wait_ge(ev("scored"), n_of(hh) + 1)
                    pr = ar(A_MG + 8 * KB + (hh % 2) * 800, 798)
                    nm, sm = small[:, 360 + (hh % 2) * 24:366 + (hh % 2) * 24], small[:, 366 + (hh % 2) * 24:372 + (hh % 2) * 24]
                    cuts = [(b * P, P) for b in range(2)] + [(S + b * S, S) for b in range(2)] + \
                           [(3 * S + tt * NC, NC) for tt in range(TT)]
                    for n, (at, w) in enumerate(cuts):
                        act.activation(pr[:, at:at + w], pr[:, at:at + w], ACT.Exp, bias=nm[:, n:n + 1],
                                              accum_out=sm[:, n:n + 1]).then_inc(ev("exps"), 1)

                def keep_pt(hh):
                    act.wait_ge(ev("p_turned"), n_of(hh) + 1)
                    if not (first and hh == 0):
                        act.wait_ge(ev("pv"), n_of(hh))
                    act.activation(ar(A_MG + 16 * KB, 2 * S), bank[5][:, :], ACT.Copy).then_inc(ev("p_kept_a"), 1)

                def keep_o(hh):
                    act.wait_ge(ev("pv"), n_of(hh) + 1)
                    act.activation(act1_hi[:, ds(i * 4 * S + hh * S, S)], bank[7][:, 0:S], ACT.Copy)\
                       .then_inc(ev("o_hi"), 1)

                def silu(b):
                    act.wait_ge(ev("conv_done"), i * 2 + (b - 1))
                    act.activation(arena[:, ds(i * 8 * S + (A_XBC + (b * 4 - 8) * S), 4 * S)], ar(A_K + 8 * KB, 4 * S),
                                   ACT.Silu).then_inc(ev("silu_done"), 1)

                for m in range(12):
                    pair(Tile(i, 12, T_ATT + m))
                    if not first and m in (4, 9):
                        silu(m // 5)
                    if m - 2 in starts:
                        exps(starts.index(m - 2))
                    if not (first and m == 0):
                        att_keep(Tile(i, 12, m - 1))
                    if m - 3 in starts:
                        keep_pt(starts.index(m - 3))
                    if m - 4 in starts:
                        keep_o(starts.index(m - 4))

            attention_turn(0, True)
            act.wait_ge(ev("cmp_kept"), 2)
            act.nop().then_inc(ev("silu_done"), 1)
            with act.Fori(1, GROUPS) as i:
                attention_turn(i, False)
            att_keep(Tile(0, 12, ATT_T - 1))

            act.wait_ge(tile_evicted, T_SSD)
            ebuf = [ar(A_K + (6 + 4 * c) * KB, PIECE) for c in range(2)]
            cs_buf = ar(A_K + 14 * KB, PIECE)
            xde = ar(A_K + 22 * KB, 512)
            btok = small[:, 700:828]
            ssd_keep = keep_in(A_MG + 8 * KB, T_SSD)

            def ssd_turn(i, first):
                def evict(m):
                    if not (first and m == 0):
                        ssd_keep(Tile(i, 6, m - 1))
                pair(Tile(i, 6, T_SSD))
                evict(0)
                act.wait_ge(ev("b_turned"), i + 1)
                if not first:
                    act.wait_ge(ev("state"), i)
                act.activation(btok, bank[6][:, 0:P], ACT.Copy).then_inc(ev("b_kept"), 1)
                pair(Tile(i, 6, T_SSD + 1))
                evict(1)
                zt = arena[:, ds(A_Z + i * 4 * S, 4 * S)]
                act.activation(zt, zt, ACT.Silu).then_inc(ev("z_done"), 1)
                pair(Tile(i, 6, T_SSD + 2))
                act.wait_ge(ev("seg_ready"), i * 2 + 1)
                act.activation(ebuf[0], ebuf[0], ACT.Exp).then_inc(ev("seg_exp"), 1)
                evict(2)
                pair(Tile(i, 6, T_SSD + 3))
                act.wait_ge(ev("acsb"), i * 2 + 2)
                act.wait_ge(ev("seg_ready"), i * 2 + 2)
                if not first:
                    act.wait_ge(ev("gsum"), i)
                for n in range(2):
                    act.activation(cs_buf[:, n * 512:(n + 1) * 512], bank[4 + n][:, :], ACT.Exp)\
                       .then_inc(ev("c_exp"), 1)
                act.activation(ebuf[1], ebuf[1], ACT.Exp).then_inc(ev("seg_exp"), 1)
                evict(3)
                act.wait_ge(ev("state"), i + 1)
                act.activation(xde, bank[7][:, :], ACT.Copy).then_inc(ev("state_kept"), 1)
                pair(Tile(i, 6, T_SSD + 4))
                evict(4)
                pair(Tile(i, 6, T_SSD + 5))
                act.wait_ge(ev("g_ready"), i + 1)
                act.nop(nofuse=True)
                act.activation(cs_buf, arena[:, ds(A_Z + i * 4 * S, 4 * S)], ACT.Square).then_inc(ev("gsq_ready"), 1)
                evict(5)

            ssd_turn(0, True)
            with act.Fori(1, SG) as i:
                ssd_turn(i, False)
            ssd_keep(Tile(0, 6, SSD_T - 1))

            def gate0(T):
                act.activation(arena[:, ds(T.times(S, A_MG), S)], arena[:, ds(T.times(S, A_MG), S)], ACT.Sigmoid,
                               bias=par[:, ds(T.times(1, V_GB), 1)]).then_inc(ev("gate_ready"), 1)

            def gate1(T):
                act.activation(arena[:, ds(T.times(S, A_MG + KT * S), S)], arena[:, ds(T.times(S, A_MG + KT * S), S)],
                               ACT.Sigmoid, bias=par[:, ds(T.times(1, V_GB + KT), 1)]).then_inc(ev("gate_ready"), 1)

            def y_norm(i, m, first):
                if m == 1:
                    act.wait_ge(ev("gvar"), i + 1)
                    act.activation(ar(A_K + S, S), ar(A_K, S), ACT.Sqrt).then_inc(ev("groot"), 1)
                if m == 3:
                    act.wait_ge(ev("gn_ready"), i + 1)
                    act.wait_ge(piece_used, 2 * T_BN)
                    act.activation(act0_hi[:, ds(i * PIECE, PIECE)], arena[:, ds(A_Z + i * PIECE, PIECE)], ACT.Copy)\
                       .then_inc(ev("gn_hi"), 1)

            stage(T_BN, KT, gate0, per=4, beside=y_norm, goes_on=True)

            def bs(T):
                gate1(T)
                act.wait_ge(ev("merged"), T.times(1, 1))
                act.activation(act1_hi[:, ds(T.times(S), S)], arena[:, ds(T.times(S, A_MG), S)], ACT.Copy)\
                   .then_inc(ev("merged_hi"), 1)

            stage(T_BS, KT, bs, begun=True, goes_on=True)

            def wo(T):
                act.wait_ge(ev("x2_ready"), T.times(1, 1))
                act.activation(act0_hi[:, ds(T.times(S), S)], arena[:, ds(T.times(S, A_MG), S)], ACT.Copy)\
                   .then_inc(ev("x2g_hi"), 1)

            stage(T_WO, KT, wo, begun=True, goes_on=True)

            def root(i, m, first):
                if first and m == 1:
                    act.wait_ge(ev("x2var"), 1)
                    act.activation(ar(A_XBC + 18 * KB, S), ar(A_XBC + 17 * KB, S), ACT.Sqrt)\
                       .then_inc(ev("x2root"), 1)

            stage(T_WQ, KT, nothing, beside=root, begun=True, goes_on=True)

            s_all = ar(A_Z, KT * S)

            def keep_scores(i, m, first):
                if not (first and m == 1):
                    return
                for n in range(1, 8, 2):
                    act.wait_ge(ev("s_sum"), n + 1)
                    act.wait_ge(ev("s_kept"), n)
                    act.wait_ge(ev("spilled"), 16)
                    act.activation(s_all[:, n * 512:(n + 1) * 512], bank[4 + n % 4][:, :], ACT.Copy)\
                       .then_inc(ev("s_kept"), 1)

            def gelu(T0):
                def evict(T):
                    act.wait_ge(tile_evicted, T.times(1, T_U + T0 + 1))
                    act.activation(arena[:, ds(T.times(S, T0 * S), S)], arena[:, ds(T.times(S, T0 * S), S)], ACT.Gelu)\
                       .then_inc(ev("g_done"), 1)
                return evict

            stage(T_U, U1_T, gelu(0), beside=keep_scores, begun=True)
            gates = ar(A_Z - 3 * KB + 2 * S, S)
            g_gelu, u2_gelu = gelu(U1_T), gelu(U1_T + G_T)
            pair(Tile(0, 2, T_U + U1_T))
            act.wait_ge(ev("gate_in"), 1)
            act.activation(gates, gates, ACT.Exp).then_inc(ev("gate_exp"), 1)
            pair(Tile(0, 2, T_U + U1_T + 1))
            g_gelu(Tile(0, 2, 0))
            pair(Tile(0, 2, T_U2))
            g_gelu(Tile(0, 2, 1))

            def u2_turn(i, first):
                for m in range(W_TILES):
                    if not (first and m == 0):
                        pair(Tile(i, W_TILES, T_U2 + m))
                        u2_gelu(Tile(i, W_TILES, m - 1))

            u2_turn(0, True)
            with act.Fori(1, W_STEPS // W_TURN) as i:
                u2_turn(i, False)
            u2_gelu(Tile(0, 2, NKEY - U1_T - G_T - U3_T - 1))
            stage(T_U3, U3_T, gelu(NKEY - U3_T))

            act.wait_ge(ev("w_used"), W_STEPS)
            act.wait_ge(piece_used, P_V)
            for s in range(4):
                if s == 2:
                    act.wait_ge(ev("w_used"), 2 * W_STEPS)
                with act.Fori(s * SWEEP, (s + 1) * SWEEP) as i:
                    for m in range(8):
                        slot = m % 4
                        act.wait_ge(raw_landed[slot], i * 32 + (P_V // 4 + m // 4 + 1) * 16)
                        act.wait_ge(piece_used, i * 8 + (P_V + m - 3))
                        act.activation(piece_ap(w_hi, slot), piece_ap(raw, slot), ACT.Copy).then_inc(hi_ready, 1)
                        act.activation(av_hi[:, slot * S:(slot + 1) * S], expert_col(s, i, m), ACT.Copy)\
                           .then_inc(ev("av_hi_r"), 1)
            for b in range(4, 8):
                act.wait_ge(ev("last_kept"), b - 3)
                act.activation(ar(b * 512, 512), x3[:, b * 512:(b + 1) * 512], ACT.Square).then_inc(ev("fsq"), 1)
            act.wait_ge(ev("fvar"), 1)
            act.activation(ar(A_XBC + S, S), ar(A_XBC, S), ACT.Sqrt).then_inc(ev("froot"), 1)

        @block.vector
        def _(v):
            st = Steps(v, v_step)

            def lo(T, h):
                slot = (T.c % 2) * 2 + h
                v.wait_ge(hi_ready, T.times(2, h + 1))
                wait(v, piece_used, T.times(2, h - 1))
                v.tensor_tensor(piece_ap(w_lo, slot % 2), piece_ap(raw, slot), piece_ap(w_hi, slot).bitcast(F32),
                                ALU.subtract).then_inc(lo_ready, 1)

            def pair(T):
                lo(T, 0)
                lo(T, 1)

            def stage(T0, n, evict=None, steps=0, late=None, per=2, beside=None, begun=False, goes_on=False):
                def turn(i, first):
                    for m in range(per):
                        if not (first and m == 0 and begun):
                            lo(Tile(i, per, T0 + m), 0)
                        lo(Tile(i, per, T0 + m), 1)
                        if beside:
                            beside(i, m, first)
                        if late and not (first and m < 2):
                            late(Tile(i, per, m - 2))
                        if evict and not (first and m == 0):
                            evict(Tile(i, per, m - 1))
                turn(0, True)
                st.turns(1, n // per, steps, lambda i: turn(i, False))
                if goes_on:
                    lo(Tile(0, per, T0 + n), 0)
                if late:
                    late(Tile(0, per, n - 2))
                if evict:
                    evict(Tile(0, per, n - 1))
                if late:
                    late(Tile(0, per, n - 1))

            def rstd(total, n, var, root, t1, out, var_ev, root_ev):
                v.tensor_scalar(var, total, 1.0 / n, EPS, ALU.mult, ALU.add).then_inc(var_ev, 1)
                v.wait_ge(root_ev, 1)
                inverse_root(var, root, t1, out)

            def inverse_root(var, root, t1, out):
                st(v.reciprocal(out, root))
                st(v.tensor_tensor(t1, out, out, ALU.mult))
                st(v.tensor_tensor(t1, t1, var, ALU.mult))
                st(v.tensor_scalar(t1, t1, -0.5, 1.5, ALU.mult, ALU.add))
                st(v.tensor_tensor(out, out, t1, ALU.mult))

            r1 = ar(A_K + 2 * S, S)
            for c in range(4):
                v.wait_ge(ev("sq_ready"), c + 1)
                v.tensor_reduce(ar(A_K + (4 + c) * S, S), ar(c * PIECE, PIECE).rearrange("p (k t) -> p t k", k=4),
                                AX.X, ALU.add).then_inc(ev("sq_added"), 1)
            v.wait_ge(ev("sum_ready"), 1)
            rstd(bank[2][:, 0:S], D, ar(A_K, S), ar(A_K + S, S), ar(A_K + 3 * S, S), r1,
                 ev("var_ready"), ev("root_ready"))
            v.wait_ge(par_in, 32)
            for c in range(4):
                buf = ar(A_MG + (16 + 4 * (c % 2)) * KB, PIECE)
                v.wait_ge(x_in[c], 16)
                for k in range(4):
                    kt = 4 * c + k
                    ins = v.scalar_tensor_tensor(buf[:, k * S:(k + 1) * S], ar(A_MG + kt * S, S),
                                                 par[:, V_AN + kt:V_AN + kt + 1], r1, ALU.mult, ALU.mult)
                ins.then_inc(ev("h_ready"), 1)
                if c == 1:
                    lo(Tile(0, 2, T_K), 0)
                v.wait_ge(ev("h_hi"), c + 1)
                v.tensor_tensor(act0_lo[:, c * PIECE:(c + 1) * PIECE], buf,
                                act0_hi[:, c * PIECE:(c + 1) * PIECE].bitcast(F32), ALU.subtract)\
                 .then_inc(ev("h_split"), 1)
            stage(T_K, K_T, begun=True)
            stage(T_VG, V_T)

            two = lambda x: x.unsqueeze(1).broadcast_to([P, 2, S])
            pair2 = lambda x: x.rearrange("p (b t) -> p b t", b=2)
            tmp = ar(A_MG + 12 * KB, 64 * 12)
            x_dt, dta, acs = small[:, 96:160], small[:, 160:224], small[:, 224:288]
            dtdte, dte = small[:, 288:320], small[:, 328:360]
            u, s_, s2, acc = tmp[:, 64:128], tmp[:, 256:320], tmp[:, 320:384], tmp[:, 384:448]

            def rope_k(n):
                k, scratch = ar(A_K + n * 512, 512), ar(A_MG + 8 * KB + (n % 2) * 512, 512)
                v.wait_ge(phase_in, 16)
                v.wait_ge(ev("krot"), n + 1)
                st.mark(v.tensor_tensor(pair2(scratch), pair2(bank[2 + n % 4][:, :]), two(sin_t), ALU.mult))
                st(v.tensor_tensor(pair2(k), pair2(k), two(cos_t), ALU.mult))
                v.tensor_tensor(k, k, scratch, ALU.add).then_inc(ev("krope"), 1)

            def dt_bias():
                v.wait_ge(ev("g_kept"), 2)
                dt2 = x_dt.rearrange("p (c h) -> p c h", c=2)
                v.tensor_tensor(dt2, bank[6][:, 2 * P:4 * P].rearrange("p (c h) -> p c h", c=2)[:, :, 0:SH],
                                par[:, V_DTB:V_DTB + SH].unsqueeze(1).broadcast_to([P, 2, SH]), ALU.add)\
                 .then_inc(ev("g_kept"), 1)
                v.wait_ge(ev("g_kept"), 3)
                st(v.tensor_scalar(tmp[:, 192:256], x_dt, -1.0, None, ALU.mult))
                v.tensor_tensor(tmp[:, 0:64], x_dt, tmp[:, 192:256], ALU.max).then_inc(ev("dt_in"), 1)

            def log1p_start():
                v.wait_ge(ev("dt_exp"), 2)
                st(v.tensor_scalar(s_, u, 2.0, None, ALU.add))
                st(v.reciprocal(s_, s_))
                st(v.tensor_tensor(s_, s_, u, ALU.mult))
                st(v.tensor_tensor(s2, s_, s_, ALU.mult))
                st(v.tensor_scalar(acc, s2, 1.0 / 17, 1.0 / 15, ALU.mult, ALU.add))

            def log1p_terms(odd):
                for k in odd:
                    st(v.tensor_tensor(acc, acc, s2, ALU.mult))
                    st(v.tensor_scalar(acc, acc, 1.0 / k, None, ALU.add))

            def dt_times_a():
                st.mark(v.tensor_tensor(acc, acc, s_, ALU.mult))
                st.mark(v.tensor_scalar(x_dt, x_dt, 0.0, None, ALU.max))
                st(v.tensor_scalar(tmp[:, 128:160], tmp[:, 128:160], -1.0, None, ALU.mult))
                st(v.scalar_tensor_tensor(x_dt, acc, 2.0, x_dt, ALU.mult, ALU.add))
                v.tensor_tensor(dta.rearrange("p (c h) -> p c h", c=2), x_dt.rearrange("p (c h) -> p c h", c=2),
                                tmp[:, 128:160].unsqueeze(1).broadcast_to([P, 2, SH]), ALU.mult)\
                 .then_inc(ev("dta_ready"), 1)

            def place_rows(c):
                if c == 0:
                    v.wait_ge(ev("krope"), 6)
                    v.wait_ge(ev("hid_sum"), 1)
                chunks = ar(A_K + (8 + 4 * c) * S, 4 * S).rearrange("p (g n l) -> p l g n", g=GROUPS, l=CS)
                placed = ar(A_MG + 16 * KB, CB * GROUPS * NC).rearrange("p (l g n) -> p l g n", g=GROUPS, n=NC)
                for r in range(CB // CS):
                    pos = par[:, V_POS + c * CB + r * CS:V_POS + c * CB + (r + 1) * CS]
                    for g in range(GROUPS):
                        ins = v.tensor_tensor(placed[:, r * CS:(r + 1) * CS, g, :], chunks[:, :, g, r:r + NC],
                                              pos.unsqueeze(2).broadcast_to([P, CS, NC]), ALU.add)
                ins.then_inc(ev("rows_placed"), 1)

            for m in range(HEADS):
                pair(Tile(0, 2, T_Q + m))
                if 1 <= m <= 6:
                    rope_k(m - 1)
                if m == 0:
                    place_rows(1)
                if m == 7:
                    dt_bias()
                    place_rows(0)
                if m == 8:
                    log1p_start()
                if m == 9:
                    log1p_terms((13, 11, 9, 7))
                if m == 10:
                    log1p_terms((5, 3, 1))
                    dt_times_a()
                if m == 12:
                    v.wait_ge(ev("acs_sum"), 1)
                    v.tensor_copy(acs, bank[2][:, 0:64]).then_inc(ev("acs_kept"), 1)
                    v.wait_ge(ev("acs_kept"), 1)
                    v.tensor_tensor(dte, bank[2][:, 64:96], acs[:, 0:32], ALU.subtract).then_inc(ev("dte_in"), 1)

            starts = (0, 2, 5, 7)
            gsig = small[:, 0:96]

            def attention_turn(i, first):
                def n_of(hh):
                    return i * 4 + hh

                def bufs(hh):
                    o = 360 + (hh % 2) * 24
                    return (ar(A_MG + 8 * KB + (hh % 2) * 800, 798), small[:, o:o + 6], small[:, o + 6:o + 12],
                            small[:, o + 12:o + 18])

                def rope(hh):
                    v.wait_ge(ev("q_rot"), n_of(hh) + 1)
                    q = ar(A_MG + 20 * KB + (hh % 2) * S, S)
                    t = ar(A_MG + 22 * KB, S)
                    st.mark(v.tensor_tensor(t, bank[2][:, 0:S], sin_t, ALU.mult))
                    st(v.tensor_tensor(q, arena[:, ds(i * 4 * S + hh * S, S)], cos_t, ALU.mult))
                    v.tensor_tensor(q, q, t, ALU.add).then_inc(ev("q_roped"), 1)
                    v.wait_ge(ev("q_roped"), n_of(hh) + 1)

                def score(hh):
                    v.wait_ge(ev("scores"), n_of(hh) + 1)
                    if not (first and hh < 2):
                        v.wait_ge(ev("p_turned"), n_of(hh) - 1)
                    pr, nm, sm, wg = bufs(hh)
                    m0 = mask_t[:, P:S].unsqueeze(1).broadcast_to([P, 2, P])
                    s0 = pr[:, 0:S].rearrange("p (b s) -> p b s", b=2)
                    s1 = pr[:, S:3 * S].rearrange("p (b s) -> p b s", b=2)
                    s2 = pr[:, 3 * S:3 * S + 2 * NC].rearrange("p (b s) -> p b s", b=2)
                    st.mark(v.scalar_tensor_tensor(s0, bank[3][:, 0:S].rearrange("p (b s) -> p b s", b=2), SCALE, m0,
                                                   ALU.mult, ALU.add))
                    st.mark(v.scalar_tensor_tensor(s1, bank[4][:, :].rearrange("p (b s) -> p b s", b=2), SCALE,
                                                   two(mask_t), ALU.mult, ALU.add))
                    st(v.scalar_tensor_tensor(pr[:, 3 * S:3 * S + 2 * NC], bank[2][:, 0:2 * NC], SCALE,
                                              cmp_bias, ALU.mult, ALU.add))
                    st.mark(v.tensor_reduce(nm[:, 0:2], s0, AX.X, ALU.max, negate=True))
                    st.mark(v.tensor_reduce(nm[:, 2:4], s1, AX.X, ALU.max, negate=True))
                    v.tensor_reduce(nm[:, 4:6], s2, AX.X, ALU.max, negate=True).then_inc(ev("scored"), 1)
                    st.wait()

                def probs(hh):
                    v.wait_ge(ev("exps"), i * 24 + 6 * (hh + 1))
                    pr, nm, sm, wg = bufs(hh)
                    st(v.reciprocal(wg, sm))
                    st(v.tensor_tensor(wg, wg, gsig_at(i, hh), ALU.mult))
                    s0 = pr[:, 0:S].rearrange("p (b s) -> p b s", b=2)
                    s1 = pr[:, S:3 * S].rearrange("p (b s) -> p b s", b=2)
                    s2 = pr[:, 3 * S:3 * S + 2 * NC].rearrange("p (b s) -> p b s", b=2)
                    st(v.tensor_tensor(s2, s2, cmp_01.rearrange("p (b s) -> p b s", b=2), ALU.mult))
                    st.mark(v.tensor_tensor(s2, s2, wg[:, 4:6].unsqueeze(2).broadcast_to([P, 2, NC]), ALU.mult))
                    st.mark(v.tensor_tensor(s0, s0, wg[:, 0:2].unsqueeze(2).broadcast_to([P, 2, P]), ALU.mult))
                    v.tensor_tensor(s1, s1, wg[:, 2:4].unsqueeze(2).broadcast_to([P, 2, S]), ALU.mult)\
                     .then_inc(ev("probs"), 1)

                def gsig_at(i, hh):
                    return small[:, ds(i * 24 + hh * 6, 6)]

                def keep_pt(hh):
                    v.wait_ge(ev("p_turned"), n_of(hh) + 1)
                    pt = ar(A_MG + 16 * KB, 4 * S)
                    if not (first and hh == 0):
                        v.wait_ge(ev("pv"), n_of(hh))
                    st(v.tensor_copy(pt[:, 2 * S:3 * S], bank[6][:, 0:S]))
                    v.tensor_copy(pt[0:NC, 3 * S:4 * S], bank[6][0:NC, S:2 * S]).then_inc(ev("p_kept_b"), 1)

                def keep_o(hh):
                    v.wait_ge(ev("o_hi"), n_of(hh) + 1)
                    v.tensor_tensor(act1_lo[:, ds(i * 4 * S + hh * S, S)], bank[7][:, 0:S],
                                    act1_hi[:, ds(i * 4 * S + hh * S, S)].bitcast(F32), ALU.subtract)\
                     .then_inc(ev("o_lo"), 1)

                def conv(b, n):
                    if n == 0:
                        v.wait_ge(tile_evicted, i * 8 + T_ATT)
                        v.wait_ge(ev("silu_done"), i * 2 + (b - 1))
                    for t in range(4):
                        out = ar(A_K + 8 * KB + t * S, S)
                        w = par[:, ds(i * 32 + (V_CW + (b * 4 - 8 + t) * 4 + 3 - n), 1)]
                        u = arena[:, ds(i * 8 * S + (A_XBC + (b * 4 - 8 + t) * S), S - n)]
                        if n == 0:
                            ins = v.tensor_scalar(out, u, w, par[:, ds(i * 8 + (V_CB + b * 4 - 8 + t), 1)],
                                                  ALU.mult, ALU.add)
                        else:
                            ins = v.scalar_tensor_tensor(out[:, n:S], u, w, out[:, n:S], ALU.mult, ALU.add)
                        if n < CONV - 1:
                            st.mark(ins)
                    if n < CONV - 1:
                        st.wait()
                    else:
                        ins.then_inc(ev("conv_done"), 1)

                for m in range(12):
                    T = Tile(i, 12, T_ATT + m)
                    lo(T, 0)
                    if not first and m < 10 and m % 5 < CONV:
                        conv(m // 5, m % 5)
                    lo(T, 1)
                    if m in starts:
                        rope(starts.index(m))
                    if m - 1 in starts:
                        score(starts.index(m - 1))
                    if m - 2 in starts:
                        probs(starts.index(m - 2))
                    if m - 3 in starts:
                        keep_pt(starts.index(m - 3))
                    if m - 4 in starts:
                        keep_o(starts.index(m - 4))

            attention_turn(0, True)
            st.turns(1, GROUPS, 4 * 13 + 2 * 4 * (CONV - 1), lambda i: attention_turn(i, False))

            v.wait_ge(ev("dte_ready"), 1)
            x_dt, dtdte, dte = small[:, 96:160], small[:, 288:320], small[:, 328:360]
            v.tensor_tensor(dtdte, dte, x_dt[:, 0:32], ALU.mult).then_inc(ev("dtdte_ready"), 1)
            v.wait_ge(ev("dtdte_ready"), 1)

            xs_stage = ar(A_K, 4 * S)
            c_stage = ar(A_K + 5 * KB, S)
            ebuf = [ar(A_K + (6 + 4 * c) * KB, PIECE) for c in range(2)]
            cs_buf = ar(A_K + 14 * KB, PIECE)
            xdt = [ar(A_K + (18 + 2 * c) * KB, 512) for c in range(2)]
            xde = ar(A_K + 22 * KB, 512)
            cbm = small[:, 444:700]
            v.wait_ge(ev("silu_done"), XBC_T // 4 + 1)

            def heads(x):
                return x.rearrange("p (r l) -> p r l", r=SHG)

            def over(x, n):
                return x.unsqueeze(2).broadcast_to([P, SHG, n])

            def ssd_turn(i, first):
                def per_head(t, c):
                    return small[:, ds(i * 8 + (t + 32 * c), 8)]
                if not first:
                    v.wait_ge(ev("y_sum"), i)
                for c in range(2):
                    v.tensor_tensor(heads(ebuf[c]), tri.unsqueeze(1).broadcast_to([P, SHG, P]),
                                    over(per_head(160, c), P), ALU.mult).then_inc(ev("dtatri"), 1)
                pair(Tile(i, 6, T_SSD))
                v.wait_ge(ev("x_turned"), i + 1)
                for c in range(2):
                    st.mark(v.tensor_tensor(xdt[c].rearrange("p (r d) -> p r d", r=SHG),
                                            bank[2 + c][:, :].rearrange("p (r d) -> p r d", r=SHG),
                                            over(per_head(96, c), SP_), ALU.mult))
                v.tensor_tensor(xde.rearrange("p (r d) -> p r d", r=SHG),
                                bank[2][:, :].rearrange("p (r d) -> p r d", r=SHG),
                                over(small[:, ds(i * 8 + 288, 8)], SP_), ALU.mult).then_inc(ev("xdt_ready"), 1)
                v.wait_ge(ev("b_kept"), i + 1)
                st(v.tensor_tensor(cbm.rearrange("p (c l) -> p c l", c=2),
                                   bank[6][:, P:3 * P].rearrange("p (c l) -> p c l", c=2),
                                   tri.unsqueeze(1).broadcast_to([P, 2, P]), ALU.mult))
                pair(Tile(i, 6, T_SSD + 1))

                def seg(c):
                    v.wait_ge(ev("acsb"), i * 2 + (c + 1))
                    for n in range(2):
                        ins = v.tensor_tensor(
                            ebuf[c][:, n * 512:(n + 1) * 512].rearrange("p (r l) -> p r l", r=4),
                            bank[4 + n][:, :].rearrange("p (r l) -> p r l", r=4),
                            small[:, ds(i * 8 + (224 + 32 * c + 4 * n), 4)].unsqueeze(2).broadcast_to([P, 4, P]),
                            ALU.subtract)
                        st.mark(ins)
                    st.wait()
                    v.tensor_scalar(ebuf[c], ebuf[c], 0.0, None, ALU.min).then_inc(ev("seg_ready"), 1)

                def decay(c):
                    v.wait_ge(ev("seg_exp"), i * 2 + (c + 1))
                    v.tensor_tensor(heads(ebuf[c]), heads(ebuf[c]),
                                    cbm[:, c * P:(c + 1) * P].unsqueeze(1).broadcast_to([P, SHG, P]),
                                    ALU.mult).then_inc(ev("m_ready"), 1)

                seg(0)
                pair(Tile(i, 6, T_SSD + 2))
                seg(1)
                pair(Tile(i, 6, T_SSD + 3))
                decay(0)
                decay(1)
                v.wait_ge(ev("c_exp"), i * 2 + 2)
                v.tensor_tensor(heads(cs_buf), heads(cs_buf), c_stage[:, P:S].unsqueeze(1).broadcast_to([P, SHG, P]),
                                ALU.mult).then_inc(ev("c_ready"), 1)
                pair(Tile(i, 6, T_SSD + 4))
                v.wait_ge(ev("y_sum"), i + 1)
                for t in range(4):
                    st.mark(v.scalar_tensor_tensor(xs_stage[:, t * S:(t + 1) * S], xs_stage[:, t * S:(t + 1) * S],
                                                   par[:, ds(i * 4 + (V_DS + t), 1)],
                                                   bank[2 + t // 2][:, (t % 2) * S:(t % 2 + 1) * S],
                                                   ALU.mult, ALU.add))
                st.wait()
                zt = arena[:, ds(A_Z + i * 4 * S, 4 * S)]
                v.wait_ge(ev("z_done"), i + 1)
                v.tensor_tensor(zt, zt, xs_stage, ALU.mult).then_inc(ev("g_ready"), 1)
                pair(Tile(i, 6, T_SSD + 5))
                v.wait_ge(ev("gsum"), i + 1)
                v.tensor_copy(arena[:, ds(A_XBC + i * 4 * S, S)], bank[7][:, 0:S]).then_inc(ev("gsum_kept"), 1)

            SSD_STEPS = 2 + 1 + 4 + 4
            ssd_turn(0, True)
            st.turns(1, SG, SSD_STEPS, lambda i: ssd_turn(i, False))

            v.wait_ge(ev("gsum_kept"), SG)
            gr = ar(A_K + 2 * S, S)

            def bn(T):
                v.wait_ge(ev("gate_ready"), T.times(1, 1))
                v.wait_ge(piece_used, T.times(2, 2 * T_BN + 2))
                m0 = arena[:, ds(T.times(S, A_MG), S)]
                v.tensor_tensor(m0, m0, bank[T.c % 2][:, 0:S], ALU.mult).then_inc(tile_evicted, 1)

            def y_norm(i, m, first):
                if m == 0:
                    v.tensor_scalar(ar(A_K, S), arena[:, ds(A_XBC + i * 4 * S, S)], 1.0 / (4 * P), EPS,
                                    ALU.mult, ALU.add).then_inc(ev("gvar"), 1)
                if m == 1:
                    v.wait_ge(ev("groot"), i + 1)
                    inverse_root(ar(A_K, S), ar(A_K + S, S), ar(A_K + 3 * S, S), gr)
                if m == 2:
                    for k in range(4):
                        z = arena[:, ds(A_Z + i * PIECE + k * S, S)]
                        ins = v.scalar_tensor_tensor(z, z, par[:, ds(i * 4 + (V_SN + k), 1)], gr, ALU.mult, ALU.mult)
                    ins.then_inc(ev("gn_ready"), 1)
                if m == 3:
                    v.wait_ge(ev("gn_hi"), i + 1)
                    v.tensor_tensor(act0_lo[:, ds(i * PIECE, PIECE)], arena[:, ds(A_Z + i * PIECE, PIECE)],
                                    act0_hi[:, ds(i * PIECE, PIECE)].bitcast(F32), ALU.subtract)\
                     .then_inc(ev("g_split"), 1)

            stage(T_BN, KT, bn, steps=5, per=4, beside=y_norm, goes_on=True)

            def bs(T):
                v.wait_ge(ev("gate_ready"), T.times(1, KT + 1))
                v.wait_ge(piece_used, T.times(2, 2 * T_BS + 2))
                m1 = arena[:, ds(T.times(S, A_MG + KT * S), S)]
                m0 = arena[:, ds(T.times(S, A_MG), S)]
                v.tensor_tensor(m1, m1, bank[T.c % 2][:, 0:S], ALU.mult).then_inc(tile_evicted, 1)
                v.wait_ge(tile_evicted, T.times(1, T_BS + 1))
                v.tensor_tensor(m0, m0, m1, ALU.add).then_inc(ev("merged"), 1)

            def bs_lo(T):
                v.wait_ge(ev("merged_hi"), T.times(1, 1))
                v.tensor_tensor(act1_lo[:, ds(T.times(S), S)], arena[:, ds(T.times(S, A_MG), S)],
                                act1_hi[:, ds(T.times(S), S)].bitcast(F32), ALU.subtract)\
                 .then_inc(ev("merged_lo"), 1)

            stage(T_BS, KT, bs, late=bs_lo, begun=True, goes_on=True)

            def wo(T):
                v.wait_ge(piece_used, T.times(2, 2 * T_WO + 2))
                x2 = arena[:, ds(T.times(S, A_Z), S)]
                v.tensor_tensor(x2, bank[T.c % 2][:, 0:S], arena[:, ds(T.times(S, A_XBC), S)], ALU.add)\
                 .then_inc(tile_evicted, 1)
                v.wait_ge(tile_evicted, T.times(1, T_WO + 1))
                v.tensor_scalar(arena[:, ds(T.times(S, A_MG), S)], x2, par[:, ds(T.times(1, V_FN), 1)], None, ALU.mult)\
                 .then_inc(ev("x2_ready"), 1)

            def wo_lo(T):
                v.wait_ge(ev("x2g_hi"), T.times(1, 1))
                v.tensor_tensor(act0_lo[:, ds(T.times(S), S)], arena[:, ds(T.times(S, A_MG), S)],
                                act0_hi[:, ds(T.times(S), S)].bitcast(F32), ALU.subtract)\
                 .then_inc(ev("x2g_lo"), 1)

            v.wait_ge(ev("res_in"), 16)
            stage(T_WO, KT, wo, late=wo_lo, begun=True, goes_on=True)

            def residual_rstd(i, m, first):
                if first and m == 1:
                    v.wait_ge(ev("x2sum"), 1)
                    rstd(bank[2][:, 0:S], D, ar(A_XBC + 17 * KB, S), ar(A_XBC + 18 * KB, S), ar(A_XBC + 19 * KB, S), r2,
                         ev("x2var"), ev("x2root"))

            def wq(T):
                v.wait_ge(piece_used, T.times(2, 2 * T_WQ + 2))
                v.tensor_tensor(arena[:, ds(T.times(S, A_MG + 16 * KB), S)], bank[T.c % 2][:, 0:S], r2, ALU.mult)\
                 .then_inc(tile_evicted, 1)

            stage(T_WQ, KT, wq, beside=residual_rstd, begun=True, goes_on=True)

            s_all = ar(A_Z, KT * S)

            def keep_scores():
                v.wait_ge(ev("spilled"), 16)
                for n in range(0, 8, 2):
                    v.wait_ge(ev("s_sum"), n + 1)
                    v.wait_ge(ev("s_kept"), n)
                    v.tensor_copy(s_all[:, n * 512:(n + 1) * 512], bank[4 + n % 4][:, :]).then_inc(ev("s_kept"), 1)
                v.wait_ge(ev("s_kept"), 8)

            top = ar(A_MG, 16 * KB)
            sc, sc2 = top[:, 0:S], top[:, S:2 * S]
            cand, cand2 = top[:, 2 * S:3 * S], top[:, 3 * S:4 * S]
            eq = top[:, 4 * S:5 * S]
            sv, sif = top[:, 5 * S:5 * S + 32], top[:, 5 * S + 32:5 * S + 64]
            si = top[:, 5 * S + 64:5 * S + 96].bitcast(U32)
            pos = top[:, 5 * S + 96:5 * S + 112].bitcast(U32)
            pa, pb = (top[:, 5 * S + k:5 * S + k + 16].bitcast(U32) for k in (112, 128))
            paf, pbf = top[:, 5 * S + 144:5 * S + 160], top[:, 5 * S + 160:5 * S + 176]
            best = top[:, 5 * S + 176:5 * S + 192]
            res_at = A_Z - 3 * KB
            mat = lambda x: x.rearrange("p (k a) -> p k a", k=16)
            rows = lambda x: x.unsqueeze(2).broadcast_to([P, 16, 16])
            cols = lambda x: x.unsqueeze(1).broadcast_to([P, 16, 16])
            FLOOR = -3.0e38

            def dots(T0):
                def evict(T):
                    v.wait_ge(piece_used, T.times(2, 2 * (T_U + T0) + 2))
                    v.tensor_tensor(arena[:, ds(T.times(S, T0 * S), S)], bank[T.c % 2][:, 0:S], r2, ALU.mult)\
                     .then_inc(tile_evicted, 1)
                return evict

            def top_parts(i):
                halves = [(sc[:, c * P:(c + 1) * P], sc2[:, c * P:(c + 1) * P], sv[:, c * 16:(c + 1) * 16],
                           si[:, c * 16:(c + 1) * 16]) for c in range(2)]

                def keys():
                    st.apart(v.tensor_copy(sc, arena[:, ds(A_Z + i * S, S)]))
                    for x, y, top, at in halves:
                        st.mark(v.max(top[:, 0:8], x))
                    st.wait()
                    v.nop(nofuse=True)
                    for x, y, top, at in halves:
                        st.mark(v.max_index(at[:, 0:8], top[:, 0:8], x))
                        st.mark(v.match_replace(y, top[:, 0:8], x, FLOOR))
                    st.wait()
                    v.nop(nofuse=True)
                    for x, y, top, at in halves:
                        st.mark(v.max(top[:, 8:16], y))
                    st.wait()
                    v.nop(nofuse=True)
                    for x, y, top, at in halves:
                        st.mark(v.max_index(at[:, 8:16], top[:, 8:16], y))

                def pairs():
                    st.apart(v.tensor_tensor(mat(cand), rows(sv[:, 0:16]), cols(sv[:, 16:32]), ALU.add))
                    st.mark(v.tensor_copy(sif, si))
                    st.apart(v.max(best[:, 0:8], cand))
                    st.mark(v.max_index(pos[:, 0:8], best[:, 0:8], cand))
                    st.apart(v.match_replace(cand2, best[:, 0:8], cand, FLOOR))

                def places():
                    st.apart(v.max(best[:, 8:16], cand2))
                    st(v.max_index(pos[:, 8:16], best[:, 8:16], cand2))
                    st.mark(v.tensor_copy(arena[:, ds(res_at + 2 * S + i * 16, 16)], best))
                    st.mark(v.tensor_scalar(pa, pos, 4, None, ALU.logical_shift_right))
                    st(v.tensor_scalar(pb, pos, 15, None, ALU.bitwise_and))
                    st.mark(v.tensor_copy(paf, pa))
                    st.mark(v.tensor_copy(pbf, pb))
                    st.wait()

                def index():
                    both = ((paf, eq), (pbf, cand))
                    for n, (place, e) in enumerate(both):
                        st.mark(v.tensor_tensor(mat(e), rows(place), cols(iota[:, 0:16]), ALU.is_equal))
                    st.wait()
                    for n, (place, e) in enumerate(both):
                        st.mark(v.tensor_tensor(mat(e), mat(e), cols(sif[:, n * 16:(n + 1) * 16]), ALU.mult))
                    st.wait()
                    for n, (place, e) in enumerate(both):
                        st.mark(v.tensor_reduce(arena[:, ds(res_at + n * S + i * 16, 16)], mat(e), AX.X, ALU.add))
                    st.wait()

                return keys, pairs, places, index

            scale1 = dots(0)

            def top_turn(i, first):
                parts = top_parts(i)
                for m in range(4):
                    if not (first and m == 0):
                        lo(Tile(i, 4, T_U + m), 0)
                    lo(Tile(i, 4, T_U + m), 1)
                    if not (first and m == 0):
                        scale1(Tile(i, 4, m - 1))
                    if not first:
                        parts[m]()
                    elif m == 1:
                        keep_scores()
                        parts[0]()
                    elif m > 1:
                        for part in parts[1:2] if m == 2 else parts[2:]:
                            part()

            top_turn(0, True)
            st.turns(1, U1_T // 4, 11 + 5 + 7 + 6, lambda i: top_turn(i, False))
            scale1(Tile(0, 4, U1_T - 1))
            g3 = ar(res_at + 2 * S, S).rearrange("p (h k) -> p h k", k=16)
            mx = small[:, 352:368]
            g_dots, u2_dots = dots(U1_T), dots(U1_T + G_T)
            lo(Tile(0, 2, T_U + U1_T), 0)
            st(v.tensor_copy(mx.unsqueeze(2), g3[:, :, 0:1]))
            v.tensor_tensor(g3, g3, mx.unsqueeze(2).broadcast_to([P, 16, 16]), ALU.subtract).then_inc(ev("gate_in"), 1)
            lo(Tile(0, 2, T_U + U1_T), 1)
            lo(Tile(0, 2, T_U + U1_T + 1), 0)
            v.wait_ge(ev("gate_exp"), 1)
            st(v.tensor_reduce(mx, g3, AX.X, ALU.add))
            st(v.reciprocal(mx, mx))
            v.tensor_tensor(g3, g3, mx.unsqueeze(2).broadcast_to([P, 16, 16]), ALU.mult).then_inc(ev("gate_done"), 1)
            lo(Tile(0, 2, T_U + U1_T + 1), 1)
            g_dots(Tile(0, 2, 0))
            v.memset(zeros, 0.0).then_inc(ev("v_zero"), 1)
            lo(Tile(0, 2, T_U2), 0)
            g_dots(Tile(0, 2, 1))
            v.wait_ge(ev("i_turned"), 3)
            v.tensor_copy(rows_i, bank[2][:, 0:S]).then_inc(ev("i_kept"), 1)
            st.mark(v.tensor_copy(cols_j, bank[3][:, 0:S]))
            st.mark(v.tensor_copy(iota_j, iota))
            st(v.tensor_copy(gate_part[0], bank[4][:, 0:S]))
            st(v.tensor_tensor(gate_rest, bank[4][:, 0:S], gate_part[0], ALU.subtract))
            st(v.tensor_copy(gate_part[1], gate_rest))
            st(v.tensor_tensor(gate_rest, gate_rest, gate_part[1], ALU.subtract))
            v.tensor_copy(gate_part[2], gate_rest).then_inc(ev("i_kept"), 1)
            v.wait_ge(ev("i_kept"), 2)
            v.wait_ge(ev("g_done"), U1_T)
            a_tj = ar(0, NKEY * S).rearrange("p (j t) -> p t j", t=S)
            tok = lambda x: x.rearrange("p (t j) -> p t j", t=WT)

            def cols(step, half, store, first=False):
                if not first:
                    v.wait_ge(ev("w_sum"), step.times(1, half * W_STEPS))
                st(v.tensor_tensor(tok(oh_cols(store, 0)),
                                   iota_j[:, half * JH:(half + 1) * JH].unsqueeze(1).broadcast_to([P, WT, JH]),
                                   over_j(cols_j, step), ALU.is_equal))

            def gated(step, store):
                for k in range(3):
                    ins = v.tensor_tensor(tok(oh_cols(store, k + 1)), tok(oh_cols(store, 0)),
                                          over_j(gate_part[k], step), ALU.mult)
                ins.then_inc(ev("gj"), 1)

            def gate_acts(step, half):
                v.wait_ge(ev("w_sum"), step.times(1, half * W_STEPS + 1))
                av = a_tj[:, ds(step.times(WT), WT), half * JH:(half + 1) * JH]
                v.tensor_tensor(av, av, tok(bank[2 + step.c % 2][:, :]), ALU.mult).then_inc(ev("w_used"), 1)

            def u2_turn(i, first):
                for m in range(W_TILES):
                    for h in range(2):
                        if not (first and m + h == 0):
                            lo(Tile(i, W_TILES, T_U2 + m), h)
                        if h == 1 and not (first and m == 0):
                            u2_dots(Tile(i, W_TILES, m - 1))
                        at = 2 * m + h
                        if at - 3 in W_AT:
                            gate_acts(Tile(i, W_TURN, W_AT.index(at - 3)), 0)
                        if at in W_AT:
                            n = W_AT.index(at)
                            cols(Tile(i, W_TURN, n), 0, onehot_early, first and n == 0)
                        if at - 1 in W_AT:
                            gated(Tile(i, W_TURN, W_AT.index(at - 1)), onehot_early)

            u2_turn(0, True)
            st.turns(1, W_STEPS // W_TURN, 8, lambda i: u2_turn(i, False))
            u2_dots(Tile(0, 2, NKEY - U1_T - G_T - U3_T - 1))
            stage(T_U3, U3_T, dots(NKEY - U3_T))

            v.wait_ge(ev("g_done"), NKEY)
            v.wait_ge(piece_used, P_V)

            def keep_sweep(s):
                v.wait_ge(ev("back_in"), 16)
                v.wait_ge(ev("sweep"), s + 1)
                wait(v, ev("sweep_used"), 4 * s)
                for b in range(4):
                    x = x3[:, ((s % 2) * 8 + 2 * b) * S:((s % 2) * 8 + 2 * b + 2) * S]
                    v.tensor_tensor(x, x, bank[SWEEP_BANKS[s][b]][:, :], ALU.add)\
                     .then_inc(ev("sweep_used" if s < 3 else "last_kept"), 1)

            def v_turn(s, i, first):
                for m in range(8):
                    slot = m % 4
                    v.wait_ge(hi_ready, i * 8 + (P_V + m + 1))
                    v.wait_ge(piece_used, i * 8 + (P_V + m - 1))
                    v.tensor_tensor(piece_ap(w_lo, slot % 2), piece_ap(raw, slot), piece_ap(w_hi, slot).bitcast(F32),
                                    ALU.subtract).then_inc(lo_ready, 1)
                    v.wait_ge(ev("av_hi_r"), i * 8 + (m + 1))
                    v.tensor_tensor(av_lo[:, slot * S:(slot + 1) * S], expert_col(s, i, m),
                                    av_hi[:, slot * S:(slot + 1) * S].bitcast(F32), ALU.subtract)\
                     .then_inc(ev("av_lo_r"), 1)
                    if first and m == 0 and s > 0:
                        keep_sweep(s - 1)
                    if s < 2 and m % 4 == 0:
                        cols(Tile(i, 2, m // 4), 1, onehot_late)
                    if s < 2 and m % 4 == 1:
                        gated(Tile(i, 2, m // 4), onehot_late)
                    if s < 2 and m % 4 == 3:
                        gate_acts(Tile(i, 2, m // 4), 1)

            for s in range(4):
                v_turn(s, s * SWEEP, True)
                st.turns(s * SWEEP + 1, (s + 1) * SWEEP, 2 if s < 2 else 0, lambda i: v_turn(s, i, False))
            keep_sweep(3)
            v.wait_ge(ev("fsum"), 1)
            r3 = ar(A_XBC + 2 * S, S)
            rstd(bank[2][:, 0:S], D, ar(A_XBC, S), ar(A_XBC + S, S), ar(A_XBC + 3 * S, S), r3,
                 ev("fvar"), ev("froot"))
            for k in range(KT):
                x = x3[:, k * S:(k + 1) * S]
                v.scalar_tensor_tensor(x, x, par[:, V_ON + k:V_ON + k + 1], r3, ALU.mult, ALU.mult)\
                 .then_inc(ev("out_ready"), 1)

        @block.gpsimd
        def _(pool):
            st = Steps(pool, p_step)
            pool.wait_ge(hi_ready, 4)
            pool.dma_start(ar(phase_at, C_PHASE), a["phase"]).then_inc(phase_in, 16)
            for n in range(4):
                pool.wait_ge(hi_ready, 12 + 8 * n)
                part = slice(n * (CB + 1) * P // 2, (n + 1) * (CB + 1) * P // 2)
                pool.dma_start(arena[:, A_XBC + part.start:A_XBC + part.stop], a["cmp_w"][:, part]).then_inc(w1_in, 16)
            pool.wait_ge(par_in, 32)

            pool.wait_ge(ev("v_kept"), 4)
            pool.wait_ge(ev("cmp_kept"), 2)

            def stage_v(i, first):
                if not first:
                    pool.wait_ge(ev("pv"), i * 4)
                vs = ar(A_MG + 23 * KB, 4 * P)
                pool.tensor_copy(vs.rearrange("p (n d) -> p n d", n=4),
                                 ar(A_VTOK, 4 * 512).rearrange("p (n g d) -> p n g d", n=4, g=GROUPS)
                                 [:, :, ds(i, 1), :].rearrange("p n g d -> p n (g d)"))\
                    .then_inc(p_step, 1)
                pool.wait_ge(p_step, i + 1)
                pool.tensor_copy(ar(A_MG + 25 * KB, P)[0:NC, :], arena[0:NC, ds(A_K + 12 * KB + i * P, P)]).then_inc(ev("v_staged"), 1)

            stage_v(0, True)
            with pool.Fori(1, GROUPS) as i:
                stage_v(i, False)
            pool.wait_ge(ev("silu_done"), XBC_T // 4 + 1)
            pool.wait_ge(ev("pv"), HEADS)

            def stage_x(i, first):
                if not first:
                    pool.wait_ge(ev("g_ready"), i)
                pool.tensor_copy(ar(A_K, 4 * S), arena[:, ds(A_XBC + i * 4 * S, 4 * S)]).then_inc(p_step, 1)
                pool.tensor_copy(ar(A_K + 4 * KB, S), arena[:, ds(A_XBC + 16 * S + i * S, S)]).then_inc(p_step, 1)
                pool.tensor_copy(ar(A_K + 5 * KB, S), arena[:, ds(A_XBC + 20 * S + i * S, S)]).then_inc(p_step, 1)
                pool.wait_ge(p_step, i * 3 + (GROUPS + 3))
                pool.nop().then_inc(ev("x_staged"), 1)

            stage_x(0, True)
            with pool.Fori(1, SG) as i:
                stage_x(i, False)
            pool.wait_ge(ev("gvar"), SG)
            pool.dma_start(ar(A_XBC, KT * S).rearrange("p (k t) -> p k t", k=KT), a["x"].rearrange("k p t -> p k t"))\
                .then_inc(ev("res_in"), 16)
            acc, sq = ar(A_XBC + 16 * KB, S), ar(A_XBC + 20 * KB, S)
            pool.memset(acc, 0.0).then_inc(p_step, 1)
            n0 = GROUPS + 3 * SG + 1
            with pool.Fori(0, KT) as i:
                pool.wait_ge(ev("x2_ready"), i + 1)
                x2 = arena[:, ds(A_Z + i * S, S)]
                pool.wait_ge(p_step, i * 2 + n0)
                pool.tensor_tensor(sq, x2, x2, ALU.mult).then_inc(p_step, 1)
                pool.wait_ge(p_step, i * 2 + (n0 + 1))
                pool.tensor_tensor(acc, acc, sq, ALU.add).then_inc(p_step, 1)
                pool.wait_ge(p_step, i * 2 + (n0 + 2))
                pool.nop().then_inc(ev("sumsq"), 1)
            pool.dma_start(a["spill"], ar(A_Z, KT * S)).then_inc(ev("spilled"), 16)
            pool.wait_ge(ev("x2g_lo"), KT)
            pool.dma_start(ar(A_MG, 8 * KB), a["subk"]).then_inc(ev("subk_in"), 16)
            pool.wait_ge(ev("spilled"), 16)

            pool.wait_ge(ev("i_kept"), 2)

            def onehot_rows(step, half, store, first=False):
                if not first:
                    pool.wait_ge(ev("w_sum"), step.times(1, half * W_STEPS))
                pool.tensor_copy(row_now, rows_i[:, ds(step.times(WT), WT)]).then_inc(ev("rows_ready"), 1)
                pool.wait_ge(ev("rows_ready"), step.times(1, half * W_STEPS + 1))
                pool.nop(nofuse=True)
                for t in range(WT):
                    pool.tensor_scalar(oh_rows(store)[:, t * P:(t + 1) * P], iota, row_now[:, t:t + 1],
                                       None, ALU.is_equal).then_inc(ev("ohi"), 1)

            onehot_rows(Tile(0, 1, 0), 0, onehot_early, True)
            with pool.Fori(1, W_STEPS) as i:
                onehot_rows(Tile(i, 1, 0), 0, onehot_early)
            pool.wait_ge(piece_used, P_V)
            pool.dma_start(x3[:, :], a["spill"]).then_inc(ev("back_in"), 16)
            with pool.Fori(0, W_STEPS) as i:
                onehot_rows(Tile(i, 1, 0), 1, onehot_late)
            pool.wait_ge(ev("sweep_used"), 12)
            done = GROUPS + 3 * SG + 1 + 2 * KT
            half = 4 * S
            pool.tensor_tensor(ar(0, 2 * half), x3[:, 0:2 * half], x3[:, 0:2 * half], ALU.mult).then_inc(p_step, 1)
            pool.wait_ge(p_step, done + 1)
            pool.tensor_tensor(ar(0, half), ar(0, half), ar(half, half), ALU.add).then_inc(p_step, 1)
            pool.wait_ge(p_step, done + 2)
            pool.tensor_tensor(ar(0, half // 2), ar(0, half // 2), ar(half // 2, half // 2), ALU.add).then_inc(p_step, 1)
            pool.wait_ge(p_step, done + 3)
            pool.tensor_tensor(ar(A_XBC + 4 * S, S), ar(0, S), ar(S, S), ALU.add).then_inc(ev("fadd"), 1)


def col_tiles(w):
    n = w.shape[1] // P
    return w.reshape(2, HKT, P, n, P).transpose(3, 0, 2, 1, 4).reshape(2 * n, P, PIECE)


def padded(w):
    return np.concatenate([w, np.zeros((w.shape[0], P - w.shape[1]), w.dtype)], axis=1)


def columns(x):
    return x.reshape(-1, P).T


def lay_out(x, attn_norm, w_in, gate_bias, nsa_cmp_pos, nsa_cmp_w1, nsa_cmp_b1, nsa_cmp_w2, ssm_conv_w, ssm_conv_b,
            ssm_dt_bias, ssm_a_log, ssm_d, ssm_norm, w_branch_nsa, w_branch_ssm, w_out, ffn_norm, peer_w_q,
            peer_sub_keys, peer_u, peer_v, final_norm):
    w = w_in[0]
    at = np.cumsum([0, HEADS * HD, 6 * GROUPS * HD, 3 * HEADS, D, XBC_T * P, SH, 2 * D])
    q, kv, gate, z, xbc, dt, merge = (w[:, at[n]:at[n + 1]] for n in range(7))
    branch = lambda b, c: kv[:, (b * 2 + c) * GROUPS * HD:(b * 2 + c + 1) * GROUPS * HD]
    w_in_t = np.concatenate([branch(1, 0), branch(2, 0), branch(0, 0), branch(0, 1),
                             branch(1, 1), branch(2, 1), padded(gate), padded(dt), q, xbc, z, merge], axis=1)
    keep, phase = shape_constants()
    u = peer_u[0].reshape(NKEY, NKEY, 2, HKT, P)
    v = peer_v[0].reshape(NKEY, 2, JH, 2, PIECE)
    cw = ssm_conv_w[0].reshape(CONV, XBC_T, P)
    par = np.concatenate([
        columns(final_norm), columns(attn_norm[0]), columns(ssm_norm[0]), columns(gate_bias[0]),
        cw.transpose(2, 1, 0).reshape(P, XBC_T * CONV), columns(ffn_norm[0]),
        columns(ssm_conv_b[0]), nsa_cmp_b1[0].T, columns(np.repeat(ssm_d[0], SP_)),
        nsa_cmp_pos[0].transpose(2, 0, 1).reshape(P, 2 * CB),
        np.tile(ssm_dt_bias[0], (P, 1)), np.tile(ssm_a_log[0], (P, 1))], axis=1)
    assert par.shape[1] == V_END
    cmp_w = np.concatenate([nsa_cmp_w1[0].reshape(2, CB, P, P).transpose(2, 0, 1, 3).reshape(P, 2 * CB * P),
                            nsa_cmp_w2[0].transpose(1, 0, 2).reshape(P, 2 * P)], axis=1)
    return {
        "x": x[0].T.reshape(KT, P, S),
        "w_in": col_tiles(w_in_t),
        "w_mix": np.concatenate([col_tiles(m[0]) for m in (w_branch_nsa, w_branch_ssm, w_out, peer_w_q)]),
        "u": u.transpose(1, 2, 4, 3, 0).reshape(2 * NKEY, P, PIECE),
        "v": v.transpose(1, 3, 2, 0, 4).reshape(2 * NKEY, P, PIECE),
        "subk": peer_sub_keys[0].transpose(3, 0, 1, 2).reshape(P, 2 * PH * NKEY),
        "cmp_w": cmp_w, "par": par, "const": keep, "phase": phase,
    }


def kernel(**inputs):
    import concourse.bacc as bacc
    from concourse.bass_utils import run_bass_kernel_spmd

    nc = bacc.Bacc("TRN2", target_bir_lowering=False, num_devices=1)
    arrays = {n: np.ascontiguousarray(x) for n, x in lay_out(**{n: np.asarray(x) for n, x in inputs.items()}).items()}
    a = {n: nc.dram_tensor(n, x.shape, F32, kind="ExternalInput").ap() for n, x in arrays.items()}
    a["out"] = nc.dram_tensor("out", (KT, P, S), F32, kind="ExternalOutput").ap()
    a["spill"] = nc.dram_tensor("spill", (P, KT * S), F32, kind="Internal").ap()
    build(nc, a)
    r = run_bass_kernel_spmd(nc, [arrays], core_ids=[0])
    return np.ascontiguousarray(r.results[0]["out"].reshape(D, S).T)[None]
```
